# Optimizing a Trainium2 kernel written in Bass

```python
import jax, jax.numpy as jnp
from jax import lax
import numpy as np
import math

D_MODEL = 1024
BATCH = 1
SEQ = 256
DEPTH = 1

GRID_W = 64
POOL_WINDOWS = (2, 4, 8, 16)
POOL_WIDTH = D_MODEL // 2
POOL_GROUP = POOL_WIDTH // len(POOL_WINDOWS)
ATTN_HEADS = 8
HEAD_DIM = (D_MODEL // 2) // ATTN_HEADS
ATTN_WIDTH = ATTN_HEADS * HEAD_DIM
MIX_WIDTH = POOL_WIDTH + ATTN_WIDTH
WIN_ROWS_MAX = 8
WIN_COLS = 16
N_EXPERTS = 16
EC_CAPACITY = 2
D_EXPERT = 2 * D_MODEL
PLE_DIM = 256
RMS_EPS = 1e-6


def rms_norm(x, g):
    x32 = x.astype(jnp.float32)
    y = x32 * lax.rsqrt(jnp.mean(x32 * x32, axis=-1, keepdims=True) + RMS_EPS)
    return (y * g.astype(jnp.float32)).astype(x.dtype)

def multiscale_pool(u, w_pool, pool_scale):
    B, S, _ = u.shape
    u32 = u.astype(jnp.float32)
    cs = jnp.concatenate([jnp.zeros((B, 1, POOL_WIDTH), jnp.float32), jnp.cumsum(u32, axis=1)], axis=1)
    t = jnp.arange(S)
    outs = []
    for gi, w in enumerate(POOL_WINDOWS):
        lo = jnp.clip(t - w // 2, 0, S - 1)
        hi = jnp.clip(t + (w - w // 2) - 1, 0, S - 1)
        sl = slice(gi * POOL_GROUP, (gi + 1) * POOL_GROUP)
        csg = cs[:, :, sl]
        cnt = (hi - lo + 1).astype(jnp.float32)[None, :, None]
        outs.append((csg[:, hi + 1] - csg[:, lo]) / cnt - u32[:, :, sl])
    d = jnp.stack(outs, axis=2).astype(u.dtype)
    y = jnp.einsum('bsgc,gcd->bsgd', d, w_pool).reshape(B, S, POOL_WIDTH)
    return y * pool_scale

def neighbourhood_attention(q, k, v, q_norm, k_norm, rpb):
    B, S, H, HD = q.shape
    rows = S // GRID_W
    kh = min(WIN_ROWS_MAX, rows)
    q = rms_norm(q, q_norm) * (HD ** -0.5)
    k = rms_norm(k, k_norm)
    to_grid = lambda a: a.reshape(B, rows, GRID_W, H, HD).transpose(0, 3, 1, 2, 4)
    qg, kg, vg = to_grid(q), to_grid(k), to_grid(v)
    c = jnp.arange(GRID_W)
    col_start = jnp.clip(c - WIN_COLS // 2, 0, GRID_W - WIN_COLS)
    col_idx = col_start[:, None] + jnp.arange(WIN_COLS)[None, :]
    dc = col_idx - c[:, None] + (WIN_COLS - 1)

    def row_block(r):
        row_start = jnp.clip(r - kh // 2, 0, rows - kh)
        q_r = lax.dynamic_index_in_dim(qg, r, axis=2, keepdims=False)
        k_band = lax.dynamic_slice_in_dim(kg, row_start, kh, axis=2)
        v_band = lax.dynamic_slice_in_dim(vg, row_start, kh, axis=2)
        k_nb = k_band[:, :, :, col_idx]
        v_nb = v_band[:, :, :, col_idx]
        s = jnp.einsum('bhcd,bhicjd->bhcij', q_r, k_nb).astype(jnp.float32)
        dr = row_start + jnp.arange(kh) - r + (WIN_ROWS_MAX - 1)
        bias = rpb[:, dr[None, :, None], dc[:, None, :]]
        s = s + bias[None].astype(jnp.float32)
        pr = jax.nn.softmax(s.reshape(B, H, GRID_W, kh * WIN_COLS), axis=-1)
        pr = pr.reshape(B, H, GRID_W, kh, WIN_COLS).astype(v.dtype)
        return jnp.einsum('bhcij,bhicjd->bhcd', pr, v_nb)

    o = lax.map(row_block, jnp.arange(rows))
    return o.transpose(1, 0, 3, 2, 4).reshape(B, S, H * HD)

def expert_choice_ffn(h, w_router, w_gate, w_up, w_down):
    B, S, D = h.shape
    cap = EC_CAPACITY * S // N_EXPERTS
    aff = jax.nn.softmax(jnp.einsum('bsd,de->bse', h, w_router).astype(jnp.float32), axis=-1)
    gates, idx = lax.top_k(aff.transpose(0, 2, 1), cap)
    bidx = jnp.arange(B)[:, None, None]
    xe = h[bidx, idx]
    a = jnp.einsum('becd,edf->becf', xe, w_gate)
    b = jnp.einsum('becd,edf->becf', xe, w_up)
    ye = jnp.einsum('becf,efd->becd', jax.nn.silu(a) * b, w_down)
    return jnp.zeros_like(h).at[bidx, idx].add(ye * gates[..., None].astype(h.dtype))

def first_inputs(seed: int = 0) -> dict:
    key = jax.random.key(seed)
    ks = jax.random.split(key, 20)
    f32 = jnp.float32
    nrm = lambda k, shape, s: jax.random.normal(k, shape, f32) * s
    gain = lambda k, shape: 1.0 + 0.02 * jax.random.normal(k, shape, f32)
    L = DEPTH
    return {
        "x": nrm(ks[0], (BATCH, SEQ, D_MODEL), 1.0),
        "p": nrm(ks[1], (L, BATCH, SEQ, PLE_DIM), 1.0),
        "norm_mix": gain(ks[2], (L, D_MODEL)),
        "w_in": nrm(ks[3], (L, D_MODEL, POOL_WIDTH + 3 * ATTN_WIDTH), D_MODEL ** -0.5),
        "w_pool": nrm(ks[4], (L, len(POOL_WINDOWS), POOL_GROUP, POOL_GROUP), POOL_GROUP ** -0.5),
        "pool_scale": gain(ks[5], (L, POOL_WIDTH)),
        "q_norm": gain(ks[6], (L, HEAD_DIM)),
        "k_norm": gain(ks[7], (L, HEAD_DIM)),
        "rpb": nrm(ks[8], (L, ATTN_HEADS, 2 * WIN_ROWS_MAX - 1, 2 * WIN_COLS - 1), 0.1),
        "w_out": nrm(ks[9], (L, MIX_WIDTH, D_MODEL), MIX_WIDTH ** -0.5),
        "norm_ffn": gain(ks[10], (L, D_MODEL)),
        "w_router": nrm(ks[11], (L, D_MODEL, N_EXPERTS), D_MODEL ** -0.5),
        "w_gate": nrm(ks[12], (L, N_EXPERTS, D_MODEL, D_EXPERT), D_MODEL ** -0.5),
        "w_up": nrm(ks[13], (L, N_EXPERTS, D_MODEL, D_EXPERT), D_MODEL ** -0.5),
        "w_down": nrm(ks[14], (L, N_EXPERTS, D_EXPERT, D_MODEL), D_EXPERT ** -0.5),
        "norm_ple": gain(ks[15], (L, D_MODEL)),
        "w_ple_gate": nrm(ks[16], (L, D_MODEL, D_MODEL), D_MODEL ** -0.5),
        "w_ple_proj": nrm(ks[17], (L, PLE_DIM, D_MODEL), PLE_DIM ** -0.5),
        "norm_ple_post": gain(ks[18], (L, D_MODEL)),
    }

def first_block(x, p, norm_mix, w_in, w_pool, pool_scale, q_norm, k_norm, rpb, w_out,
              norm_ffn, w_router, w_gate, w_up, w_down, norm_ple, w_ple_gate,
              w_ple_proj, norm_ple_post):
    B, S, _ = x.shape
    for i in range(DEPTH):
        h = rms_norm(x, norm_mix[i])
        z = h @ w_in[i]
        u = z[..., :POOL_WIDTH]
        qkv = z[..., POOL_WIDTH:].reshape(B, S, 3, ATTN_HEADS, HEAD_DIM)
        y_pool = multiscale_pool(u, w_pool[i], pool_scale[i])
        y_attn = neighbourhood_attention(qkv[:, :, 0], qkv[:, :, 1], qkv[:, :, 2],
                                         q_norm[i], k_norm[i], rpb[i])
        x = x + jnp.concatenate([y_pool, y_attn], axis=-1) @ w_out[i]
        x = x + expert_choice_ffn(rms_norm(x, norm_ffn[i]), w_router[i], w_gate[i], w_up[i], w_down[i])
        g = jax.nn.sigmoid(rms_norm(x, norm_ple[i]) @ w_ple_gate[i])
        e = rms_norm(p[i] @ w_ple_proj[i], norm_ple_post[i])
        x = x + g * e
    return x


MEM_LEN = 256
EPS = 1e-6
NEG_INF = -1e30
BIG = 1e30

NSA_HEADS = 16
NSA_GROUPS = 4
NSA_HPG = NSA_HEADS // NSA_GROUPS
NSA_DH = 64
NSA_SCALE = NSA_DH ** -0.5
CMP_BLOCK = 32
CMP_STRIDE = 16
CMP_HIDDEN = 128
SEL_BLOCK = 64
SEL_TOPK = 16
N_LOCAL_FORCED = 2
WINDOW = 512
SEL_QBLOCK = 32
WIN_QBLOCK = 128

ML_HEADS = 4
ML_DH = 128
ML_CHUNK = 64
CONV_WIDTH = 4

MEM_HEADS = 4
MEM_DH = 128
MEM_SCALE = MEM_DH ** -0.5

D_FF = -(-8 * D_MODEL // (3 * 256)) * 256

N_BRANCH = 3
NSA_Q = NSA_HEADS * NSA_DH
NSA_KV = NSA_GROUPS * NSA_DH
ML_W = ML_HEADS * ML_DH
MEM_W = MEM_HEADS * MEM_DH
IN_SPLITS = (NSA_Q, 6 * NSA_KV, 3 * NSA_HEADS, 3 * ML_W, 2 * ML_HEADS, ML_W, MEM_W, N_BRANCH * D_MODEL)
IN_WIDTH = NSA_Q + 6 * NSA_KV + 3 * NSA_HEADS + 3 * ML_W + 2 * ML_HEADS + ML_W + MEM_W + N_BRANCH * D_MODEL


def rmsnorm(x, g):
    xf = x.astype(jnp.float32)
    y = xf * lax.rsqrt(jnp.mean(xf * xf, axis=-1, keepdims=True) + EPS)
    return (y * g.astype(jnp.float32)).astype(x.dtype)

def masked_softmax(s, mask):
    s = jnp.where(mask, s.astype(jnp.float32), NEG_INF)
    return jax.nn.softmax(s, axis=-1) * mask

def compress_blocks(kv, pe, w1, w2):
    S = kv.shape[1]
    n_cmp = (S - CMP_BLOCK) // CMP_STRIDE + 1
    idx = jnp.arange(n_cmp)[:, None] * CMP_STRIDE + jnp.arange(CMP_BLOCK)[None, :]
    blocks = kv[:, idx] + pe[None, None, :, None, :]
    hid = jax.nn.silu(jnp.einsum('bnlgd,ldh->bngh', blocks, w1))
    return jnp.einsum('bngh,hd->bngd', hid, w2)

def nsa_compressed(q, k, v, pe_k, w1_k, w2_k, pe_v, w1_v, w2_v):
    S = q.shape[1]
    kc = compress_blocks(k, pe_k, w1_k, w2_k)
    vc = compress_blocks(v, pe_v, w1_v, w2_v)
    n_cmp = kc.shape[1]
    s = jnp.einsum('bsghd,bngd->bghsn', q, kc) * NSA_SCALE
    t = jnp.arange(S)
    end = jnp.arange(n_cmp) * CMP_STRIDE + CMP_BLOCK - 1
    p = masked_softmax(s, end[None, :] <= t[:, None])
    o = jnp.einsum('bghsn,bngd->bsghd', p.astype(vc.dtype), vc)
    return o, p

def cmp_to_sel_map(n_cmp, n_sel):
    c0 = jnp.arange(n_cmp) * CMP_STRIDE
    s0 = jnp.arange(n_sel) * SEL_BLOCK
    ov = jnp.minimum(c0[:, None] + CMP_BLOCK, s0[None, :] + SEL_BLOCK) - jnp.maximum(c0[:, None], s0[None, :])
    return jnp.clip(ov, 0, None).astype(jnp.float32) / CMP_BLOCK

def nsa_select(p_cmp, S):
    n_cmp = p_cmp.shape[-1]
    n_sel = S // SEL_BLOCK
    imp = jnp.einsum('bghsn,nj->bgsj', p_cmp, cmp_to_sel_map(n_cmp, n_sel))
    qblk = jnp.arange(S) // SEL_BLOCK
    j = jnp.arange(n_sel)
    rel = qblk[:, None] - j[None, :]
    causal = rel >= 0
    forced = causal & ((j[None, :] == 0) | (rel < N_LOCAL_FORCED))
    score = jnp.where(forced, BIG, jnp.where(causal, imp, NEG_INF))
    top_s, top_i = lax.top_k(score, min(SEL_TOPK, n_sel))
    return top_i, top_s > 0.5 * NEG_INF

def nsa_selected(q, k, v, top_i, top_ok):
    B, S, G, HPG, dh = q.shape
    n_sel = S // SEL_BLOCK
    nk = top_i.shape[-1]
    nq = S // SEL_QBLOCK
    kb = k.reshape(B, n_sel, SEL_BLOCK, G, dh).transpose(0, 3, 1, 2, 4)
    vb = v.reshape(B, n_sel, SEL_BLOCK, G, dh).transpose(0, 3, 1, 2, 4)
    qb = jnp.moveaxis(q.reshape(B, nq, SEL_QBLOCK, G, HPG, dh), 1, 0)
    ib = jnp.moveaxis(top_i.reshape(B, G, nq, SEL_QBLOCK, nk), 2, 0)
    mb = jnp.moveaxis(top_ok.reshape(B, G, nq, SEL_QBLOCK, nk), 2, 0)
    bi = jnp.arange(B)[:, None, None, None]
    gi = jnp.arange(G)[None, :, None, None]

    def body(args):
        qi, ii, mi, blk = args
        kg = kb[bi, gi, ii]
        vg = vb[bi, gi, ii]
        tpos = blk * SEL_QBLOCK + jnp.arange(SEL_QBLOCK)
        kpos = ii[..., None] * SEL_BLOCK + jnp.arange(SEL_BLOCK)
        mask = mi[..., None] & (kpos <= tpos[None, None, :, None, None])
        s = jnp.einsum('bqghd,bgqnld->bghqnl', qi, kg) * NSA_SCALE
        p = masked_softmax(s.reshape(B, G, HPG, SEL_QBLOCK, nk * SEL_BLOCK),
                           mask.reshape(B, G, 1, SEL_QBLOCK, nk * SEL_BLOCK))
        p = p.reshape(B, G, HPG, SEL_QBLOCK, nk, SEL_BLOCK).astype(vg.dtype)
        return jnp.einsum('bghqnl,bgqnld->bqghd', p, vg)

    out = lax.map(body, (qb, ib, mb, jnp.arange(nq)))
    return jnp.moveaxis(out, 0, 1).reshape(B, S, G, HPG, dh)

def nsa_window(q, k, v):
    B, S, G, HPG, dh = q.shape
    nq = S // WIN_QBLOCK
    span = WIN_QBLOCK + WINDOW
    kp = jnp.pad(k, ((0, 0), (WINDOW, 0), (0, 0), (0, 0)))
    vp = jnp.pad(v, ((0, 0), (WINDOW, 0), (0, 0), (0, 0)))
    qb = jnp.moveaxis(q.reshape(B, nq, WIN_QBLOCK, G, HPG, dh), 1, 0)

    def body(args):
        qi, blk = args
        start = blk * WIN_QBLOCK
        ks = lax.dynamic_slice_in_dim(kp, start, span, axis=1)
        vs = lax.dynamic_slice_in_dim(vp, start, span, axis=1)
        tpos = start + jnp.arange(WIN_QBLOCK)
        kpos = start - WINDOW + jnp.arange(span)
        d = tpos[:, None] - kpos[None, :]
        mask = (d >= 0) & (d < WINDOW) & (kpos[None, :] >= 0)
        s = jnp.einsum('bqghd,bkgd->bghqk', qi, ks) * NSA_SCALE
        p = masked_softmax(s, mask).astype(vs.dtype)
        return jnp.einsum('bghqk,bkgd->bqghd', p, vs)

    out = lax.map(body, (qb, jnp.arange(nq)))
    return jnp.moveaxis(out, 0, 1).reshape(B, S, G, HPG, dh)

def causal_conv(x, w, b):
    C = x.shape[-1]
    y = lax.conv_general_dilated(x, w[:, None, :], window_strides=(1,), padding=[(CONV_WIDTH - 1, 0)],
                                 dimension_numbers=('NWC', 'WIO', 'NWC'), feature_group_count=C)
    return y + b

def mlstm_chunkwise(q, k, v, i_pre, logf):
    B, S, H, dh = q.shape
    L = ML_CHUNK
    nc = S // L
    q = q.astype(jnp.float32)
    k = k.astype(jnp.float32) * (dh ** -0.5)
    v = v.astype(jnp.float32)

    def chunks(a):
        return jnp.moveaxis(a.reshape(B, nc, L, *a.shape[2:]), 1, 0)

    tril = jnp.tril(jnp.ones((L, L), dtype=bool))

    def step(carry, xs):
        C, n, m = carry
        qj, kj, vj, ij, fj = xs
        qh = qj.transpose(0, 2, 1, 3)
        kh = kj.transpose(0, 2, 1, 3)
        vh = vj.transpose(0, 2, 1, 3)
        b = jnp.cumsum(fj, axis=1).transpose(0, 2, 1)
        ih = ij.transpose(0, 2, 1)
        dlog = jnp.where(tril, b[..., :, None] - b[..., None, :] + ih[..., None, :], -jnp.inf)
        inter = b + m[..., None]
        m_t = jnp.maximum(inter, jnp.max(dlog, axis=-1))
        dw = jnp.exp(dlog - m_t[..., None])
        iw = jnp.exp(inter - m_t)
        sqk = jnp.einsum('bhld,bhsd->bhls', qh, kh) * dw
        num = jnp.einsum('bhls,bhsd->bhld', sqk, vh) + iw[..., None] * jnp.einsum('bhed,bhld->bhle', C, qh)
        den = jnp.sum(sqk, axis=-1) + iw * jnp.einsum('bhd,bhld->bhl', n, qh)
        h = num / jnp.maximum(jnp.abs(den), jnp.exp(-m_t))[..., None]
        b_end = b[..., -1]
        wlog = b_end[..., None] - b + ih
        m_new = jnp.maximum(b_end + m, jnp.max(wlog, axis=-1))
        ws = jnp.exp(wlog - m_new[..., None])
        decay = jnp.exp(b_end + m - m_new)
        C_new = decay[..., None, None] * C + jnp.einsum('bhs,bhse,bhsd->bhed', ws, vh, kh)
        n_new = decay[..., None] * n + jnp.einsum('bhs,bhsd->bhd', ws, kh)
        return (C_new, n_new, m_new), h

    init = (jnp.zeros((B, H, dh, dh), jnp.float32), jnp.zeros((B, H, dh), jnp.float32), jnp.zeros((B, H), jnp.float32))
    _, hs = lax.scan(step, init, (chunks(q), chunks(k), chunks(v), chunks(i_pre), chunks(logf)))
    return hs.transpose(1, 0, 3, 2, 4).reshape(B, S, H, dh)

def memory_xattn(q, mem, g, w_kv):
    B, S, _ = q.shape
    M = mem.shape[1]
    kv = rmsnorm(mem, g) @ w_kv
    k = kv[..., :MEM_W].reshape(B, M, MEM_HEADS, MEM_DH)
    v = kv[..., MEM_W:].reshape(B, M, MEM_HEADS, MEM_DH)
    qh = q.reshape(B, S, MEM_HEADS, MEM_DH)
    s = jnp.einsum('bshd,bmhd->bhsm', qh, k).astype(jnp.float32) * MEM_SCALE
    p = jax.nn.softmax(s, axis=-1).astype(v.dtype)
    return jnp.einsum('bhsm,bmhd->bshd', p, v).reshape(B, S, MEM_W)

def second_inputs(seed: int = 0) -> dict:
    key = jax.random.key(seed)
    ks = jax.random.split(key, 32)
    L = DEPTH

    def nrm(k, shape, scale):
        return jax.random.normal(k, shape, jnp.float32) * scale

    def gain(k, shape):
        return 1.0 + 0.05 * jax.random.normal(k, shape, jnp.float32)

    gate_b = jnp.concatenate([
        0.1 * jax.random.normal(ks[10], (L, ML_HEADS), jnp.float32),
        jnp.linspace(3.0, 6.0, ML_HEADS, dtype=jnp.float32)[None, :] + 0.1 * jax.random.normal(ks[11], (L, ML_HEADS), jnp.float32),
    ], axis=-1)
    return {
        "x": nrm(ks[0], (BATCH, SEQ, D_MODEL), 1.0),
        "mem": nrm(ks[1], (BATCH, MEM_LEN, D_MODEL), 1.0),
        "g_pre_mix": gain(ks[2], (L, D_MODEL)),
        "w_in": nrm(ks[3], (L, D_MODEL, IN_WIDTH), D_MODEL ** -0.5),
        "cmp_pe_k": nrm(ks[4], (L, CMP_BLOCK, NSA_DH), 0.1),
        "cmp_w1_k": nrm(ks[5], (L, CMP_BLOCK, NSA_DH, CMP_HIDDEN), (CMP_BLOCK * NSA_DH) ** -0.5),
        "cmp_w2_k": nrm(ks[6], (L, CMP_HIDDEN, NSA_DH), CMP_HIDDEN ** -0.5),
        "cmp_pe_v": nrm(ks[7], (L, CMP_BLOCK, NSA_DH), 0.1),
        "cmp_w1_v": nrm(ks[8], (L, CMP_BLOCK, NSA_DH, CMP_HIDDEN), (CMP_BLOCK * NSA_DH) ** -0.5),
        "cmp_w2_v": nrm(ks[9], (L, CMP_HIDDEN, NSA_DH), CMP_HIDDEN ** -0.5),
        "ml_conv_w": nrm(ks[12], (L, CONV_WIDTH, 2 * ML_W), CONV_WIDTH ** -0.5),
        "ml_conv_b": nrm(ks[13], (L, 2 * ML_W), 0.02),
        "ml_gate_b": gate_b,
        "ml_head_g": gain(ks[14], (L, ML_W)),
        "g_mem": gain(ks[15], (L, D_MODEL)),
        "w_mem_kv": nrm(ks[16], (L, D_MODEL, 2 * MEM_W), D_MODEL ** -0.5),
        "w_proj_nsa": nrm(ks[17], (L, NSA_Q, D_MODEL), NSA_Q ** -0.5),
        "w_proj_ml": nrm(ks[18], (L, ML_W, D_MODEL), ML_W ** -0.5),
        "w_proj_mem": nrm(ks[19], (L, MEM_W, D_MODEL), MEM_W ** -0.5),
        "w_out": nrm(ks[20], (L, D_MODEL, D_MODEL), D_MODEL ** -0.5),
        "g_post_mix": gain(ks[21], (L, D_MODEL)),
        "g_pre_ffn": gain(ks[22], (L, D_MODEL)),
        "w_ffn_in": nrm(ks[23], (L, D_MODEL, 2 * D_FF), D_MODEL ** -0.5),
        "w_ffn_down": nrm(ks[24], (L, D_FF, D_MODEL), D_FF ** -0.5),
        "g_post_ffn": gain(ks[25], (L, D_MODEL)),
    }

def second_block(x, mem, g_pre_mix, w_in, cmp_pe_k, cmp_w1_k, cmp_w2_k, cmp_pe_v, cmp_w1_v, cmp_w2_v,
              ml_conv_w, ml_conv_b, ml_gate_b, ml_head_g, g_mem, w_mem_kv, w_proj_nsa, w_proj_ml,
              w_proj_mem, w_out, g_post_mix, g_pre_ffn, w_ffn_in, w_ffn_down, g_post_ffn):
    B, S, _ = x.shape
    offsets = np.cumsum(IN_SPLITS)[:-1].tolist()
    for l in range(DEPTH):
        h = rmsnorm(x, g_pre_mix[l])
        z = h @ w_in[l]
        q_nsa, kv_nsa, g_nsa, qkv_ml, if_ml, o_ml, q_mem, g_merge = jnp.split(z, offsets, axis=-1)

        q = q_nsa.reshape(B, S, NSA_GROUPS, NSA_HPG, NSA_DH)
        kv = kv_nsa.reshape(B, S, 6, NSA_GROUPS, NSA_DH)
        o_cmp, p_cmp = nsa_compressed(q, kv[:, :, 0], kv[:, :, 1], cmp_pe_k[l], cmp_w1_k[l], cmp_w2_k[l],
                                      cmp_pe_v[l], cmp_w1_v[l], cmp_w2_v[l])
        top_i, top_ok = nsa_select(p_cmp, S)
        o_slc = nsa_selected(q, kv[:, :, 2], kv[:, :, 3], top_i, top_ok)
        o_win = nsa_window(q, kv[:, :, 4], kv[:, :, 5])
        gb = jax.nn.sigmoid(g_nsa.reshape(B, S, NSA_GROUPS, NSA_HPG, 3))
        y_nsa = (gb[..., 0:1] * o_cmp + gb[..., 1:2] * o_slc + gb[..., 2:3] * o_win).reshape(B, S, NSA_Q)

        qk = jax.nn.silu(causal_conv(qkv_ml[..., :2 * ML_W], ml_conv_w[l], ml_conv_b[l]))
        q_m = qk[..., :ML_W].reshape(B, S, ML_HEADS, ML_DH)
        k_m = qk[..., ML_W:].reshape(B, S, ML_HEADS, ML_DH)
        v_m = qkv_ml[..., 2 * ML_W:].reshape(B, S, ML_HEADS, ML_DH)
        gates = if_ml.astype(jnp.float32) + ml_gate_b[l].astype(jnp.float32)
        i_pre = gates[..., :ML_HEADS]
        logf = jax.nn.log_sigmoid(gates[..., ML_HEADS:])
        h_ml = mlstm_chunkwise(q_m, k_m, v_m, i_pre, logf)
        h_ml = h_ml * lax.rsqrt(jnp.mean(h_ml * h_ml, axis=-1, keepdims=True) + EPS)
        h_ml = h_ml.reshape(B, S, ML_W) * ml_head_g[l].astype(jnp.float32)
        y_ml = (jax.nn.sigmoid(o_ml.astype(jnp.float32)) * h_ml).astype(x.dtype)

        y_mem = memory_xattn(q_mem, mem, g_mem[l], w_mem_kv[l])

        gm = jax.nn.sigmoid(g_merge.reshape(B, S, N_BRANCH, D_MODEL))
        y = (gm[:, :, 0] * (y_nsa @ w_proj_nsa[l]) + gm[:, :, 1] * (y_ml @ w_proj_ml[l])
             + gm[:, :, 2] * (y_mem @ w_proj_mem[l]))
        x = x + rmsnorm(y @ w_out[l], g_post_mix[l])

        h = rmsnorm(x, g_pre_ffn[l])
        gu = h @ w_ffn_in[l]
        gate, up = gu[..., :D_FF], gu[..., D_FF:]
        x = x + rmsnorm((jax.nn.silu(gate) * up) @ w_ffn_down[l], g_post_ffn[l])
    return x


def setup_inputs(seed=0):
    out = dict(first_inputs(seed))
    for name, value in second_inputs(seed + 1).items():
        if name != "x":
            out[name + "_2"] = value
    return out


def reference(
    x, p, norm_mix, w_in, w_pool, pool_scale, q_norm, k_norm, rpb, w_out, norm_ffn, w_router,
    w_gate, w_up, w_down, norm_ple, w_ple_gate, w_ple_proj, norm_ple_post, mem_2, g_pre_mix_2,
    w_in_2, cmp_pe_k_2, cmp_w1_k_2, cmp_w2_k_2, cmp_pe_v_2, cmp_w1_v_2, cmp_w2_v_2, ml_conv_w_2,
    ml_conv_b_2, ml_gate_b_2, ml_head_g_2, g_mem_2, w_mem_kv_2, w_proj_nsa_2, w_proj_ml_2,
    w_proj_mem_2, w_out_2, g_post_mix_2, g_pre_ffn_2, w_ffn_in_2, w_ffn_down_2, g_post_ffn_2,
):
    x = first_block(
        x, p, norm_mix, w_in, w_pool, pool_scale, q_norm, k_norm, rpb, w_out, norm_ffn,
        w_router, w_gate, w_up, w_down, norm_ple, w_ple_gate, w_ple_proj, norm_ple_post,
    )
    return second_block(
        x, mem_2, g_pre_mix_2, w_in_2, cmp_pe_k_2, cmp_w1_k_2, cmp_w2_k_2, cmp_pe_v_2,
        cmp_w1_v_2, cmp_w2_v_2, ml_conv_w_2, ml_conv_b_2, ml_gate_b_2, ml_head_g_2, g_mem_2,
        w_mem_kv_2, w_proj_nsa_2, w_proj_ml_2, w_proj_mem_2, w_out_2, g_post_mix_2, g_pre_ffn_2,
        w_ffn_in_2, w_ffn_down_2, g_post_ffn_2,
    )


_drawn_inputs = setup_inputs


def setup_inputs(seed=0):
    import zlib

    import numpy as np

    out = dict(_drawn_inputs(seed))
    spreads = {}
    factors = {'q_norm': 7.367,
     'k_norm': 5.599,
     'norm_ffn': 2.669,
     'norm_ple': 26.603,
     'norm_ple_post': 17.835,
     'cmp_pe_k_2': 64.0,
     'ml_conv_b_2': 200.0,
     'g_mem_2': 29.757,
     'cmp_w1_k_2': 8.0,
     'cmp_w2_k_2': 8.0,
     'cmp_pe_v_2': 8.0,
     'cmp_w1_v_2': 8.0,
     'cmp_w2_v_2': 6.978,
     'ml_conv_w_2': 11.65,
     'ml_gate_b_2': 3.19,
     'ml_head_g_2': 64.0,
     'w_proj_nsa_2': 5.187,
     'g_post_mix_2': 15.092,
     'g_pre_ffn_2': 4.005,
     'g_post_ffn_2': 16.88}
    for name, (base, spread) in spreads.items():
        noise = np.random.default_rng([zlib.crc32(name.encode()), seed]).standard_normal(out[name].shape)
        drawn = base * np.exp(spread * noise) if base else spread * noise
        out[name] = __import__('jax').numpy.asarray(drawn.astype(out[name].dtype))
    for name, factor in factors.items():
        out[name] = (out[name] * factor).astype(out[name].dtype)
    return out
```

```python
from contextlib import ExitStack

import numpy as np
import concourse.bass as bass
from concourse import mybir

F32 = mybir.dt.float32
I32 = mybir.dt.int32
ALU = mybir.AluOpType
ACT = mybir.ActivationFunctionType
AX = mybir.AxisListType.X

P = 128
T = 256
NT = T // P
D = 1024
KC = D // P
EPS = 1e-6
NEG = -1e30
SLOTS = 6
SLOT = 4096
RSQRT_SEED = float(0x5F3759DF)

PAIRS = 4
HD = 64
GRID_W, WIN_COLS, RPB_R, RPB_C = 64, 16, 15, 31
POOL_WINDOWS = (2, 4, 8, 16)
EXPERTS, CAP, DE = 16, 32, 2048
PLE = 256

GROUPS = 4
N_CMP, CMP_L, CMP_STRIDE = 15, 32, 16
ML_DH = 128
D_FF = 2816
FF_STEPS = D_FF // 256

Q0 = 0
KV0 = 1024
GATE0 = KV0 + 6 * 256
ML0 = GATE0 + 48
IF0 = ML0 + 3 * 512
O0 = IF0 + 8
MEMQ0 = O0 + 512
MERGE0 = MEMQ0 + 512

GAIN = lambda c: 8 * c
PSCALE = 48
CONV = 52
QN, KN = 92, 93
NVEC = 94

CONSTS = [("ident", 128), ("caus", 128), ("causT", 128), ("causTz", 256), ("wmask", 64), ("cmpadd", 32),
          ("cmpmul", 32), ("iota1", 32), ("ones", 128), ("eye4", 4)]
COFF = {}
_n = 0
for _name, _w in CONSTS:
    COFF[_name] = _n
    _n += _w
NCONST = _n


def constants():
    c = np.zeros((P, NCONST), np.float32)

    def put(name, a):
        a = np.asarray(a, np.float32)
        c[:a.shape[0], COFF[name]:COFF[name] + a.shape[1]] = a

    i = np.arange(P)
    put("ident", np.eye(P))
    put("caus", np.where(i[None, :] <= i[:, None], 0.0, NEG))
    put("causT", np.where(i[:, None] <= i[None, :], 0.0, NEG))
    put("causTz", np.concatenate([np.where(i[:, None] <= i[None, :], 0.0, NEG), np.zeros((P, P))], 1))
    col = i % GRID_W
    start = np.clip(col - WIN_COLS // 2, 0, GRID_W - WIN_COLS)
    kc = np.arange(GRID_W)
    put("wmask", np.where((kc[None] >= start[:, None]) & (kc[None] < start[:, None] + WIN_COLS), 0.0, NEG))
    t = np.arange(NT)[None, :, None] * P + i[:, None, None]
    n = np.arange(16)[None, None, :]
    seen = n * CMP_STRIDE + CMP_L - 1 <= t
    put("cmpadd", np.where(seen, 0.0, NEG).reshape(P, 32))
    put("cmpmul", np.where(seen, 1.0, 0.0).reshape(P, 32))
    put("iota1", np.tile(np.arange(1, CAP + 1), (P, 1)))
    put("ones", np.ones((P, P)))
    put("eye4", np.eye(4))
    pool = np.zeros((len(POOL_WINDOWS), T, T), np.float32)
    for g, w in enumerate(POOL_WINDOWS):
        for s in range(T):
            lo = min(max(s - w // 2, 0), T - 1)
            hi = min(max(s + (w - w // 2) - 1, 0), T - 1)
            pool[g, lo:hi + 1, s] += 1.0 / (hi - lo + 1)
            pool[g, s, s] -= 1.0
    return c, np.ascontiguousarray(pool.reshape(4, NT, P, T).transpose(2, 1, 0, 3).reshape(P, NT * 4 * T))


class Chain:

    def __init__(self, eng, sem):
        self.eng, self.sem, self.base, self.n = eng, sem, 0, 0

    def __call__(self, ins):
        ins.then_inc(self.sem, 1)
        self.n += 1
        self.eng.wait_ge(self.sem, self.base + self.n)

    def enter(self, i, per):
        self.before, self.per = self.n, per
        self.base, self.n = i * per + self.before, 0

    def leave(self, times):
        assert self.n == self.per, (self.n, self.per)
        self.base, self.n = 0, self.before + times * self.per


class Ring:

    def __init__(self, eng, full, free):
        self.eng, self.full, self.free = eng, full, free
        self.rounds, self.incs = [0] * SLOTS, [0] * SLOTS

    def load(self, slot, *copies):
        r = self.rounds[slot]
        if not (isinstance(r, int) and r == 0):
            self.eng.wait_ge(self.free[slot], r)
            if not isinstance(r, int):
                self.eng.nop(nofuse=True)
        for dst, src in copies:
            self.eng.dma_start(dst, src).then_inc(self.full[slot], 16)
        self.count(slot, len(copies))

    def count(self, slot, copies):
        self.rounds[slot] = self.rounds[slot] + 1
        self.incs[slot] = self.incs[slot] + 16 * copies

    def arrived(self, slot, copies):
        self.count(slot, copies)
        self.eng.wait_ge(self.full[slot], self.incs[slot])

    def enter(self, i, per):
        self.before, self.per = (list(self.rounds), list(self.incs)), per
        for s, (loads, copies) in per.items():
            self.rounds[s] = i * loads + self.rounds[s]
            self.incs[s] = i * (16 * copies) + self.incs[s]

    def leave(self, times):
        self.rounds, self.incs = list(self.before[0]), list(self.before[1])
        for s, (loads, copies) in self.per.items():
            self.rounds[s] += times * loads
            self.incs[s] += 16 * times * copies


def two_blocks(nc, a, out):
    ctx = ExitStack()
    with ctx:
        def sb(name, n, parts=P):
            return ctx.enter_context(nc.sbuf_tensor(name, [parts, n], F32))

        def sem(name):
            return ctx.enter_context(nc.semaphore(name))

        ring = sb("ring", SLOTS * SLOT)
        slot = [ring[:, s * SLOT:(s + 1) * SLOT] for s in range(SLOTS)]
        strip = [s.rearrange("p (k n) -> p k n", k=KC) for s in slot]
        x = sb("x", NT * D)[:, :].rearrange("p (t d) -> p t d", t=NT)
        xn = sb("xn", NT * D)[:, :].rearrange("p (t d) -> p t d", t=NT)
        hT = sb("hT", KC * T)[:, :].rearrange("p (k t) -> p k t", k=KC)
        yT = sb("yT", KC * T)[:, :].rearrange("p (k t) -> p k t", k=KC)
        yml = sb("yml", 4 * T)[:, :].rearrange("p (k t) -> p k t", k=4)
        ymem = sb("ymem", 4 * T)[:, :].rearrange("p (k t) -> p k t", k=4)
        kTm = sb("kTm", 4 * T)
        vm = sb("vm", NT * 512)[:, :].rearrange("p (t n) -> p t n", t=NT)
        grows = sb("grows", 3 * D)[:, :].rearrange("p (c d) -> p c d", c=3)
        hgrow = sb("hgrow", 512)
        consts = sb("consts", NCONST)
        vec = sb("vec", NVEC)
        peT = sb("peT", CMP_L)
        wr = sb("wr", KC * EXPERTS)[:, :].rearrange("p (k e) -> p k e", k=KC)
        wsm = sb("wsm", KC * 56)[:, :].rearrange("p (k e) -> p k e", k=KC)
        w2 = sb("w2", 2 * HD)
        wp = sb("wp", P)
        ifb = sb("ifb", 2)
        stat = sb("stat", 16)
        rst = sb("rst", 16)
        nt_ = sb("nt_", 40)
        scr = sb("scr", 10420)

        class Area:

            def __init__(self, at=0):
                self.at = at

            def __call__(self, n, pat=None, parts=P, **kw):
                v = scr[0:parts, self.at:self.at + n]
                self.at += n
                assert self.at <= 10420, self.at
                return v.rearrange(pat, **kw) if pat else v

        def const(name, parts=P):
            w = dict(CONSTS)[name]
            return consts[0:parts, COFF[name]:COFF[name] + w]

        ident, caus, causT, causTz = const("ident"), const("caus"), const("causT"), const("causTz")

        ps = ctx.enter_context(nc.psum_tensor("ps", [P, 8, 512], F32))
        bank = [ps[:, b, :] for b in range(8)]

        A = Area()
        poolm = A(NT * 4 * T, "p (t g s) -> p t g s", t=NT, g=4)
        mx = A(NT * D, "p (t d) -> p t d", t=NT)
        zA = A(NT * 512, "p (t n) -> p t n", t=NT)
        sqA = A(NT * T, "p (t n) -> p t n", t=NT)
        qkn = A(NT * T, "p (t n) -> p t n", t=NT)
        qkT = A(2 * T, "p (m t) -> p m t", m=2)
        sA = A(2 * NT * T, "p (a t k) -> p a t k", a=2, t=NT)
        PTA = A(2 * NT * T, "p (a k q) -> p a k q", a=2, k=NT)
        dT = A(T)
        junk = A(D)
        rows = A(P)
        ssA, rsA, nmA, sumA, rcA = A(8), A(8), A(4), A(4), A(4)
        perow = A(P)
        braw = slot[5][:, 0:8 * 6 * GRID_W].rearrange("p (h r c) -> p h r c", h=8, r=6)
        btab = grows.rearrange("p c d -> p (c d)").rearrange("p (h r c) -> p h r c", h=8, r=6)

        B = Area(at=NT * 4 * T + NT * D)
        lgE = B(32, "p (t e) -> p t e", t=NT)
        nmE, smE = B(2), B(2)
        affT, selT, cumT, onesT = (B(T, parts=EXPERTS) for _ in range(4))
        m8 = B(8, parts=EXPERTS)
        posT = B(32, "p (t e) -> p t e", t=NT)
        selall = B(EXPERTS * 128, "p (e t w s) -> p e t w s", e=EXPERTS, t=NT, w=2)
        selflat = scr[:, B.at - EXPERTS * 128:B.at]
        B = Area()
        sele = B(128, "p (t w s) -> p t w s", t=NT, w=2)
        sele_flat = scr[:, 0:128]
        xeT = B(KC * CAP, "p (k s) -> p k s", k=KC)
        thE = B(512)
        hE = B(512)
        hTe = B(512, "p (c n) -> p c n", c=4)
        gT = B(T)
        ysb = B(D)
        assert B.at <= NT * 4 * T + NT * D

        C = Area()
        pin = C(NT * PLE, "p (t n) -> p t n", t=NT)
        pT = C(2 * T, "p (k t) -> p k t", k=2)
        thP = C(NT * D, "p (t d) -> p t d", t=NT)
        uP = C(NT * D, "p (t d) -> p t d", t=NT)

        E = Area()
        gball = E(96)
        stall = E(16)
        kcall = E(4 * 16)
        vcall = E(4 * HD)
        negMd = E(4 * T, parts=4)
        gst, lst, cst, kcg, vcg = E(24), E(4), E(10), E(16), E(HD)
        vmg = E(NT * P, "p (t d) -> p t d", t=NT)
        hgg = E(P)
        zp = E(2 * 259, "p (m t) -> p m t", m=2)
        v1 = E(NT * 132, "p (t e) -> p t e", t=NT)
        Pc = E(NT * 4 * 32, "p (t i n) -> p t i n", t=NT, i=4)
        loop_at = E.at
        qs = E(2 * T, "p (m t) -> p m t", m=2)
        kxy = E(2 * T, "p (m t) -> p m t", m=2)
        vsb = E(NT * P, "p (t d) -> p t d", t=NT)
        yc = E(2 * T, "p (m t) -> p m t", m=2)
        thc = E(2 * T, "p (m t) -> p m t", m=2)
        so = E(NT * P, "p (t d) -> p t d", t=NT)
        tm = E(384)
        Wm = E(384)
        hh = E(NT * P, "p (t d) -> p t d", t=NT)
        y1 = E(NT * P, "p (t d) -> p t d", t=NT)
        qm = E(T)
        Pm = E(NT * T, "p (t k) -> p t k", t=NT)
        PTm = E(NT * T, "p (k q) -> p k q", k=NT)
        sc = E(8 * 16, "p (j n) -> p j n", j=8)
        PTc = E(T)
        Pn = xn.rearrange("p t d -> p (t d)")[:, 0:1536].rearrange("p (a b n) -> p a b n", a=2, b=2)
        PTn = E(2 * 384, "p (b n) -> p b n", b=2)
        nmC, smC, rcC = E(8), E(8), E(8)
        nmN, smN, rcN = (E(8, "p (a b t) -> p a b t", a=2, b=2) for _ in range(3))
        nmM, smM, rcM, dn, ab, rd, ssM = (E(2) for _ in range(7))
        E2 = Area(at=loop_at)
        kvc = E2(5 * T, "p (g t) -> p g t", g=5)
        hidb = E2(2)
        hpre = E2(2 * 60, "p (m n) -> p m n", m=2)
        hth = E2(2 * 60, "p (m n) -> p m n", m=2)
        hidk = E2(60)
        hidv = E2(4 * 32, "p (g n) -> p g n", g=4)
        gth = E2(NT * 48, "p (t n) -> p t n", t=NT)
        iR, fR, mnR, abR, lnR, BR, aR, MR, mR, emR, nMR = (E2(T, parts=4) for _ in range(11))
        G = Area(at=0)
        thG = G(2 * 768, "p (u n) -> p u n", u=2)
        yG = G(2 * 768, "p (u n) -> p u n", u=2)
        yT2 = xn.rearrange("p t d -> p (t d)").rearrange("p (k t) -> p k t", k=KC)
        thF = G(4 * T, "p (u f t) -> p u f t", u=2, f=2)
        vF = G(4 * T, "p (u f t) -> p u f t", u=2, f=2)
        hF = G(4 * T, "p (u f t) -> p u f t", u=2, f=2)
        ysF = G(NT * D, "p (t d) -> p t d", t=NT)

        full = [sem(f"slot{s}_full") for s in range(SLOTS)]
        free = [sem(f"slot{s}_free") for s in range(SLOTS)]
        in_x, in_first, in_pool, in_bias, in_mem, in_late, in_p, in_wp = (
            sem(n) for n in ("in_x", "in_first", "in_pool", "in_bias", "in_mem", "in_late", "in_p", "in_wp"))
        out_done = sem("out_done")
        dve_chain, act_chain, pool_chain = sem("dve_chain"), sem("act_chain"), sem("pool_chain")
        vec_ps, vec_sb, exp_warm = sem("vec_ps"), sem("vec_sb"), sem("exp_warm")
        bias_sb, in_rows = sem("bias_sb"), sem("in_rows")
        ssq_done, xn_done, tr_done, hT_done = sem("ssq_done"), sem("xn_done"), sem("tr_done"), sem("hT_done")
        zA_ps, zA_sb, qknA, qkT_ps, qkT_sb, poolA_ps, dT_sb, poolY_ps, yA_pool = (
            sem(n) for n in ("zA_ps", "zA_sb", "qknA", "qkT_ps", "qkT_sb", "poolA_ps", "dT_sb", "poolY_ps", "yA_pool"))
        sA_ps, maxA, expA, pA, ptA_ps, ptA_sb, oA_ps, yA_attn, wp_used = (
            sem(n) for n in ("sA_ps", "maxA", "expA", "pA", "ptA_ps", "ptA_sb", "oA_ps", "yA_attn", "wp_used"))
        out1_ps, x1_done, mkv_ps, mkv_sb = sem("out1_ps"), sem("x1_done"), sem("mkv_ps"), sem("mkv_sb")
        lg_ps, lg_max, lg_exp, aff_sb, aff_ps, pos_sb, pos_ps, sel_done = (
            sem(n) for n in ("lg_ps", "lg_max", "lg_exp", "aff_sb", "aff_ps", "pos_sb", "pos_ps", "sel_done"))
        sele_sb, xe_ps, xe_sb, gt_ps, gt_sb, gate_ps, up_ps, gate_th, h_sb, ht_ps, ht_sb, y_ps, y_sb, sc_ps, x_acc = (
            sem(n) for n in ("sele_sb", "xe_ps", "xe_sb", "gt_ps", "gt_sb", "gate_ps", "up_ps", "gate_th", "h_sb",
                             "ht_ps", "ht_sb", "y_ps", "y_sb", "sc_ps", "x_acc"))
        pT_ps, pT_sb, g_ps, g_th, e_ps, e_sb, e_sq, x3_done = (
            sem(n) for n in ("pT_ps", "pT_sb", "g_ps", "g_th", "e_ps", "e_sb", "e_sq", "x3_done"))
        ga_ps, if_ps, ga_th, ga_sb, ab_sb, ab_exp, ab_ln, em_in, em_sb, st_sb, st_ps = (
            sem(n) for n in ("ga_ps", "if_ps", "ga_th", "ga_sb", "ab_sb", "ab_exp", "ab_ln", "em_in", "em_sb",
                             "st_sb", "st_ps"))
        kvc_ps, kvc_sb, hid_ps, hid_pre, hid_th, hid_sb, kc_ps, kc_sb = (
            sem(n) for n in ("kvc_ps", "kvc_sb", "hid_ps", "hid_pre", "hid_th", "hid_sb", "kc_ps", "kc_sb"))
        staged, proj_ps, proj_sb, c_conv, c_th, c_qk, d_ps, d_in, d_exp, st_mm, w_sb, n_ps, h_div, h_sq, ym_sb, ym_ps = (
            sem(n) for n in ("staged", "proj_ps", "proj_sb", "c_conv", "c_th", "c_qk", "d_ps", "d_in", "d_exp",
                             "st_mm", "w_sb", "n_ps", "h_div", "h_sq", "ym_sb", "ym_ps"))
        xs_ps, xs_max, xs_exp, xp_sb, xt_ps, xt_sb, xo_ps, ymem_done, yml_done, ynsa_done = (
            sem(n) for n in ("xs_ps", "xs_max", "xs_exp", "xp_sb", "xt_ps", "xt_sb", "xo_ps", "ymem_done",
                             "yml_done", "ynsa_done"))
        cs_ps, cs_in, cs_exp, cp_sb, ct_ps, ct_sb, ns_ps, ns_max, ns_exp, np_sb, nt_ps, nt_sb, no_ps = (
            sem(n) for n in ("cs_ps", "cs_in", "cs_exp", "cp_sb", "ct_ps", "ct_sb", "ns_ps", "ns_max", "ns_exp",
                             "np_sb", "nt_ps", "nt_sb", "no_ps"))
        mg_ps, mp_ps, mg_th, mg_free, out2_ps, y_evac, y_sq, x4_done = (
            sem(n) for n in ("mg_ps", "mp_ps", "mg_th", "mg_free", "out2_ps", "y_evac", "y_sq", "x4_done"))
        ff_ps, ff_th, ff_h, ffo_ps = sem("ff_ps"), sem("ff_th"), sem("ff_h"), sem("ffo_ps")

        FIRST = 1 + 6 + 1 + 10 + 4 + 2
        LATE = 1 + 1 + 2 + 2 + 2
        block = ctx.enter_context(nc.Block())

        def chunks(w):
            return w.rearrange("(k p) n -> p k n", p=P)

        @block.sync
        def _(sp):
            r = Ring(sp, full, free)
            w_in1, w_in2 = a["w_in"][0], a["w_in_2"][0]

            def pair_strip(j):
                src = w_in1.rearrange("(k p) (m n) -> p k m n", p=P, m=4)
                dst = strip[0].rearrange("p k (m n) -> p k m n", m=4)
                return [(dst[:, h:h + 4, m, :], src[:, h:h + 4, m, bass.ds(j * 128, 128)])
                        for h in (0, 4) for m in range(4)]

            def halves(s, w, c0):
                src = chunks(w)
                return [(strip[s][:, h:h + 4, :], src[:, h:h + 4, c0:c0 + 512]) for h in (0, 4)]

            sp.dma_start(x[:, :, :], a["x"][0].rearrange("(t p) d -> p t d", p=P)).then_inc(in_x, 16)
            r.load(0, *pair_strip(0))
            r.load(1, *halves(1, a["w_out"][0], 0))
            r.load(2, *halves(2, a["w_out"][0], 512))
            r.load(0, *pair_strip(1))
            r.load(3, *halves(3, a["w_mem_kv_2"][0], 0))
            r.load(4, *halves(4, a["w_mem_kv_2"][0], 512))
            r.load(0, *pair_strip(2))
            r.load(0, *pair_strip(3))
            r.count(5, 0)

            wide = [s.rearrange("p (k n) -> p k n", k=2) for s in slot]
            tall = [s.rearrange("p (k n) -> p k n", k=4) for s in slot]
            gate = a["w_gate"][0].rearrange("e k f -> (e k) f")
            up = a["w_up"][0].rearrange("e k f -> (e k) f")
            down = a["w_down"][0].rearrange("e k f -> (e k) f")
            with sp.Fori(0, EXPERTS) as e:
                r.enter(e, {s: (2, 2) for s in range(SLOTS)})
                for n in range(8):
                    w, i, s = (gate, up)[n // 4], n % 4, n % SLOTS
                    src = w[bass.ds(e * D + i * 256, 256), :].rearrange("(k p) f -> p k f", p=P)
                    r.load(s, (wide[s], src))
                for n in range(8, 12):
                    i, s = n - 8, n % SLOTS
                    src = down[bass.ds(e * DE + i * 512, 512), :].rearrange("(k p) f -> p k f", p=P)
                    r.load(s, (tall[s], src))
                r.leave(EXPERTS)

            r.load(0, *halves(0, a["w_ple_gate"][0], 0))
            r.load(1, *halves(1, a["w_ple_gate"][0], 512))
            r.load(2, (slot[2][:, 0:2 * D].rearrange("p (k n) -> p k n", k=2), chunks(a["w_ple_proj"][0])))
            r.load(3, *halves(3, w_in2, KV0))
            r.load(4, *[(slot[4][h * HD:h * HD + HD, :].rearrange("p (l h) -> p l h", l=CMP_L),
                         a[n][0].rearrange("l d h -> d l h")) for h, n in enumerate(("cmp_w1_k_2", "cmp_w1_v_2"))])
            w2c = chunks(w_in2)
            kv = w_in2[:, KV0:KV0 + 1536].rearrange("(k p) (s n) -> p k s n", p=P, s=6)
            ml = w_in2[:, ML0:ML0 + 1536].rearrange("(k p) (s n) -> p k s n", p=P, s=3)
            kvd = strip[5][:, :, 256:512].rearrange("p k (s n) -> p k s n", s=4)
            mld = strip[0][:, :, 0:384].rearrange("p k (s n) -> p k s n", s=3)
            with sp.Fori(0, GROUPS) as g:
                r.enter(g, {0: (1, 4), 1: (1, 1), 5: (1, 5)})
                r.load(0, *[(mld[:, :, s, :], ml[:, :, s, bass.ds(g * 128, 128)]) for s in range(3)],
                       (strip[0][:, :, 384:512], w2c[:, :, bass.ds(g * 128 + O0, 128)]))
                r.load(1, (slot[1][:, 0:D].rearrange("p (k n) -> p k n", k=KC),
                           w2c[:, :, bass.ds(g * 128 + MEMQ0, 128)]))
                r.load(5, (strip[5][:, :, 0:256], w2c[:, :, bass.ds(g * 256, 256)]),
                       *[(kvd[:, :, n, :], kv[:, :, s, bass.ds(g * HD, HD)]) for n, s in enumerate((2, 4, 3, 5))])
                r.leave(GROUPS)
            gm = w_in2[:, MERGE0:MERGE0 + 3 * D].rearrange("(k p) (b n) -> p k b n", p=P, b=3)
            pn, pl, pe_ = (chunks(a[n][0]) for n in ("w_proj_nsa_2", "w_proj_ml_2", "w_proj_mem_2"))
            with sp.Fori(0, 4) as i:
                r.enter(i, {s: (1, 3) for s in (2, 3, 4, 5)})
                for u in range(2):
                    c = bass.ds(i * 256 + u * 128, 128)
                    gd = slot[2 + 2 * u][:, 0:3072].rearrange("p (k b n) -> p k b n", k=KC, b=3)
                    pd = slot[3 + 2 * u][:, 0:2048].rearrange("p (k n) -> p k n", k=16)
                    r.load(2 + 2 * u, *[(gd[:, :, b, :], gm[:, :, b, c]) for b in range(3)])
                    r.load(3 + 2 * u, (pd[:, 0:8, :], pn[:, :, c]), (pd[:, 8:12, :], pl[:, :, c]),
                           (pd[:, 12:16, :], pe_[:, :, c]))
                r.leave(4)
            r.load(0, *halves(0, a["w_out_2"][0], 0))
            r.load(1, *halves(1, a["w_out_2"][0], 512))
            gu = a["w_ffn_in_2"][0].rearrange("(k p) (m n) -> p k m n", p=P, m=2)
            dn_ = a["w_ffn_down_2"][0]

            def ff(s, par):
                A_ = strip[2 + 2 * par].rearrange("p k (m n) -> p k m n", m=2)
                B_ = slot[3 + 2 * par][:, 0:2 * D].rearrange("p (k n) -> p k n", k=2)
                r.load(2 + 2 * par, *[(A_[:, :, m, :], gu[:, :, m, bass.ds(s * 256, 256)]) for m in range(2)])
                r.load(3 + 2 * par, (B_, chunks(dn_[bass.ds(s * 256, 256), :])))

            ff(0, 0)
            ff(1, 1)
            with sp.Fori(0, 4) as i:
                r.enter(i, {2: (1, 2), 3: (1, 1), 4: (1, 2), 5: (1, 1)})
                ff(i * 2 + 2, 0)
                ff(i * 2 + 3, 1)
                r.leave(4)
            ff(10, 0)
            for t in range(NT):
                sp.wait_ge(x4_done, 3 + t)
                sp.dma_start(out[0][t * P:(t + 1) * P, :], x[:, t, :]).then_inc(out_done, 16)
            sp.wait_ge(out_done, 16 * NT)

        @block.gpsimd
        def _(g_):
            g_.dma_start(wp[:, :], a["w_pool"][0, 0]).then_inc(in_wp, 16)
            for j in range(1, PAIRS):
                g_.wait_ge(wp_used, j)
                g_.dma_start(wp[:, :], a["w_pool"][0, j]).then_inc(in_wp, 16)
            g_.wait_ge(sel_done, 2)
            with g_.Fori(0, EXPERTS) as e:
                g_.tensor_copy(sele_flat, selflat[:, bass.ds(e * 128, 128)]).then_inc(sele_sb, 1)
                g_.wait_ge(gt_ps, e + 1)
            g_.wait_ge(st_sb, 2)
            g_.wait_ge(ga_sb, 1)
            g_.wait_ge(kc_sb, 2)
            with g_.Fori(0, GROUPS) as g:
                for dst, src, n in ((cst, vec[:, CONV:CONV + 40], 10), (lst, stall, 4), (hgg, hgrow[:, :], P),
                                    (kcg, kcall, 16), (vcg, vcall, HD), (gst, gball, 24)):
                    g_.tensor_copy(dst, src[:, bass.ds(g * n, n)]).then_inc(staged, 1)
                g_.tensor_copy(vmg, vm[:, :, bass.ds(g * P, P)]).then_inc(staged, 1)
                g_.wait_ge(ynsa_done, g * 2 + 2)
                g_.wait_ge(yml_done, g + 1)
                g_.wait_ge(ymem_done, g + 1)

        @block.scalar
        def _(act):
            chain = Chain(act, act_chain)
            small = [(consts[:, :], a["consts"])]
            for c, n in enumerate(("norm_mix", "g_mem_2", "norm_ffn", "norm_ple", "g_pre_mix_2", "g_pre_ffn_2")):
                small.append((rows[GAIN(c):GAIN(c) + 8, :], a[n][0].rearrange("(k p) -> k p", p=P)))
            small.append((rows[PSCALE:PSCALE + 4, :], a["pool_scale"][0].rearrange("(k p) -> k p", p=P)))
            for m in range(2):
                for j in range(4):
                    small.append((rows[CONV + 5 * m + j:CONV + 40:10, :],
                                  a["ml_conv_w_2"][0, j].rearrange("(m h p) -> m h p", m=2, p=P)[m]))
                small.append((rows[CONV + 5 * m + 4:CONV + 40:10, :],
                              a["ml_conv_b_2"][0].rearrange("(m h p) -> m h p", m=2, p=P)[m]))
            for n, c in (("q_norm", QN), ("k_norm", KN)):
                for h in range(2):
                    small.append((rows[c:c + 1, h * HD:h * HD + HD], a[n]))
            for h, n in enumerate(("cmp_pe_k_2", "cmp_pe_v_2")):
                small.append((perow[0:CMP_L, h * HD:h * HD + HD], a[n][0]))
            assert len(small) == FIRST
            for dst, src in small:
                act.dma_start(dst, src).then_inc(in_first, 16)
            for half in range(2):
                for h in range(8):
                    src = bass.AP(a["rpb"].tensor, h * RPB_R * RPB_C + (5 - half) * RPB_C + WIN_COLS
                                  - GRID_W, [[1, GRID_W], [RPB_C, 6], [1, GRID_W]])
                    act.dma_start(braw[half * 64:half * 64 + 64, h, :, :], src).then_inc(in_bias, 16)
            act.dma_start(poolm[:, :, :, :], a["pool"].rearrange("p (t g s) -> p t g s", t=NT, g=4)).then_inc(in_pool, 16)
            act.dma_start(mx[:, :, :], a["mem_2"][0].rearrange("(t p) d -> p t d", p=P)).then_inc(in_mem, 16)
            late = []
            late.append((hgrow[:, :], a["ml_head_g_2"][0].partition_broadcast(P)))
            late.append((wr[:, :, :], chunks(a["w_router"][0])))
            late.append((wsm[:, :, 0:48], chunks(a["w_in_2"][0])[:, :, GATE0:GATE0 + 48]))
            late.append((wsm[:, :, 48:56], chunks(a["w_in_2"][0])[:, :, IF0:IF0 + 8]))
            late.append((w2[:, 0:HD], a["cmp_w2_k_2"][0]))
            late.append((w2[:, HD:2 * HD], a["cmp_w2_v_2"][0]))
            for c in range(2):
                late.append((ifb[0:4, c:c + 1], a["ml_gate_b_2"][0].rearrange("(c h u) -> c h u", c=2, u=1)[c]))
            assert len(late) == LATE
            for dst, src in late:
                act.dma_start(dst, src).then_inc(in_late, 16)
            act.wait_ge(exp_warm, 1)
            act.activation(nt_[:, 33:34], nt_[:, 32:33], ACT.Exp)

            def squares(c, src):
                for t in range(NT):
                    if 2 * c + t:
                        act.wait_ge(ssq_done, 2 * c + t)
                    act.activation(junk, src[:, t, :], ACT.Square, accum_out=stat[:, 2 * c + t:2 * c + t + 1])\
                       .then_inc(ssq_done, 1)

            act.wait_ge(in_x, 16)
            squares(0, x)
            act.wait_ge(in_mem, 16)
            squares(1, mx)

            with act.Fori(0, PAIRS) as j:
                for t in range(NT):
                    act.wait_ge(zA_ps, j * 2 + t + 1)
                    act.activation(zA[:, t, :], bank[t], ACT.Copy).then_inc(zA_sb, 1)
                act.wait_ge(poolA_ps, j + 1)
                act.activation(dT, bank[3][:, 0:T], ACT.Copy).then_inc(dT_sb, 1)
                for h in range(2):
                    act.wait_ge(maxA, j * 2 + h + 1)
                    for t in range(NT):
                        e = act.activation(sA[:, h, t, :], sA[:, h, t, :], ACT.Exp,
                                           bias=nmA[:, 2 * h + t:2 * h + t + 1],
                                           accum_out=sumA[:, 2 * h + t:2 * h + t + 1])
                    e.then_inc(expA, 1)
                for h in range(2):
                    act.wait_ge(ptA_ps, j * 2 + h + 1)
                    act.activation(PTA[:, h, :, :], bank[6 + h].rearrange("p (k q) -> p k q", k=NT), ACT.Copy)\
                       .then_inc(ptA_sb, 1)
                act.wait_ge(oA_ps, j * 2 + 2)
                act.nop(nofuse=True)
                act.activation(yT[:, bass.ds(j + 4, 1), :].rearrange("p a t -> p (a t)"), bank[2][:, 0:T], ACT.Copy)\
                   .then_inc(yA_attn, 1)

            for c, n in enumerate(("norm_ple_post", "g_post_mix_2", "g_post_ffn_2")):
                act.dma_start(grows[:, c, :], a[n][0].partition_broadcast(P)).then_inc(in_rows, 16)
            for b in range(4):
                act.wait_ge(mkv_ps, b + 1)
                dst = kTm[:, (b % 2) * 512:(b % 2) * 512 + 512] if b < 2 else vm[:, b - 2, :]
                act.activation(dst, bank[4 + b], ACT.Copy).then_inc(mkv_sb, 1)
            act.wait_ge(x1_done, 4)
            squares(2, x)
            act.wait_ge(lg_max, 1)
            for t in range(NT):
                e = act.activation(lgE[:, t, :], bank[4][:, t * 16:t * 16 + 16], ACT.Exp, bias=nmE[:, t:t + 1],
                                   accum_out=smE[:, t:t + 1])
            e.then_inc(lg_exp, 1)

            with act.Fori(0, EXPERTS) as e:
                act.wait_ge(gt_ps, e + 1)
                act.activation(gT, bank[2][:, 0:T], ACT.Copy).then_inc(gt_sb, 1)
                act.wait_ge(gate_ps, e + 1)
                act.activation(thE, bank[0], ACT.Tanh, scale=0.5).then_inc(gate_th, 1)
                act.wait_ge(ht_ps, e + 1)
                act.activation(hTe.rearrange("p c n -> p (c n)"), bank[2], ACT.Copy).then_inc(ht_sb, 1)
                act.wait_ge(y_ps, e + 1)
                act.activation(ysb[:, 0:512], bank[4], ACT.Copy).then_inc(y_sb, 1)
                act.wait_ge(sc_ps, e * 4 + 4)

            act.dma_start(pin[:, :, :], a["p"][0, 0].rearrange("(t p) d -> p t d", p=P)).then_inc(in_p, 16)
            act.wait_ge(x_acc, 4 * EXPERTS)
            squares(3, x)
            act.wait_ge(pT_ps, 1)
            act.activation(pT.rearrange("p k t -> p (k t)"), bank[0], ACT.Copy).then_inc(pT_sb, 1)
            for b in range(4):
                act.wait_ge(e_ps, b + 1)
                act.activation(xn[:, b // 2, (b % 2) * 512:(b % 2) * 512 + 512], bank[b], ACT.Copy)\
                   .then_inc(e_sb, 1)
            act.wait_ge(e_sb, 4)
            for t in range(NT):
                if t:
                    act.wait_ge(e_sq, t)
                act.activation(junk, xn[:, t, :], ACT.Square, accum_out=stat[:, 12 + t:13 + t]).then_inc(e_sq, 1)
            for b in range(4):
                act.wait_ge(g_ps, b + 1)
                act.activation(thP[:, b // 2, (b % 2) * 512:(b % 2) * 512 + 512], bank[4 + b], ACT.Tanh, scale=0.5)\
                   .then_inc(g_th, 1)
            act.wait_ge(e_sq, 2)
            act.wait_ge(x3_done, 2)
            squares(4, x)

            act.wait_ge(ga_ps, 1)
            act.activation(gth.rearrange("p t n -> p (t n)"), bank[4][:, 0:96], ACT.Tanh, scale=0.5).then_inc(ga_th, 1)
            for b in range(2):
                act.wait_ge(kvc_ps, b + 1)
                act.activation(kvc[:, 2 * b:2 * b + 2, :], bank[6 + b].rearrange("p (g t) -> p g t", g=2), ACT.Copy)\
                   .then_inc(kvc_sb, 1)
            act.wait_ge(hid_pre, 1)
            act.activation(hth, hpre, ACT.Tanh, scale=0.5).then_inc(hid_th, 1)
            act.wait_ge(ab_sb, 1)
            chain(act.activation(lnR, abR, ACT.Exp, scale=-1.0))
            act.activation(lnR, lnR, ACT.Ln, bias=1.0).then_inc(ab_ln, 1)
            act.wait_ge(em_in, 1)
            act.activation(emR, mR, ACT.Exp, scale=-1.0).then_inc(em_sb, 1)
            act.activation(nt_[:, 33:34], nt_[:, 32:33], ACT.Tanh)

            def heads_exp(n, i):
                act.wait_ge(ns_max, n + i + 1)
                o = i % 2
                for b in range(2):
                    for t, c in ((0, slice(0, 128)), (1, slice(128, 384))):
                        e = act.activation(Pn[:, o, b, c], bank[2 * o + b][:, c], ACT.Exp,
                                           bias=nmN[:, o, b, t:t + 1], accum_out=smN[:, o, b, t:t + 1])
                e.then_inc(ns_exp, 1)

            def heads_turned(n, i):
                act.wait_ge(nt_ps, n + i + 1)
                act.activation(PTn, ps[:, 4:6, 0:384], ACT.Copy).then_inc(nt_sb, 1)

            def nsa_out(n, g, pair):
                act.wait_ge(no_ps, n + 2 * pair + 2)
                act.nop(nofuse=True)
                act.activation(yT[:, bass.ds(g * 2 + pair, 1), :].rearrange("p a t -> p (a t)"),
                               bank[6 + pair][:, 0:T], ACT.Copy).then_inc(ynsa_done, 1)

            with act.Fori(0, GROUPS) as g:
                n4 = g * 4
                act.wait_ge(staged, g * 7 + 7)
                act.wait_ge(proj_ps, g * 6 + 1)
                act.activation(zp[:, :, 3:259], bank[3].rearrange("p (m t) -> p m t", m=2), ACT.Copy)\
                   .then_inc(proj_sb, 1)
                act.wait_ge(proj_ps, g * 6 + 2)
                vo = bank[4].rearrange("p (t n) -> p t n", t=NT)
                act.activation(v1[:, :, 0:128], vo[:, :, 0:128], ACT.Copy).then_inc(proj_sb, 1)
                act.activation(so, vo[:, :, 128:256], ACT.Tanh, scale=0.5).then_inc(proj_sb, 1)
                act.wait_ge(proj_ps, g * 6 + 3)
                act.activation(qm, bank[5][:, 0:T], ACT.Copy, scale=ML_DH ** -0.5).then_inc(proj_sb, 1)
                act.wait_ge(c_conv, g + 1)
                act.activation(thc, yc, ACT.Tanh, scale=0.5).then_inc(c_th, 1)
                act.wait_ge(proj_ps, g * 6 + 4)
                act.activation(qs, bank[0].rearrange("p (m t) -> p m t", m=2), ACT.Copy, scale=HD ** -0.5)\
                   .then_inc(proj_sb, 1)
                act.wait_ge(d_in, g + 1)
                act.activation(tm[:, 0:256], tm[:, 0:256], ACT.Exp, bias=lst[:, 0:1])
                act.activation(tm[:, 256:384], tm[:, 256:384], ACT.Exp, bias=lst[:, 1:2]).then_inc(d_exp, 1)
                act.wait_ge(xs_max, g + 1)
                for t in range(NT):
                    e = act.activation(Pm[:, t, :], bank[7][:, t * T:t * T + T], ACT.Exp, bias=nmM[:, t:t + 1],
                                       accum_out=smM[:, t:t + 1])
                e.then_inc(xs_exp, 1)
                act.wait_ge(proj_ps, g * 6 + 5)
                act.activation(kxy, bank[1].rearrange("p (m t) -> p m t", m=2), ACT.Copy).then_inc(proj_sb, 1)
                act.wait_ge(proj_ps, g * 6 + 6)
                act.activation(vsb, bank[2][:, 0:256].rearrange("p (t n) -> p t n", t=NT), ACT.Copy)\
                   .then_inc(proj_sb, 1)
                act.wait_ge(xt_ps, g + 1)
                act.activation(PTm, bank[3].rearrange("p (k q) -> p k q", k=NT), ACT.Copy).then_inc(xt_sb, 1)
                act.wait_ge(cs_in, g + 1)
                act.activation(sc[:, :, 0:N_CMP], sc[:, :, 0:N_CMP], ACT.Exp).then_inc(cs_exp, 1)
                act.wait_ge(xo_ps, g + 1)
                act.nop(nofuse=True)
                act.activation(ymem[:, bass.ds(g, 1), :].rearrange("p a t -> p (a t)"), bank[4][:, 0:T], ACT.Copy)\
                   .then_inc(ymem_done, 1)
                act.wait_ge(h_div, g + 1)
                for t in range(NT):
                    e = act.activation(y1[:, t, :], hh[:, t, :], ACT.Square, accum_out=ssM[:, t:t + 1])
                e.then_inc(h_sq, 1)
                heads_exp(n4, 0)
                act.wait_ge(ct_ps, g + 1)
                act.activation(PTc, bank[4][:, 0:T], ACT.Copy).then_inc(ct_sb, 1)
                heads_exp(n4, 1)
                heads_turned(n4, 0)
                heads_exp(n4, 2)
                heads_turned(n4, 1)
                nsa_out(n4, g, 0)
                heads_exp(n4, 3)
                heads_turned(n4, 2)
                heads_turned(n4, 3)
                nsa_out(n4, g, 1)
                act.wait_ge(ym_ps, g + 1)
                act.nop(nofuse=True)
                act.activation(yml[:, bass.ds(g, 1), :].rearrange("p a t -> p (a t)"), bank[0][:, 0:T], ACT.Copy,
                               scale=0.5).then_inc(yml_done, 1)

            with act.Fori(0, 4) as i:
                for u in range(2):
                    m = i * 2 + u
                    act.wait_ge(mg_free, m + 1)
                    act.wait_ge(mg_ps, m + 1)
                    act.activation(thG[:, u, 0:512], bank[4 * u], ACT.Tanh, scale=0.5)
                    act.activation(thG[:, u, 512:768], bank[4 * u + 1][:, 0:T], ACT.Tanh, scale=0.5)\
                       .then_inc(mg_th, 1)

            def post(base, dst, scale):
                if base:
                    act.wait_ge(ssq_done, 12)
                for b in range(4):
                    act.wait_ge((out2_ps, ffo_ps)[base], b + 1)
                    act.activation(dst[:, b // 2, (b % 2) * 512:(b % 2) * 512 + 512], bank[b], ACT.Copy,
                                   scale=scale).then_inc(y_evac, 1)
                act.wait_ge(y_evac, 4 * base + 4)
                for t in range(NT):
                    if base or t:
                        act.wait_ge(y_sq, 2 * base + t)
                    act.activation(junk, dst[:, t, :], ACT.Square,
                                   accum_out=stat[:, 14 - 2 * base + t:15 - 2 * base + t]).then_inc(y_sq, 1)

            post(0, ysF, 0.5)
            act.wait_ge(y_sq, 2)
            act.wait_ge(x4_done, 2)
            squares(5, x)

            def ff(s, par):
                for f in range(2):
                    act.wait_ge(ff_ps, s * 2 + f + 1)
                    act.activation(thF[:, par, f, :], bank[4 + 2 * par + f][:, 0:T], ACT.Tanh, scale=0.5)\
                       .then_inc(ff_th, 1)

            ff(0, 0)
            ff(1, 1)
            with act.Fori(0, 4) as i:
                ff(i * 2 + 2, 0)
                ff(i * 2 + 3, 1)
            ff(10, 0)
            post(1, ysF, 1.0)

        @block.tensor
        def _(pe):
            r = Ring(pe, full, free)

            def mm(o, l, rr, start=True, stop=True):
                return pe.matmul(o, l, rr, start=start, stop=stop)

            def turn(c, src, b0):
                pe.wait_ge(xn_done, 2 * c + 2)
                for t in range(NT):
                    for h in range(2):
                        for k in range(4):
                            kk = 4 * h + k
                            ins = pe.transpose(bank[b0 + 2 * t + h][:, k * P:(k + 1) * P],
                                               src[:, t, kk * P:(kk + 1) * P], ident)
                        ins.then_inc(tr_done, 1)

            def product(o, w, n=KC, src=None, l0=0):
                for k in range(n):
                    ins = mm(o, w(k), (hT if src is None else src)[:, k, :], k == 0, k == n - 1)
                return ins

            pe.wait_ge(in_first, 16 * FIRST)
            pe.transpose(bank[7][:, 0:NVEC], rows[0:NVEC, :], ident[0:NVEC, 0:NVEC])
            pe.transpose(bank[7][:, 128:128 + CMP_L], perow[0:CMP_L, :], ident[0:CMP_L, 0:CMP_L]).then_inc(vec_ps, 1)
            turn(0, xn, 0)
            pe.wait_ge(hT_done, 4)
            pe.wait_ge(vec_sb, 2)
            pe.wait_ge(in_pool, 16)

            with pe.Fori(0, PAIRS) as j:
                r.enter(j, {0: (1, 8)})
                r.arrived(0, 8)
                for t in range(NT):
                    for k in range(KC):
                        ins = mm(bank[t], hT[:, k, t * P:(t + 1) * P], strip[0][:, k, :], k == 0, k == KC - 1)
                    ins.then_inc(zA_ps, 1)
                pe.wait_ge(zA_sb, j * 2 + 2)
                for t in range(NT):
                    ins = mm(bank[3][:, 0:T], zA[:, t, 0:P], poolm[:, t, bass.ds(j, 1), :].rearrange("p a s -> p (a s)"),
                             t == 0, t == NT - 1)
                    if t == 0:
                        ins.then_inc(free[0], 1)
                ins.then_inc(poolA_ps, 1)
                pe.wait_ge(qknA, j + 1)
                for m in range(2):
                    for t in range(NT):
                        ins = pe.transpose(bank[2][:, m * T + t * P:m * T + (t + 1) * P],
                                           qkn[:, t, m * P:(m + 1) * P], ident)
                ins.then_inc(qkT_ps, 1)
                pe.wait_ge(in_wp, j * 16 + 16)
                pe.wait_ge(dT_sb, j + 1)
                mm(bank[3][:, T:2 * T], wp[:, :], dT).then_inc(poolY_ps, 1)
                pe.wait_ge(qkT_sb, j * 2 + 2)
                pe.nop(nofuse=True)
                for h in range(2):
                    for t in range(NT):
                        ins = mm(bank[4 + h][:, t * T:(t + 1) * T], qkT[64 * h:64 * h + 64, 0, t * P:(t + 1) * P],
                                 qkT[64 * h:64 * h + 64, 1, :])
                        if h == 0 and t == 0:
                            ins.then_inc(wp_used, 1)
                    ins.then_inc(sA_ps, 1)
                for h in range(2):
                    pe.wait_ge(pA, j * 2 + h + 1)
                    for k in range(NT):
                        for t in range(NT):
                            ins = pe.transpose(bank[6 + h][:, k * T + t * P:k * T + (t + 1) * P],
                                               sA[:, h, t, k * P:(k + 1) * P], ident)
                    ins.then_inc(ptA_ps, 1)
                for h in range(2):
                    pe.wait_ge(ptA_sb, j * 2 + h + 1)
                    for k in range(NT):
                        ins = mm(bank[2][64 * h:64 * h + 64, 0:T], zA[:, k, 384 + 64 * h:448 + 64 * h],
                                 PTA[:, h, k, :], k == 0, k == NT - 1)
                    ins.then_inc(oA_ps, 1)
                r.leave(PAIRS)

            pe.wait_ge(yA_attn, PAIRS)
            pe.wait_ge(yA_pool, PAIRS)
            r.count(5, 0)
            for n in range(2):
                r.arrived(1 + n, 2)
                for t in range(NT):
                    for k in range(KC):
                        ins = mm(bank[2 * n + t], yT[:, k, t * P:(t + 1) * P], strip[1 + n][:, k, :], k == 0, k == KC - 1)
                    ins.then_inc(out1_ps, 1)
            turn(1, mx, 4)
            pe.wait_ge(hT_done, 8)
            r.arrived(3, 2)
            for h in range(4):
                for k in range(KC):
                    ins = mm(bank[4 + h // 2][:, (h % 2) * T:(h % 2) * T + T], strip[3][:, k, h * P:(h + 1) * P],
                             hT[:, k, :], k == 0, k == KC - 1)
                    if h == 0 and k < 2:
                        ins.then_inc(free[1 + k], 1)
                if h % 2:
                    ins.then_inc(mkv_ps, 1)
            r.arrived(4, 2)
            for t in range(NT):
                for k in range(KC):
                    ins = mm(bank[6 + t], hT[:, k, t * P:(t + 1) * P], strip[4][:, k, :], k == 0, k == KC - 1)
                    if t == 0 and k == 0:
                        ins.then_inc(free[3], 1)
                ins.then_inc(mkv_ps, 1)
            turn(2, xn, 0)
            pe.wait_ge(hT_done, 12)
            pe.wait_ge(in_late, 16 * LATE)
            pe.wait_ge(mkv_sb, 4)
            for t in range(NT):
                for k in range(KC):
                    ins = mm(bank[4][:, t * 16:t * 16 + 16], hT[:, k, t * P:(t + 1) * P], wr[:, k, :], k == 0, k == KC - 1)
                    if t == 0 and k == 0:
                        ins.then_inc(free[4], 1)
            ins.then_inc(lg_ps, 1)
            pe.wait_ge(aff_sb, 1)
            for t in range(NT):
                ins = pe.transpose(bank[5][0:EXPERTS, t * P:(t + 1) * P], lgE[:, t, :], ident)
            ins.then_inc(aff_ps, 1)
            pe.wait_ge(pos_sb, 1)
            for t in range(NT):
                ins = pe.transpose(bank[6][:, t * 16:t * 16 + 16], cumT[:, t * P:(t + 1) * P], ident[0:EXPERTS, 0:EXPERTS])
            ins.then_inc(pos_ps, 1)

            wide = [s.rearrange("p (k n) -> p k n", k=2) for s in slot]
            tall = [s.rearrange("p (k n) -> p k n", k=4) for s in slot]
            with pe.Fori(0, EXPERTS) as e:
                r.enter(e, {s: (2, 2) for s in range(SLOTS)})
                pe.wait_ge(sele_sb, e + 1)
                for k in range(KC):
                    for t in range(NT):
                        ins = mm(bank[3][:, k * CAP:(k + 1) * CAP], xn[:, t, k * P:(k + 1) * P], sele[:, t, 0, :],
                                 t == 0, t == NT - 1)
                ins.then_inc(xe_ps, 1)
                for t in range(NT):
                    for c in range(4):
                        ins = mm(bank[2][32 * c:32 * c + 32, t * P:(t + 1) * P], sele[:, t, 1, :], ident)
                ins.then_inc(gt_ps, 1)
                pe.wait_ge(xe_sb, e + 1)
                for n in range(8):
                    s = n % SLOTS
                    r.arrived(s, 1)
                    for k in (2 * (n % 4), 2 * (n % 4) + 1):
                        for c in range(4):
                            ins = mm(bank[n // 4][32 * c:32 * c + 32, :], xeT[:, k, :],
                                     wide[s][:, k % 2, c * 512:(c + 1) * 512], k == 0, k == KC - 1)
                            if k % 2 and c == 3 and n % 4 != 3:
                                ins.then_inc(free[s], 1)
                            if n == 4 and k == 0 and c == 0:
                                ins.then_inc(free[3], 1)
                    if n % 4 == 3:
                        ins.then_inc((gate_ps, up_ps)[n // 4], 1)
                pe.wait_ge(h_sb, e + 1)
                pe.wait_ge(gt_sb, e + 1)
                for c in range(4):
                    ins = pe.transpose(bank[2][:, c * P:(c + 1) * P], hE[:, c * P:(c + 1) * P], ident)
                    if c == 0:
                        ins.then_inc(free[1], 1)
                ins.then_inc(ht_ps, 1)
                pe.wait_ge(ht_sb, e + 1)
                for i in range(4):
                    s = (8 + i) % SLOTS
                    r.arrived(s, 1)
                    for h in range(2):
                        for c in range(4):
                            ins = mm(bank[4 + h][32 * c:32 * c + 32, :], hTe[:, c, 32 * i:32 * i + 32],
                                     tall[s][:, c, h * 512:(h + 1) * 512], i == 0, i == 3)
                    if i < 3:
                        ins.then_inc(free[s], 1)
                ins.then_inc(y_ps, 1)
                pe.wait_ge(y_sb, e * 2 + 2)
                for t in range(NT):
                    for h in range(2):
                        ins = mm(bank[(6, 4)[t] + h], gT[:, t * P:(t + 1) * P], ysb[:, h * 512:(h + 1) * 512])
                        ins.then_inc(sc_ps, 1)
                pe.wait_ge(sc_ps, e * 4 + 4)
                pe.sem_inc(free[5], 1)
                r.leave(EXPERTS)

            pe.wait_ge(in_p, 16)
            for k in range(2):
                for t in range(NT):
                    ins = pe.transpose(bank[0][:, k * T + t * P:k * T + (t + 1) * P], pin[:, t, k * P:(k + 1) * P], ident)
            ins.then_inc(pT_ps, 1)
            turn(3, xn, 4)
            pe.wait_ge(pT_sb, 1)
            r.arrived(2, 1)
            wple = slot[2][:, 0:2 * D].rearrange("p (k n) -> p k n", k=2)
            for t in range(NT):
                for h in range(2):
                    for k in range(2):
                        ins = mm(bank[2 * t + h], pT[:, k, t * P:(t + 1) * P], wple[:, k, h * 512:(h + 1) * 512], k == 0, k == 1)
                    ins.then_inc(e_ps, 1)
            pe.wait_ge(hT_done, 16)
            r.arrived(0, 2)
            r.arrived(1, 2)
            first = True
            for t in range(NT):
                for h in range(2):
                    for k in range(KC):
                        ins = mm(bank[4 + 2 * t + h], hT[:, k, t * P:(t + 1) * P], strip[h][:, k, :], k == 0, k == KC - 1)
                        if first:
                            ins.then_inc(free[2], 1)
                            first = False
                    ins.then_inc(g_ps, 1)

            turn(4, xn, 0)
            pe.wait_ge(hT_done, 20)
            for t in range(NT):
                for k in range(KC):
                    ins = mm(bank[4][:, t * 48:t * 48 + 48], hT[:, k, t * P:(t + 1) * P], wsm[:, k, 0:48], k == 0, k == KC - 1)
                    if t == 0 and k < 2:
                        ins.then_inc(free[k], 1)
            ins.then_inc(ga_ps, 1)
            for m in range(2):
                for k in range(KC):
                    ins = mm(bank[5][0:4, m * T:(m + 1) * T], wsm[:, k, 48 + 4 * m:52 + 4 * m], hT[:, k, :], k == 0, k == KC - 1)
            ins.then_inc(if_ps, 1)
            r.arrived(3, 2)
            for g in range(GROUPS):
                o = bank[6 + g // 2][:, (g % 2) * T:(g % 2) * T + T]
                for k in range(KC):
                    for m in range(2):
                        ins = mm(o[64 * m:64 * m + 64, :], strip[3][:, k, m * 256 + g * HD:m * 256 + g * HD + HD],
                                 hT[:, k, :], k == 0, k == KC - 1)
                if g % 2:
                    ins.then_inc(kvc_ps, 1)
            pe.wait_ge(kvc_sb, 3)
            r.arrived(4, 2)
            w1 = slot[4].rearrange("p (l h) -> p l h", l=CMP_L)
            for l in range(CMP_L):
                for m in range(2):
                    ins = mm(bank[m][:, 0:75].rearrange("p (g n) -> p g n", g=5), w1[64 * m:64 * m + 64, l, :],
                             kvc[64 * m:64 * m + 64, :, l:l + CMP_STRIDE * (N_CMP - 1) + 1:CMP_STRIDE],
                             l == 0, l == CMP_L - 1)
                    if l == 0 and m == 0:
                        ins.then_inc(free[3], 1)
            ins.then_inc(hid_ps, 1)
            pe.wait_ge(hid_sb, 1)
            for m in range(2):
                mm(bank[2][64 * m:64 * m + 64, 0:60], w2[:, 0:HD], hidk)
            for g in range(GROUPS):
                for i in range(4):
                    ins = mm(bank[3][32 * i:32 * i + 32, g * HD:(g + 1) * HD], hidv[:, g, :], w2[:, HD:2 * HD])
            ins.then_inc(kc_ps, 1)
            pe.wait_ge(em_sb, 1)
            for n, row in enumerate((aR, emR)):
                for t in range(NT):
                    ins = pe.transpose(bank[7][:, (n * 2 + t) * 4:(n * 2 + t) * 4 + 4], row[:, t * P:(t + 1) * P],
                                       ident[0:4, 0:4])
                    if n == 0 and t == 0:
                        ins.then_inc(free[4], 1)
            ins.then_inc(st_ps, 1)
            pe.wait_ge(st_sb, 2)
            pe.wait_ge(kc_sb, 2)

            def scores(g, i):
                par, hp = i % 2, i // 2
                for b in range(2):
                    key = kxy[64 * par:64 * par + 64, b ^ par, :]
                    q = qs[64 * par:64 * par + 64, hp, :]
                    o = bank[2 * par + b]
                    mm(o[:, 0:128], q[:, 0:128], key[:, 0:128])
                    ins = mm(o[:, 128:384], q[:, 128:256], key)
                ins.then_inc(ns_ps, 1)

            def turned(n4, i):
                pe.wait_ge(np_sb, n4 + i + 1)
                for b in range(2):
                    for c in range(3):
                        ins = pe.transpose(bank[4 + b][:, c * P:(c + 1) * P], Pn[:, i % 2, b, c * P:(c + 1) * P], ident)
                ins.then_inc(nt_ps, 1)

            def values(n4, i):
                pe.wait_ge(nt_sb, n4 + i + 1)
                par, hp = i % 2, i // 2
                o = bank[6 + hp][64 * par:64 * par + 64, :]
                mm(o[:, 0:T], vsb[:, 0, 0:64], PTn[:, 0, 0:256], True, False)
                mm(o[:, 0:T], vsb[:, 0, 64:128], PTn[:, 1, 0:256], False, False)
                mm(o[:, 128:256], vsb[:, 1, 0:64], PTn[:, 0, 256:384], False, False)
                mm(o[:, 128:256], vsb[:, 1, 64:128], PTn[:, 1, 256:384], False, False)
                mm(o[:, 0:T], vcg[32 * i:32 * i + 32, :], PTc[32 * i:32 * i + 32, :], False, True).then_inc(no_ps, 1)

            memq = slot[1][:, 0:D].rearrange("p (k n) -> p k n", k=KC)
            with pe.Fori(0, GROUPS) as g:
                r.enter(g, {0: (1, 4), 1: (1, 1), 5: (1, 5)})
                n4 = g * 4
                pe.wait_ge(staged, g * 7 + 7)
                r.arrived(0, 4)
                for m in range(2):
                    ins = product(bank[3][:, m * T:(m + 1) * T], lambda k: strip[0][:, k, m * P:(m + 1) * P])
                ins.then_inc(proj_ps, 1)
                for t in range(NT):
                    for k in range(KC):
                        ins = mm(bank[4][:, t * T:(t + 1) * T], hT[:, k, t * P:(t + 1) * P], strip[0][:, k, 256:512],
                                 k == 0, k == KC - 1)
                ins.then_inc(proj_ps, 1)
                r.arrived(1, 1)
                product(bank[5][:, 0:T], lambda k: memq[:, k, :]).then_inc(proj_ps, 1)
                r.arrived(5, 5)
                for m in range(2):
                    ins = product(bank[0][:, m * T:(m + 1) * T], lambda k: strip[5][:, k, m * P:(m + 1) * P])
                ins.then_inc(proj_ps, 1)
                mm(bank[6][:, 0:T], const("ones", 4), negMd[:, bass.ds(g * T, T)]).then_inc(d_ps, 1)
                pe.wait_ge(proj_sb, g * 7 + 4)
                for t in range(NT):
                    ins = mm(bank[7][:, t * T:(t + 1) * T], qm[:, t * P:(t + 1) * P], kTm[:, bass.ds(g * T, T)])
                    if t == 0:
                        ins.then_inc(free[0], 1)
                ins.then_inc(xs_ps, 1)
                for k in range(KC):
                    ins = mm(bank[1][:, 0:T], strip[5][:, k, 256:384], hT[:, k, :], k == 0, k == KC - 1)
                    if k == 0:
                        ins.then_inc(free[1], 1)
                for k in range(KC):
                    mm(bank[1][0:64, T:2 * T], strip[5][:, k, 320:384], hT[:, k, :], k == 0, k == KC - 1)
                    ins = mm(bank[1][64:128, T:2 * T], strip[5][:, k, 256:320], hT[:, k, :], k == 0, k == KC - 1)
                ins.then_inc(proj_ps, 1)
                pe.wait_ge(c_qk, g + 1)
                mm(bank[5][:, 0:T], yc[:, 1, 0:P], yc[:, 0, :])
                mm(bank[5][:, T:T + P], yc[:, 1, P:T], yc[:, 0, P:T]).then_inc(st_mm, 1)
                for t in range(NT):
                    for k in range(KC):
                        ins = mm(bank[2][:, t * P:(t + 1) * P], hT[:, k, t * P:(t + 1) * P], strip[5][:, k, 384:512],
                                 k == 0, k == KC - 1)
                ins.then_inc(proj_ps, 1)
                pe.wait_ge(xp_sb, g + 1)
                for k in range(NT):
                    for t in range(NT):
                        ins = pe.transpose(bank[3][:, k * T + t * P:k * T + (t + 1) * P], Pm[:, t, k * P:(k + 1) * P], ident)
                        if k == 0 and t == 0:
                            ins.then_inc(free[5], 1)
                ins.then_inc(xt_ps, 1)
                pe.wait_ge(d_in, g + 1)
                pe.wait_ge(proj_sb, g * 7 + 5)
                pe.nop(nofuse=True)
                for par in range(2):
                    for hp in range(2):
                        for t in range(NT):
                            c = (hp * 2 + t) * 16
                            ins = mm(bank[6 + par][:, c:c + N_CMP], qs[64 * par:64 * par + 64, hp, t * P:(t + 1) * P],
                                     kcg[64 * par:64 * par + 64, 0:N_CMP])
                ins.then_inc(cs_ps, 1)
                pe.wait_ge(xt_sb, g + 1)
                for k in range(NT):
                    ins = mm(bank[4][:, 0:T], vmg[:, k, :], PTm[:, k, :], k == 0, k == NT - 1)
                ins.then_inc(xo_ps, 1)
                pe.wait_ge(w_sb, g + 1)
                mm(bank[5][:, 0:129], Wm[:, 0:128], v1[:, 0, 0:129])
                mm(bank[5][:, 132:261], Wm[:, 128:256], v1[:, 0, 0:129], True, False)
                mm(bank[5][:, 132:261], Wm[:, 256:384], v1[:, 1, 0:129], False, True).then_inc(n_ps, 1)
                pe.wait_ge(proj_sb, g * 7 + 7)
                pe.nop(nofuse=True)
                scores(g, 0)
                scores(g, 1)
                pe.wait_ge(ymem_done, g + 1)
                pe.wait_ge(cp_sb, g + 1)
                for t in range(NT):
                    ins = pe.transpose(bank[4][:, t * P:(t + 1) * P], Pc[:, t, :, :].rearrange("p i n -> p (i n)"), ident)
                ins.then_inc(ct_ps, 1)
                pe.wait_ge(ct_sb, g + 1)
                pe.wait_ge(h_div, g + 1)
                turned(n4, 0)
                scores(g, 2)
                values(n4, 0)
                turned(n4, 1)
                scores(g, 3)
                values(n4, 1)
                turned(n4, 2)
                values(n4, 2)
                turned(n4, 3)
                values(n4, 3)
                pe.wait_ge(ym_sb, g + 1)
                for t in range(NT):
                    ins = pe.transpose(bank[0][:, t * P:(t + 1) * P], y1[:, t, :], ident)
                ins.then_inc(ym_ps, 1)
                r.leave(GROUPS)

            pe.wait_ge(ynsa_done, 8)
            pe.wait_ge(yml_done, 4)
            pe.wait_ge(ymem_done, 4)
            with pe.Fori(0, 4) as i:
                r.enter(i, {s: (1, 3) for s in (2, 3, 4, 5)})
                for u in range(2):
                    gs = slot[2 + 2 * u][:, 0:3072].rearrange("p (k n) -> p k n", k=KC)
                    pj = slot[3 + 2 * u][:, 0:2048].rearrange("p (k n) -> p k n", k=16)
                    pe.wait_ge(mg_free, i * 2 + u + 1)
                    r.arrived(2 + 2 * u, 3)
                    for b in range(3):
                        ins = product(bank[4 * u + b // 2][:, (b % 2) * T:(b % 2) * T + T],
                                      lambda k: gs[:, k, b * P:(b + 1) * P])
                    ins.then_inc(mg_ps, 1)
                    r.arrived(3 + 2 * u, 3)
                    ins = product(bank[4 * u + 2][:, 0:T], lambda k: pj[:, k, :], KC, yT)
                    ins.then_inc(free[2 + 2 * u], 1)
                    product(bank[4 * u + 2][:, T:2 * T], lambda k: pj[:, 8 + k, :], 4, yml)
                    ins = product(bank[4 * u + 3][:, 0:T], lambda k: pj[:, 12 + k, :], 4, ymem)
                    ins.then_inc(mp_ps, 1)
                    pe.wait_ge(mp_ps, i * 2 + u + 1)
                    pe.sem_inc(free[3 + 2 * u], 1)
                r.leave(4)
            pe.wait_ge(mg_free, 10)
            r.arrived(0, 2)
            r.arrived(1, 2)
            for t in range(NT):
                for h in range(2):
                    for k in range(KC):
                        ins = mm(bank[2 * t + h], yT2[:, k, t * P:(t + 1) * P], strip[h][:, k, :], k == 0, k == KC - 1)
                    ins.then_inc(out2_ps, 1)
            turn(5, xn, 4)
            pe.wait_ge(hT_done, 24)

            def ff_in(s, par):
                r.arrived(2 + 2 * par, 2)
                for f in range(2):
                    o = bank[4 + 2 * par + f]
                    for m in range(2):
                        ins = product(o[:, m * T:(m + 1) * T],
                                      lambda k: strip[2 + 2 * par][:, k, m * 256 + f * P:m * 256 + (f + 1) * P])
                    ins.then_inc(ff_ps, 1)

            def ff_down(s, par, first=False, last=False):
                r.arrived(3 + 2 * par, 1)
                w = slot[3 + 2 * par][:, 0:2 * D].rearrange("p (k n) -> p k n", k=2)
                pe.wait_ge(ff_h, s * 2 + 2)
                for k in range(2):
                    for t in range(NT):
                        for h in range(2):
                            ins = mm(bank[2 * t + h], hF[:, par, k, t * P:(t + 1) * P], w[:, k, h * 512:(h + 1) * 512],
                                     first and k == 0, last and k == 1)
                            if last and k == 1:
                                ins.then_inc(ffo_ps, 1)
                            elif k == 0 and t == 0 and h == 0:
                                ins.then_inc(free[2 + 2 * par], 1)
                if not last:
                    ins.then_inc(free[3 + 2 * par], 1)

            ff_in(0, 0)
            ff_in(1, 1)
            ff_down(0, 0, first=True)
            with pe.Fori(0, 4) as i:
                r.enter(i, {2: (1, 2), 3: (1, 1), 4: (1, 2), 5: (1, 1)})
                ff_in(i * 2 + 2, 0)
                ff_down(i * 2 + 1, 1)
                ff_in(i * 2 + 3, 1)
                ff_down(i * 2 + 2, 0)
                r.leave(4)
            ff_in(10, 0)
            ff_down(9, 1)
            ff_down(10, 0, last=True)

        @block.vector
        def _(dve):
            chain = Chain(dve, dve_chain)
            RS = 12

            def rsqrt(o, ss, n, w):
                v, y, q = nt_[:, 0:w], nt_[:, 8:8 + w], nt_[:, 16:16 + w]
                chain(dve.tensor_scalar(v, ss, 1.0 / n, EPS, ALU.mult, ALU.add))
                chain(dve.tensor_scalar(y.bitcast(I32), v.bitcast(I32), 1, None, ALU.logical_shift_right))
                chain(dve.tensor_scalar(y.bitcast(I32), y.bitcast(I32), -1.0, RSQRT_SEED, ALU.mult, ALU.add))
                for it in range(3):
                    chain(dve.tensor_tensor(q, y, y, ALU.mult))
                    chain(dve.scalar_tensor_tensor(out=q, in0=q, scalar=-0.5, in1=v, op0=ALU.mult, op1=ALU.mult))
                    chain(dve.scalar_tensor_tensor(out=y if it < 2 else o, in0=q, scalar=1.5, in1=y, op0=ALU.add,
                                                   op1=ALU.mult))

            def normed(c, src, dst):
                dve.wait_ge(ssq_done, 2 * c + 2)
                rsqrt(rst[:, 2 * c:2 * c + 2], stat[:, 2 * c:2 * c + 2], D, 2)
                for t in range(NT):
                    dve.tensor_scalar(dst[:, t, :], src[:, t, :], rst[:, 2 * c + t:2 * c + t + 1], None, ALU.mult)\
                       .then_inc(xn_done, 1)

            def gained(c, b0):
                for t in range(NT):
                    for h in range(2):
                        n = 4 * c + 2 * t + h
                        dve.wait_ge(tr_done, n + 1)
                        gain = vec[:, GAIN(c) + 4 * h:GAIN(c) + 4 * h + 4].unsqueeze(2).broadcast_to([P, 4, P])
                        dve.tensor_tensor(hT[:, 4 * h:4 * h + 4, t * P:(t + 1) * P],
                                          bank[b0 + 2 * t + h].rearrange("p (k t) -> p k t", k=4), gain, ALU.mult)\
                           .then_inc(hT_done, 1)

            dve.memset(nt_[:, 32:33], 0.0).then_inc(exp_warm, 1)
            normed(0, x, xn)
            dve.wait_ge(vec_ps, 1)
            dve.tensor_copy(vec[:, :], bank[7][:, 0:NVEC]).then_inc(vec_sb, 1)
            dve.tensor_copy(peT[:, :], bank[7][:, 128:128 + CMP_L]).then_inc(vec_sb, 1)
            dve.wait_ge(vec_sb, 2)
            gained(0, 0)
            dve.wait_ge(in_bias, 16 * 16)
            dve.tensor_tensor(btab.rearrange("p h r c -> p (h r) c"), braw.rearrange("p h r c -> p (h r) c")[:, :, ::-1],
                              const("wmask").unsqueeze(1).broadcast_to([P, 48, GRID_W]), ALU.add).then_inc(bias_sb, 1)
            dve.wait_ge(bias_sb, 1)
            dve.memset(nt_[:, 35:36], 0.0).then_inc(free[5], 1)
            normed(1, mx, mx)

            with dve.Fori(0, PAIRS) as j:
                chain.enter(j, 2 + RS + 2 + 2)
                dve.wait_ge(zA_sb, j * 2 + 2)
                chain(dve.tensor_tensor(sqA, zA[:, :, 128:384], zA[:, :, 128:384], ALU.mult))
                chain(dve.tensor_reduce(ssA, sqA.rearrange("p t (h d) -> p (t h) d", d=HD), AX, ALU.add))
                rsqrt(rsA, ssA, HD, 8)
                for t in range(NT):
                    ins = dve.tensor_tensor(qkn[:, t, :].rearrange("p (h d) -> p h d", d=HD),
                                            zA[:, t, 128:384].rearrange("p (h d) -> p h d", d=HD),
                                            rsA[:, 4 * t:4 * t + 4].unsqueeze(2).broadcast_to([P, 4, HD]), ALU.mult)
                ins.then_inc(qknA, 1)
                dve.wait_ge(qkT_ps, j + 1)
                dve.tensor_scalar(qkT[:, 0, :], bank[2][:, 0:T], vec[:, QN:QN + 1], HD ** -0.5, ALU.mult, ALU.mult)\
                   .then_inc(qkT_sb, 1)
                dve.tensor_scalar(qkT[:, 1, :], bank[2][:, T:2 * T], vec[:, KN:KN + 1], None, ALU.mult)\
                   .then_inc(qkT_sb, 1)
                dve.wait_ge(poolY_ps, j + 1)
                dve.tensor_scalar(yT[:, bass.ds(j, 1), :].rearrange("p a t -> p (a t)"), bank[3][:, T:2 * T],
                                  vec[:, bass.ds(j + PSCALE, 1)], None, ALU.mult).then_inc(yA_pool, 1)
                for h in range(2):
                    dve.wait_ge(sA_ps, j * 2 + h + 1)
                    for t in range(NT):
                        bias = btab[:, bass.ds(j * 2 + h, 1), 2 - 2 * t:6 - 2 * t, :].rearrange("p a r c -> p (a r c)")
                        ins = dve.tensor_tensor(sA[:, h, t, :], bank[4 + h][:, t * T:(t + 1) * T], bias, ALU.add)
                    chain(ins)
                    dve.tensor_reduce(nmA[:, 2 * h:2 * h + 2], sA[:, h, :, :], AX, ALU.max, negate=True).then_inc(maxA, 1)
                for h in range(2):
                    dve.wait_ge(expA, j * 2 + h + 1)
                    chain(dve.reciprocal(rcA[:, 2 * h:2 * h + 2], sumA[:, 2 * h:2 * h + 2]))
                    for t in range(NT):
                        ins = dve.tensor_scalar(sA[:, h, t, :], sA[:, h, t, :], rcA[:, 2 * h + t:2 * h + t + 1], None,
                                                ALU.mult)
                    ins.then_inc(pA, 1)
                chain.leave(PAIRS)

            for n in range(2):
                for t in range(NT):
                    dve.wait_ge(out1_ps, 2 * n + t + 1)
                    dve.tensor_tensor(x[:, t, n * 512:(n + 1) * 512], x[:, t, n * 512:(n + 1) * 512],
                                      bank[2 * n + t], ALU.add).then_inc(x1_done, 1)
            gained(1, 4)
            normed(2, x, xn)
            gained(2, 0)

            dve.wait_ge(lg_ps, 1)
            dve.tensor_reduce(nmE, bank[4][:, 0:32].rearrange("p (t e) -> p t e", t=NT), AX, ALU.max, negate=True)\
               .then_inc(lg_max, 1)
            dve.memset(onesT, 1.0)
            dve.wait_ge(lg_exp, 1)
            chain(dve.reciprocal(smE, smE))
            dve.tensor_tensor(lgE, lgE, smE.unsqueeze(2).broadcast_to([P, NT, EXPERTS]), ALU.mult).then_inc(aff_sb, 1)
            dve.wait_ge(aff_ps, 1)
            chain(dve.tensor_copy(affT, bank[5][0:EXPERTS, 0:T]))
            for it in range(CAP // 8):
                chain(dve.max(m8, affT))
                chain(dve.match_replace(affT, m8, affT, -1.0))
            chain(dve.tensor_scalar(selT, affT, 0.0, None, ALU.is_lt))
            chain(dve.tensor_tensor_scan(cumT, onesT, selT, 0.0, ALU.mult, ALU.add))
            dve.tensor_tensor(cumT, cumT, selT, ALU.mult).then_inc(pos_sb, 1)
            dve.wait_ge(pos_ps, 1)
            chain(dve.tensor_copy(posT, bank[6][:, 0:32].rearrange("p (t e) -> p t e", t=NT)))
            for t in range(NT):
                pos = posT[:, t, :].unsqueeze(2).broadcast_to([P, EXPERTS, CAP])
                aff = lgE[:, t, :].unsqueeze(2).broadcast_to([P, EXPERTS, CAP])
                place = const("iota1").unsqueeze(1).broadcast_to([P, EXPERTS, CAP])
                chain(dve.tensor_tensor(selall[:, :, t, 0, :], pos, place, ALU.is_equal))
                dve.tensor_tensor(selall[:, :, t, 1, :], selall[:, :, t, 0, :], aff, ALU.mult).then_inc(sel_done, 1)

            gain = vec[:, GAIN(2):GAIN(2) + 8].unsqueeze(2).broadcast_to([P, KC, CAP])
            with dve.Fori(0, EXPERTS) as e:
                chain.enter(e, 1)
                dve.wait_ge(xe_ps, e + 1)
                dve.tensor_tensor(xeT, bank[3][:, 0:KC * CAP].rearrange("p (k s) -> p k s", k=KC), gain, ALU.mult)\
                   .then_inc(xe_sb, 1)
                dve.wait_ge(gate_th, e + 1)
                chain(dve.scalar_tensor_tensor(out=thE, in0=thE, scalar=1.0, in1=bank[0], op0=ALU.add, op1=ALU.mult))
                dve.wait_ge(up_ps, e + 1)
                dve.scalar_tensor_tensor(out=hE, in0=thE, scalar=0.5, in1=bank[1], op0=ALU.mult, op1=ALU.mult)\
                   .then_inc(h_sb, 1)
                dve.wait_ge(y_ps, e + 1)
                dve.tensor_copy(ysb[:, 512:1024], bank[5]).then_inc(y_sb, 1)
                for t in range(NT):
                    for h in range(2):
                        dve.wait_ge(sc_ps, e * 4 + 2 * t + h + 1)
                        dve.tensor_tensor(x[:, t, h * 512:(h + 1) * 512], x[:, t, h * 512:(h + 1) * 512],
                                          bank[(6, 4)[t] + h], ALU.add).then_inc(x_acc, 1)
                chain.leave(EXPERTS)

            normed(3, x, xn)
            gained(3, 4)
            dve.wait_ge(e_sq, 2)
            dve.wait_ge(in_rows, 16 * 3)
            rsqrt(rst[:, 12:14], stat[:, 12:14], D, 2)
            for t in range(NT):
                chain(dve.scalar_tensor_tensor(out=uP[:, t, :], in0=xn[:, t, :], scalar=rst[:, 12 + t:13 + t],
                                               in1=grows[:, 0, :], op0=ALU.mult, op1=ALU.mult))
                dve.wait_ge(g_th, 2 * t + 2)
                chain(dve.scalar_tensor_tensor(out=uP[:, t, :], in0=thP[:, t, :], scalar=1.0, in1=uP[:, t, :],
                                               op0=ALU.add, op1=ALU.mult))
                dve.scalar_tensor_tensor(out=x[:, t, :], in0=uP[:, t, :], scalar=0.5, in1=x[:, t, :],
                                         op0=ALU.mult, op1=ALU.add).then_inc(x3_done, 1)
            normed(4, x, xn)
            gained(4, 0)

            dve.memset(kvc[:, 4, :], 0.0)
            dve.memset(hidv, 0.0)
            dve.memset(zp[:, :, 0:3], 0.0)
            dve.memset(v1[:, :, 128:132], 1.0)
            chain(dve.memset(Pc, 0.0))
            dve.wait_ge(kvc_sb, 2)
            dve.tensor_copy(kvc[:, 4, 0:CMP_L], peT[:, :]).then_inc(kvc_sb, 1)
            dve.wait_ge(if_ps, 1)
            chain(dve.tensor_scalar(iR, bank[5][0:4, 0:T], ifb[0:4, 0:1], None, ALU.add))
            chain(dve.tensor_scalar(fR, bank[5][0:4, T:2 * T], ifb[0:4, 1:2], None, ALU.add))
            chain(dve.tensor_scalar(mnR, fR, 0.0, None, ALU.min))
            chain(dve.tensor_scalar(MR, fR, -1.0, None, ALU.mult))
            dve.tensor_tensor(abR, fR, MR, ALU.max).then_inc(ab_sb, 1)
            dve.wait_ge(ga_th, 1)
            for b in range(3):
                for q in range(2):
                    o = gball.rearrange("p (g b q i t) -> p g b q i t", g=4, b=3, q=2, i=2)[:, :, b, q, :, :]
                    for t in range(NT):
                        src = gth[:, t, :].rearrange("p (g i q b) -> p g i q b", g=4, i=2, q=2)[:, :, :, q, b]
                        ins = dve.tensor_scalar(o[:, :, :, t], src, 1.0, 0.5, ALU.add, ALU.mult)
            ins.then_inc(ga_sb, 1)
            dve.wait_ge(hid_ps, 1)
            for m in range(2):
                chain(dve.tensor_copy(hidb[:, m:m + 1], bank[m][:, 60:61]))
            for m in range(2):
                ins = dve.tensor_scalar(hpre[:, m, :], bank[m][:, 0:60], hidb[:, m:m + 1], None, ALU.add)
            ins.then_inc(hid_pre, 1)
            dve.wait_ge(hid_pre, 1)
            dve.wait_ge(hid_th, 1)
            chain(dve.scalar_tensor_tensor(out=hth, in0=hth, scalar=1.0, in1=hpre, op0=ALU.add, op1=ALU.mult))
            dve.tensor_scalar(hidk, hth[:, 0, :], 0.5, None, ALU.mult)
            dve.tensor_scalar(hidv[:, :, 0:N_CMP], hth[:, 1, :].rearrange("p (g n) -> p g n", g=4), 0.5, None, ALU.mult)\
               .then_inc(hid_sb, 1)
            dve.wait_ge(ab_ln, 1)
            chain(dve.tensor_tensor(mnR, mnR, lnR, ALU.subtract))
            chain(dve.tensor_scalar(MR, mnR, 0.0, 1.0, ALU.mult, ALU.add))
            chain(dve.tensor_tensor_scan(BR, MR, mnR, 0.0, ALU.mult, ALU.add))
            chain(dve.tensor_tensor(aR, iR, BR, ALU.subtract))
            chain(dve.tensor_tensor_scan(MR, aR, aR, 0.0, ALU.max, ALU.max))
            dve.tensor_tensor(mR, BR, MR, ALU.add).then_inc(em_in, 1)
            chain(dve.tensor_scalar(nMR, MR, -1.0, None, ALU.mult))
            dve.tensor_tensor(negMd.rearrange("p (h t) -> p h t", h=4), nMR.unsqueeze(1).broadcast_to([4, 4, T]),
                              const("eye4", 4).unsqueeze(2).broadcast_to([4, 4, T]), ALU.mult).then_inc(st_sb, 1)
            dve.wait_ge(kc_ps, 1)
            dve.tensor_copy(kcall.rearrange("p (g n) -> p g n", g=4)[:, :, 0:N_CMP],
                            bank[2][:, 0:60].rearrange("p (g n) -> p g n", g=4)).then_inc(kc_sb, 1)
            dve.memset(kcall.rearrange("p (g n) -> p g n", g=4)[:, :, N_CMP:16], 0.0)
            dve.tensor_copy(vcall, bank[3][:, 0:256]).then_inc(kc_sb, 1)
            dve.wait_ge(st_ps, 1)
            dve.tensor_copy(stall.rearrange("p (h n) -> p h n", h=4),
                            bank[7][:, 0:16].rearrange("p (n h) -> p h n", h=4)).then_inc(st_sb, 1)

            cadd = const("cmpadd").rearrange("p (t n) -> p t n", t=NT)[:, :, 0:N_CMP].unsqueeze(1)\
                .broadcast_to([P, 2, NT, N_CMP])
            cmul = const("cmpmul").rearrange("p (t n) -> p t n", t=NT)[:, :, 0:N_CMP].unsqueeze(1)\
                .broadcast_to([P, 2, NT, N_CMP])
            gv = gst.rearrange("p (b q i t) -> p b q i t", b=3, q=2, i=2)

            def head_max(n4, i):
                par = i % 2
                dve.wait_ge(ns_ps, n4 + i + 1)
                s = ps[:, 2 * par:2 * par + 2, 0:384].rearrange("p b (c k) -> p b c k", c=3)
                chain(dve.tensor_tensor(s[:, :, 0, :], s[:, :, 0, :], caus.unsqueeze(1).broadcast_to([P, 2, P]), ALU.add))
                chain(dve.tensor_tensor(s[:, :, 2, :], s[:, :, 2, :], caus.unsqueeze(1).broadcast_to([P, 2, P]), ALU.add))
                dve.tensor_reduce(nmN[:, par, :, 0], s[:, :, 0, :], AX, ALU.max, negate=True)
                dve.tensor_reduce(nmN[:, par, :, 1], ps[:, 2 * par:2 * par + 2, 128:384], AX, ALU.max, negate=True)\
                   .then_inc(ns_max, 1)

            def head_probs(n4, i):
                par, hp = i % 2, i // 2
                dve.wait_ge(ns_exp, n4 + i + 1)
                chain(dve.reciprocal(rcN[:, par, :, :], smN[:, par, :, :]))
                chain(dve.tensor_tensor(rcN[:, par, :, :], rcN[:, par, :, :], gv[:, 1:3, par, hp, :], ALU.mult))
                for b in range(2):
                    for t, c in ((0, slice(0, 128)), (1, slice(128, 384))):
                        ins = dve.tensor_scalar(Pn[:, par, b, c], Pn[:, par, b, c], rcN[:, par, b, t:t + 1], None, ALU.mult)
                ins.then_inc(np_sb, 1)

            with dve.Fori(0, GROUPS) as g:
                n4 = g * 4
                chain.enter(g, 7 + 1 + 2 + 4 + 4 + 4 * 2 + 4 * 2 + RS + 2)
                dve.wait_ge(staged, g * 7 + 7)
                dve.wait_ge(proj_sb, g * 7 + 1)
                for j in range(4):
                    for m in range(2):
                        w = cst[:, 5 * m + j:5 * m + j + 1]
                        if j == 0:
                            ins = dve.tensor_scalar(yc[:, m, :], zp[:, m, 0:T], w, cst[:, 5 * m + 4:5 * m + 5],
                                                    ALU.mult, ALU.add)
                        else:
                            ins = dve.scalar_tensor_tensor(out=yc[:, m, :], in0=zp[:, m, j:j + T], scalar=w,
                                                           in1=yc[:, m, :], op0=ALU.mult, op1=ALU.add)
                        if j < 3:
                            chain(ins)
                        elif m == 0:
                            chain(ins)
                        else:
                            ins.then_inc(c_conv, 1)
                dve.wait_ge(d_ps, g + 1)
                dve.tensor_tensor(tm[:, 0:T], bank[6][:, 0:T], causTz, ALU.add)
                dve.tensor_tensor(tm[:, T:384], bank[6][:, P:T], causT, ALU.add).then_inc(d_in, 1)
                dve.wait_ge(c_th, g + 1)
                dve.scalar_tensor_tensor(out=yc, in0=thc, scalar=1.0, in1=yc, op0=ALU.add, op1=ALU.mult).then_inc(c_qk, 1)
                dve.wait_ge(xs_ps, g + 1)
                dve.tensor_reduce(nmM, bank[7].rearrange("p (t k) -> p t k", t=NT), AX, ALU.max, negate=True)\
                   .then_inc(xs_max, 1)
                dve.wait_ge(d_exp, g + 1)
                dve.wait_ge(st_mm, g + 1)
                dve.scalar_tensor_tensor(out=Wm, in0=bank[5][:, 0:384], scalar=0.25 * ML_DH ** -0.5, in1=tm,
                                         op0=ALU.mult, op1=ALU.mult).then_inc(w_sb, 1)
                dve.wait_ge(xs_exp, g + 1)
                chain(dve.reciprocal(rcM, smM))
                for t in range(NT):
                    ins = dve.tensor_scalar(Pm[:, t, :], Pm[:, t, :], rcM[:, t:t + 1], None, ALU.mult)
                ins.then_inc(xp_sb, 1)
                dve.wait_ge(cs_ps, g + 1)
                for par in range(2):
                    ins = dve.tensor_tensor(
                        sc[:, 4 * par:4 * par + 4, 0:N_CMP].rearrange("p (i t) n -> p i t n", i=2),
                        bank[6 + par][:, 0:64].rearrange("p (i t n) -> p i t n", i=2, t=NT)[:, :, :, 0:N_CMP], cadd, ALU.add)
                chain(ins)
                chain(dve.tensor_reduce(nmC, sc[:, :, 0:N_CMP], AX, ALU.max, negate=True))
                dve.tensor_tensor(sc[:, :, 0:N_CMP], sc[:, :, 0:N_CMP], nmC.unsqueeze(2).broadcast_to([P, 8, N_CMP]),
                                  ALU.add).then_inc(cs_in, 1)
                dve.wait_ge(n_ps, g + 1)
                num = bank[5][:, 0:264].rearrange("p (t e) -> p t e", t=NT)
                chain(dve.tensor_copy(dn, num[:, :, 128]))
                chain(dve.scalar_tensor_tensor(out=ab, in0=dn, scalar=-1.0, in1=dn, op0=ALU.mult, op1=ALU.max))
                chain(dve.tensor_tensor(ab, ab, lst[:, 2:4], ALU.max))
                chain(dve.reciprocal(rd, ab))
                for t in range(NT):
                    ins = dve.tensor_scalar(hh[:, t, :], num[:, t, 0:128], rd[:, t:t + 1], None, ALU.mult)
                ins.then_inc(h_div, 1)
                head_max(n4, 0)
                dve.wait_ge(cs_exp, g + 1)
                chain(dve.tensor_reduce(smC, sc[:, :, 0:N_CMP], AX, ALU.add))
                chain(dve.reciprocal(rcC, smC))
                chain(dve.tensor_tensor(rcC, rcC, gst[:, 0:8], ALU.mult))
                chain(dve.tensor_tensor(sc[:, :, 0:N_CMP], sc[:, :, 0:N_CMP],
                                        rcC.unsqueeze(2).broadcast_to([P, 8, N_CMP]), ALU.mult))
                pcv = Pc.rearrange("p t (i q) n -> p q i t n", q=2)
                for par in range(2):
                    ins = dve.tensor_tensor(pcv[:, par, :, :, 0:N_CMP],
                                            sc[:, 4 * par:4 * par + 4, 0:N_CMP].rearrange("p (i t) n -> p i t n", i=2),
                                            cmul, ALU.mult)
                ins.then_inc(cp_sb, 1)
                head_max(n4, 1)
                head_probs(n4, 0)
                dve.wait_ge(h_sq, g + 1)
                rsqrt(rd, ssM, ML_DH, 2)
                for t in range(NT):
                    ins = dve.scalar_tensor_tensor(out=y1[:, t, :], in0=hh[:, t, :], scalar=rd[:, t:t + 1], in1=hgg,
                                                   op0=ALU.mult, op1=ALU.mult)
                    chain(ins)
                dve.scalar_tensor_tensor(out=y1, in0=so, scalar=1.0, in1=y1, op0=ALU.add, op1=ALU.mult).then_inc(ym_sb, 1)
                head_max(n4, 2)
                head_probs(n4, 1)
                head_max(n4, 3)
                head_probs(n4, 2)
                head_probs(n4, 3)
                chain.leave(GROUPS)

            dve.wait_ge(ynsa_done, 8)
            dve.wait_ge(yml_done, 4)
            dve.memset(nt_[:, 34:35], 0.0).then_inc(mg_free, 2)
            with dve.Fori(0, 4) as i:
                chain.enter(i, 6)
                for u in range(2):
                    m = i * 2 + u
                    dve.wait_ge(mg_th, m + 1)
                    dve.wait_ge(mp_ps, m + 1)
                    chain(dve.scalar_tensor_tensor(out=yG[:, u, 0:512], in0=thG[:, u, 0:512], scalar=1.0,
                                                   in1=bank[4 * u + 2], op0=ALU.add, op1=ALU.mult))
                    chain(dve.scalar_tensor_tensor(out=yG[:, u, 512:768], in0=thG[:, u, 512:768], scalar=1.0,
                                                   in1=bank[4 * u + 3][:, 0:T], op0=ALU.add, op1=ALU.mult))
                    chain(dve.tensor_tensor(yG[:, u, 0:T], yG[:, u, 0:T], yG[:, u, T:512], ALU.add))
                    dve.tensor_tensor(yT2[:, bass.ds(m, 1), :].rearrange("p a t -> p (a t)"), yG[:, u, 0:T],
                                      yG[:, u, 512:768], ALU.add).then_inc(mg_free, 1)
                chain.leave(4)

            def post(base):
                dve.wait_ge(y_sq, 2 * base + 2)
                c = 14 - 2 * base
                rsqrt(rst[:, c:c + 2], stat[:, c:c + 2], D, 2)
                for t in range(NT):
                    chain(dve.scalar_tensor_tensor(out=ysF[:, t, :], in0=ysF[:, t, :], scalar=rst[:, c + t:c + t + 1],
                                                   in1=grows[:, 1 + base, :], op0=ALU.mult, op1=ALU.mult))
                    dve.tensor_tensor(x[:, t, :], x[:, t, :], ysF[:, t, :], ALU.add).then_inc(x4_done, 1)

            post(0)
            normed(5, x, xn)
            gained(5, 4)

            def ff(s, par):
                for f in range(2):
                    b = bank[4 + 2 * par + f]
                    dve.wait_ge(ff_th, s * 2 + f + 1)
                    chain(dve.scalar_tensor_tensor(out=vF[:, par, f, :], in0=thF[:, par, f, :], scalar=1.0,
                                                   in1=b[:, 0:T], op0=ALU.add, op1=ALU.mult))
                    dve.scalar_tensor_tensor(out=hF[:, par, f, :], in0=vF[:, par, f, :], scalar=0.5, in1=b[:, T:2 * T],
                                             op0=ALU.mult, op1=ALU.mult).then_inc(ff_h, 1)

            ff(0, 0)
            ff(1, 1)
            with dve.Fori(0, 4) as i:
                chain.enter(i, 4)
                ff(i * 2 + 2, 0)
                ff(i * 2 + 3, 1)
                chain.leave(4)
            ff(10, 0)
            post(1)


_NAMES = ["x", "p", "norm_mix", "w_in", "w_pool", "pool_scale", "q_norm", "k_norm", "rpb", "w_out", "norm_ffn",
          "w_router", "w_gate", "w_up", "w_down", "norm_ple", "w_ple_gate", "w_ple_proj", "norm_ple_post", "mem_2",
          "g_pre_mix_2", "w_in_2", "cmp_pe_k_2", "cmp_w1_k_2", "cmp_w2_k_2", "cmp_pe_v_2", "cmp_w1_v_2",
          "cmp_w2_v_2", "ml_conv_w_2", "ml_conv_b_2", "ml_gate_b_2", "ml_head_g_2", "g_mem_2", "w_mem_kv_2",
          "w_proj_nsa_2", "w_proj_ml_2", "w_proj_mem_2", "w_out_2", "g_post_mix_2", "g_pre_ffn_2", "w_ffn_in_2",
          "w_ffn_down_2", "g_post_ffn_2"]


def laid_out(name, value):
    value = np.asarray(value)
    return np.ascontiguousarray(value[..., ::-1] if name == "rpb" else value)


def kernel(**inputs):
    import concourse.bacc as _bacc
    from concourse.bass_utils import run_bass_kernel_spmd as _run

    nc = _bacc.Bacc("TRN2", target_bir_lowering=False, num_devices=1)
    arrays, aps = {}, {}
    masks, pool = constants()
    for name, value in [(n, laid_out(n, inputs[n])) for n in _NAMES] + [("consts", masks), ("pool", pool)]:
        arrays[f"in_{name}"] = value
        aps[name] = nc.dram_tensor(f"in_{name}", value.shape, mybir.dt.from_np(value.dtype), kind="ExternalInput").ap()
    out = nc.dram_tensor("out_0", (1, T, D), F32, kind="ExternalOutput").ap()
    two_blocks(nc, aps, out)
    r = _run(nc, [arrays], core_ids=[0])
    return r.results[0]["out_0"]
```

```python
from contextlib import ExitStack

import numpy as np
import concourse.bass as bass
from concourse import mybir

F32 = mybir.dt.float32
I32 = mybir.dt.int32
ALU = mybir.AluOpType
ACT = mybir.ActivationFunctionType
AX = mybir.AxisListType.X

P = 128
T = 256
NT = T // P
D = 1024
KC = D // P
EPS = 1e-6
NEG = -1e30
SLOTS = 6
SLOT = 4096
RSQRT_SEED = float(0x5F3759DF)

PAIRS = 4
HD = 64
GRID_W, WIN_COLS, RPB_R, RPB_C = 64, 16, 15, 31
POOL_WINDOWS = (2, 4, 8, 16)
EXPERTS, CAP, DE = 16, 32, 2048
PARTS = (1, 5, 5, 5)
PLE = 256

GROUPS = 4
N_CMP, CMP_L, CMP_STRIDE = 15, 32, 16
ML_DH = 128
D_FF = 2816
FF_STEPS = D_FF // 256

Q0 = 0
KV0 = 1024
GATE0 = KV0 + 6 * 256
ML0 = GATE0 + 48
IF0 = ML0 + 3 * 512
O0 = IF0 + 8
MEMQ0 = O0 + 512
MERGE0 = MEMQ0 + 512

GAIN = lambda c: 8 * c
PSCALE = 48
CONV = 52
QN, KN = 92, 93
NVEC = 94
NSMALL = KC * (EXPERTS + 56) + 2 * HD

CONSTS = [("ident", 128), ("caus", 128), ("causT", 128), ("causTz", 256), ("wmask", 64), ("cmpadd", 32),
          ("cmpmul", 32), ("iota1", 32), ("ones", 128), ("eye4", 4)]
COFF = {}
_n = 0
for _name, _w in CONSTS:
    COFF[_name] = _n
    _n += _w
NCONST = _n


def constants():
    c = np.zeros((P, NCONST), np.float32)

    def put(name, a):
        a = np.asarray(a, np.float32)
        c[:a.shape[0], COFF[name]:COFF[name] + a.shape[1]] = a

    i = np.arange(P)
    put("ident", np.eye(P))
    put("caus", np.where(i[None, :] <= i[:, None], 0.0, NEG))
    put("causT", np.where(i[:, None] <= i[None, :], 0.0, NEG))
    put("causTz", np.concatenate([np.where(i[:, None] <= i[None, :], 0.0, NEG), np.zeros((P, P))], 1))
    col = i % GRID_W
    start = np.clip(col - WIN_COLS // 2, 0, GRID_W - WIN_COLS)
    kc = np.arange(GRID_W)
    put("wmask", np.where((kc[None] >= start[:, None]) & (kc[None] < start[:, None] + WIN_COLS), 0.0, NEG))
    t = np.arange(NT)[None, :, None] * P + i[:, None, None]
    n = np.arange(16)[None, None, :]
    seen = n * CMP_STRIDE + CMP_L - 1 <= t
    put("cmpadd", np.where(seen, 0.0, NEG).reshape(P, 32))
    put("cmpmul", np.where(seen, 1.0, 0.0).reshape(P, 32))
    put("iota1", np.tile(np.arange(1, CAP + 1), (P, 1)))
    put("ones", np.ones((P, P)))
    put("eye4", np.eye(4))
    pool = np.zeros((len(POOL_WINDOWS), T, T), np.float32)
    for g, w in enumerate(POOL_WINDOWS):
        for s in range(T):
            lo = min(max(s - w // 2, 0), T - 1)
            hi = min(max(s + (w - w // 2) - 1, 0), T - 1)
            pool[g, lo:hi + 1, s] += 1.0 / (hi - lo + 1)
            pool[g, s, s] -= 1.0
    return c, np.ascontiguousarray(pool.reshape(4, NT, P, T).transpose(2, 1, 0, 3).reshape(P, NT * 4 * T))


FIRST_SLOTS = [0, 1, 2, 3, 4, 5, 6, 7, 0, 1, 2, 3]


def around(rot):
    return [(n + rot) % SLOTS for n in range(12)]


class Chain:

    def __init__(self, eng, sem):
        self.eng, self.sem, self.base, self.n = eng, sem, 0, 0

    def __call__(self, ins):
        ins.then_inc(self.sem, 1)
        self.n += 1
        self.eng.wait_ge(self.sem, self.base + self.n)

    def enter(self, i, per):
        self.before, self.per = self.n, per
        self.base, self.n = i * per + self.before, 0

    def leave(self, times):
        assert self.n == self.per, (self.n, self.per)
        self.base, self.n = 0, self.before + times * self.per


class Ring:

    def __init__(self, eng, full, free):
        self.eng, self.full, self.free = eng, full, free
        self.rounds, self.incs = [0] * len(full), [0] * len(full)

    def load(self, slot, *copies):
        r = self.rounds[slot]
        if not (isinstance(r, int) and r == 0):
            self.eng.wait_ge(self.free[slot], r)
            if not isinstance(r, int):
                self.eng.nop(nofuse=True)
        for dst, src in copies:
            self.eng.dma_start(dst, src).then_inc(self.full[slot], 16)
        self.count(slot, len(copies))

    def count(self, slot, copies):
        self.rounds[slot] = self.rounds[slot] + 1
        self.incs[slot] = self.incs[slot] + 16 * copies

    def arrived(self, slot, copies):
        self.count(slot, copies)
        self.eng.wait_ge(self.full[slot], self.incs[slot])

    def enter(self, i, per):
        self.before, self.per = (list(self.rounds), list(self.incs)), per
        for s, (loads, copies) in per.items():
            self.rounds[s] = i * loads + self.rounds[s]
            self.incs[s] = i * (16 * copies) + self.incs[s]

    def leave(self, times):
        self.rounds, self.incs = list(self.before[0]), list(self.before[1])
        for s, (loads, copies) in self.per.items():
            self.rounds[s] += times * loads
            self.incs[s] += 16 * times * copies


def two_blocks(nc, a, out):
    ctx = ExitStack()
    with ctx:
        def sb(name, n, parts=P):
            return ctx.enter_context(nc.sbuf_tensor(name, [parts, n], F32))

        def sem(name):
            return ctx.enter_context(nc.semaphore(name))

        ring = sb("ring", SLOTS * SLOT)
        slot = [ring[:, s * SLOT:(s + 1) * SLOT] for s in range(SLOTS)]
        strip = [s.rearrange("p (k n) -> p k n", k=KC) for s in slot]
        x = sb("x", NT * D)[:, :].rearrange("p (t d) -> p t d", t=NT)
        xn = sb("xn", NT * D)[:, :].rearrange("p (t d) -> p t d", t=NT)
        turned_ = sb("turned", 2 * KC * T)
        hT = turned_[:, 0:KC * T].rearrange("p (k t) -> p k t", k=KC)
        yT = turned_[:, KC * T:].rearrange("p (k t) -> p k t", k=KC)
        later = sb("later", SLOT)
        yml = later[:, 0:1024].rearrange("p (k t) -> p k t", k=4)
        ymem = later[:, 1024:2048].rearrange("p (k t) -> p k t", k=4)
        kTm = later[:, 2048:3072]
        vm = later[:, 3072:4096].rearrange("p (t n) -> p t n", t=NT)
        slot += [later[:, :], turned_[:, :]]
        grows = sb("grows", 3 * D)[:, :].rearrange("p (c d) -> p c d", c=3)
        hgrow = sb("hgrow", 512)
        consts = sb("consts", NCONST)
        vecs = sb("vecs", NVEC + CMP_L + 2)
        vec = vecs[:, 0:NVEC]
        peT = vecs[:, NVEC:NVEC + CMP_L]
        ifb = vecs[:, NVEC + CMP_L:NVEC + CMP_L + 2]
        small = sb("small", NSMALL)
        wr = small[:, 0:128].rearrange("p (k e) -> p k e", k=KC)
        wsm = small[:, 128:576].rearrange("p (k e) -> p k e", k=KC)
        w2 = small[:, 576:704]
        wp = sb("wp", P)
        stat = sb("stat", 16)
        rst = sb("rst", 16)
        nt_ = sb("nt_", 40)
        scr = sb("scr", 10420)

        class Area:

            def __init__(self, at=0):
                self.at = at

            def __call__(self, n, pat=None, parts=P, **kw):
                v = scr[0:parts, self.at:self.at + n]
                self.at += n
                assert self.at <= 10420, self.at
                return v.rearrange(pat, **kw) if pat else v

        def const(name, parts=P):
            w = dict(CONSTS)[name]
            return consts[0:parts, COFF[name]:COFF[name] + w]

        ident, caus, causT, causTz = const("ident"), const("caus"), const("causT"), const("causTz")

        ps = ctx.enter_context(nc.psum_tensor("ps", [P, 8, 512], F32))
        bank = [ps[:, b, :] for b in range(8)]

        A = Area()
        poolm = A(NT * 4 * T, "p (t g s) -> p t g s", t=NT, g=4)
        mx = A(NT * D, "p (t d) -> p t d", t=NT)
        zA = A(NT * 512, "p (t n) -> p t n", t=NT)
        sqA = A(NT * T, "p (t n) -> p t n", t=NT)
        qkn = A(NT * T, "p (t n) -> p t n", t=NT)
        qkT = A(2 * T, "p (m t) -> p m t", m=2)
        sA = A(2 * NT * T, "p (a t k) -> p a t k", a=2, t=NT)
        PTA = A(2 * NT * T, "p (a k q) -> p a k q", a=2, k=NT)
        dT = A(T)
        junk = A(D)
        ssA, rsA, nmA, sumA, rcA = A(8), A(8), A(4), A(4), A(4)
        braw = slot[5][:, 0:6 * 8 * GRID_W].rearrange("p (r h c) -> p h r c", h=8, r=6)
        btab = grows.rearrange("p c d -> p (c d)").rearrange("p (h r c) -> p h r c", h=8, r=6)

        B = Area(at=NT * 4 * T + NT * D)
        lgE = B(32, "p (t e) -> p t e", t=NT)
        nmE, smE = B(2), B(2)
        affT, selT, cumT, onesT = (B(T, parts=EXPERTS) for _ in range(4))
        m8 = B(8, parts=EXPERTS)
        posT = B(32, "p (t e) -> p t e", t=NT)
        selall = B(EXPERTS * 128, "p (e t w s) -> p e t w s", e=EXPERTS, t=NT, w=2)
        selflat = scr[:, B.at - EXPERTS * 128:B.at]
        gT = B(T)
        ysb = B(D)
        pin = B(NT * PLE, "p (t n) -> p t n", t=NT)
        pT = B(2 * T, "p (k t) -> p k t", k=2)
        B = Area()
        sele = B(128, "p (t w s) -> p t w s", t=NT, w=2)
        sele_flat = scr[:, 0:128]
        xeT = B(KC * CAP, "p (k s) -> p k s", k=KC)
        thE = B(512)
        hE = B(512)
        hTe = B(512, "p (c n) -> p c n", c=4)
        assert B.at <= NT * 4 * T

        uP = mx
        C = Area(at=NT * 4 * T + NT * D)
        thP = C(NT * D, "p (t d) -> p t d", t=NT)

        E = Area()
        gball = E(96)
        stall = E(16)
        kcall = E(4 * 16)
        vcall = E(4 * HD)
        negMd = E(4 * T, parts=4)
        gst, lst, cst, kcg, vcg = E(24), E(4), E(10), E(16), E(HD)
        vmg = E(NT * P, "p (t d) -> p t d", t=NT)
        hgg = E(P)
        zp = E(2 * 259, "p (m t) -> p m t", m=2)
        v1 = E(NT * 132, "p (t e) -> p t e", t=NT)
        Pc = E(NT * 4 * 32, "p (t i n) -> p t i n", t=NT, i=4)
        loop_at = E.at
        qs = E(2 * T, "p (m t) -> p m t", m=2)
        kxy = E(2 * T, "p (m t) -> p m t", m=2)
        vsb = E(NT * P, "p (t d) -> p t d", t=NT)
        yc = E(2 * T, "p (m t) -> p m t", m=2)
        thc = E(2 * T, "p (m t) -> p m t", m=2)
        so = E(NT * P, "p (t d) -> p t d", t=NT)
        tm = E(384)
        Wm = E(384)
        hh = E(NT * P, "p (t d) -> p t d", t=NT)
        y1 = E(NT * P, "p (t d) -> p t d", t=NT)
        qm = E(T)
        Pm = E(NT * T, "p (t k) -> p t k", t=NT)
        PTm = E(NT * T, "p (k q) -> p k q", k=NT)
        sc = E(8 * 16, "p (j n) -> p j n", j=8)
        PTc = E(T)
        Pn = xn.rearrange("p t d -> p (t d)")[:, 0:1536].rearrange("p (a b n) -> p a b n", a=2, b=2)
        PTn = E(2 * 384, "p (b n) -> p b n", b=2)
        nmC, smC, rcC = E(8), E(8), E(8)
        nmN, smN, rcN = (E(8, "p (a b t) -> p a b t", a=2, b=2) for _ in range(3))
        nmM, smM, rcM, dn, ab, rd, ssM = (E(2) for _ in range(7))
        E2 = Area(at=loop_at)
        kvc = E2(5 * T, "p (g t) -> p g t", g=5)
        hidb = E2(2)
        hpre = E2(2 * 60, "p (m n) -> p m n", m=2)
        hth = E2(2 * 60, "p (m n) -> p m n", m=2)
        hidk = E2(60)
        hidv = E2(4 * 32, "p (g n) -> p g n", g=4)
        gth = E2(NT * 48, "p (t n) -> p t n", t=NT)
        ifT = E2(NT * 8, "p (t n) -> p t n", t=NT)
        iR, fR, mnR, abR, lnR, BR, aR, MR, mR, emR, nMR = (E2(T, parts=4) for _ in range(11))
        G = Area(at=0)
        thG = G(2 * 768, "p (u n) -> p u n", u=2)
        yG = G(2 * 768, "p (u n) -> p u n", u=2)
        yT2 = xn.rearrange("p t d -> p (t d)").rearrange("p (k t) -> p k t", k=KC)
        thF = G(4 * T, "p (u f t) -> p u f t", u=2, f=2)
        vF = G(4 * T, "p (u f t) -> p u f t", u=2, f=2)
        hF = G(4 * T, "p (u f t) -> p u f t", u=2, f=2)
        ysF = G(NT * D, "p (t d) -> p t d", t=NT)
        xF = Area(at=0)(NT * D, "p (t d) -> p t d", t=NT)

        full = [sem(f"slot{s}_full") for s in range(SLOTS + 2)]
        free = [sem(f"slot{s}_free") for s in range(SLOTS)]
        in_x1 = sem("in_x1")
        in_x, in_consts, in_pool, in_bias, in_mem, in_p, in_wp = (
            sem(n) for n in ("in_x", "in_consts", "in_pool", "in_bias", "in_mem",
                             "in_p", "in_wp"))
        out_done = sem("out_done")
        dve_chain, act_chain, pool_chain = sem("dve_chain"), sem("act_chain"), sem("pool_chain")
        exp_warm = sem("exp_warm")
        bias_sb, in_rows = sem("bias_sb"), sem("in_rows")
        ssq_done, xn_done, tr_done, hT_done = sem("ssq_done"), sem("xn_done"), sem("tr_done"), sem("hT_done")
        zA_ps, zA_sb, qknA, qkT_ps, qkT_sb, poolA_ps, dT_sb, poolY_ps, yA_pool = (
            sem(n) for n in ("zA_ps", "zA_sb", "qknA", "qkT_ps", "qkT_sb", "poolA_ps", "dT_sb", "poolY_ps", "yA_pool"))
        sA_ps, maxA, expA, pA, ptA_ps, ptA_sb, oA_ps, yA_attn, wp_used = (
            sem(n) for n in ("sA_ps", "maxA", "expA", "pA", "ptA_ps", "ptA_sb", "oA_ps", "yA_attn", "wp_used"))
        vA_sb = sem("vA_sb")
        out1_ps, x1_done, mkv_ps, mkv_sb = sem("out1_ps"), sem("x1_done"), sem("mkv_ps"), sem("mkv_sb")
        lg_ps, lg_max, lg_exp, aff_sb, aff_ps, pos_sb, pos_ps, sel_done = (
            sem(n) for n in ("lg_ps", "lg_max", "lg_exp", "aff_sb", "aff_ps", "pos_sb", "pos_ps", "sel_done"))
        sele_sb, xe_ps, xe_sb, gt_ps, gt_sb, gate_ps, up_ps, gate_th, h_sb, ht_ps, ht_sb, y_ps, y_sb, sc_ps, x_acc = (
            sem(n) for n in ("sele_sb", "xe_ps", "xe_sb", "gt_ps", "gt_sb", "gate_ps", "up_ps", "gate_th", "h_sb",
                             "ht_ps", "ht_sb", "y_ps", "y_sb", "sc_ps", "x_acc"))
        pT_ps, pT_sb, g_ps, g_th, e_ps, e_sb, e_sq, x3_done = (
            sem(n) for n in ("pT_ps", "pT_sb", "g_ps", "g_th", "e_ps", "e_sb", "e_sq", "x3_done"))
        ga_ps, if_ps, ga_th, ga_sb, ab_sb, ab_exp, ab_ln, em_in, em_sb, st_sb, st_ps = (
            sem(n) for n in ("ga_ps", "if_ps", "ga_th", "ga_sb", "ab_sb", "ab_exp", "ab_ln", "em_in", "em_sb",
                             "st_sb", "st_ps"))
        kvc_ps, kvc_sb, hid_ps, hid_pre, hid_th, hid_sb, kc_ps, kc_sb = (
            sem(n) for n in ("kvc_ps", "kvc_sb", "hid_ps", "hid_pre", "hid_th", "hid_sb", "kc_ps", "kc_sb"))
        staged, proj_ps, proj_sb, c_conv, c_th, c_qk, d_ps, d_in, d_exp, w_sb, n_ps, h_div, h_sq, ym_sb, ym_ps = (
            sem(n) for n in ("staged", "proj_ps", "proj_sb", "c_conv", "c_th", "c_qk", "d_ps", "d_in", "d_exp",
                             "w_sb", "n_ps", "h_div", "h_sq", "ym_sb", "ym_ps"))
        xs_ps, xs_max, xs_exp, xp_sb, xt_ps, xt_sb, xo_ps, ymem_done, yml_done, ynsa_done = (
            sem(n) for n in ("xs_ps", "xs_max", "xs_exp", "xp_sb", "xt_ps", "xt_sb", "xo_ps", "ymem_done",
                             "yml_done", "ynsa_done"))
        kx_swap = sem("kx_swap")
        cs_ps, cs_in, cs_exp, cp_sb, ct_ps, ct_sb, ns_ps, ns_max, ns_exp, np_sb, nt_ps, nt_sb, no_ps = (
            sem(n) for n in ("cs_ps", "cs_in", "cs_exp", "cp_sb", "ct_ps", "ct_sb", "ns_ps", "ns_max", "ns_exp",
                             "np_sb", "nt_ps", "nt_sb", "no_ps"))
        mg_ps, mp_ps, mg_th, mg_free, out2_ps, y_evac, y_sq, x4_done = (
            sem(n) for n in ("mg_ps", "mp_ps", "mg_th", "mg_free", "out2_ps", "y_evac", "y_sq", "x4_done"))
        ff_ps, ff_th, ff_h, ffo_ps = sem("ff_ps"), sem("ff_th"), sem("ff_h"), sem("ffo_ps")

        TURNS = {0: 0, 2: 1, 1: 2, 3: 3, 4: 4, 5: 5}
        block = ctx.enter_context(nc.Block())

        def chunks(w):
            return w.rearrange("(k p) n -> p k n", p=P)

        @block.sync
        def _(sp):
            r = Ring(sp, full, free)
            w_in1, w_in2 = a["w_in"][0], a["w_in_2"][0]

            def pair_strip(j, s):
                src = w_in1.rearrange("(k p) (m n) -> p k m n", p=P, m=4)
                dst = strip[s].rearrange("p k (m n) -> p k m n", m=4)
                return [(dst[:, :, m, :], src[:, :, m, bass.ds(j * 128, 128)]) for m in range(4)]

            def halves(s, w, c0):
                src = chunks(w)
                return [(strip[s][:, h:h + 4, :], src[:, h:h + 4, c0:c0 + 512]) for h in (0, 4)]

            for t in range(NT):
                sp.dma_start(x[:, t, :], a["x"][0][t * P:(t + 1) * P, :]).then_inc((in_x, in_x1)[t], 16)
            for j in range(PAIRS):
                r.load(j, *pair_strip(j, j))
            r.load(4, *halves(4, a["w_out"][0], 0))
            r.count(5, 0)
            r.load(5, *halves(5, a["w_out"][0], 512))

            wide = [s.rearrange("p (k n) -> p k n", k=2) for s in slot]
            tall = [s.rearrange("p (k n) -> p k n", k=4) for s in slot]
            gate = a["w_gate"][0].rearrange("e k f -> (e k) f")
            up = a["w_up"][0].rearrange("e k f -> (e k) f")
            down = a["w_down"][0].rearrange("e k f -> (e k) f")

            def expert(e, slots):
                for n in range(8):
                    w, i, s = (gate, up)[n // 4], n % 4, slots[n]
                    if s == 7:
                        sp.wait_ge(lg_ps, 1)
                    src = w[bass.ds(e * D + i * 256, 256), :].rearrange("(k p) f -> p k f", p=P)
                    r.load(s, (wide[s], src))
                for n in range(8, 12):
                    i, s = n - 8, slots[n]
                    src = down[bass.ds(e * DE + i * 512, 512), :].rearrange("(k p) f -> p k f", p=P)
                    r.load(s, (tall[s], src))

            def experts(part, rot):
                with sp.Fori(0, PARTS[part]) as i:
                    r.enter(i, {s: (2, 2) for s in range(SLOTS)})
                    expert(i + sum(PARTS[:part]), around(rot))
                    r.leave(PARTS[part])

            expert(0, FIRST_SLOTS)
            experts(1, 4)
            r.load(4, (slot[4][:, 0:2 * D].rearrange("p (k n) -> p k n", k=2), chunks(a["w_ple_proj"][0])))
            r.load(5, *halves(5, a["w_mem_kv_2"][0], 0))
            experts(2, 0)
            r.load(0, *halves(0, a["w_mem_kv_2"][0], 512))
            experts(3, 3)

            r.load(3, *halves(3, a["w_ple_gate"][0], 0))
            r.load(4, *halves(4, a["w_ple_gate"][0], 512))
            r.load(5, *halves(5, w_in2, KV0))
            r.load(2, *[(slot[2][h * HD:h * HD + HD, :].rearrange("p (l h) -> p l h", l=CMP_L),
                         a[n][0].rearrange("l d h -> d l h")) for h, n in enumerate(("cmp_w1_k_2", "cmp_w1_v_2"))])
            w2c = chunks(w_in2)
            kv = w_in2[:, KV0:KV0 + 1536].rearrange("(k p) (s n) -> p k s n", p=P, s=6)
            ml = w_in2[:, ML0:ML0 + 1536].rearrange("(k p) (s n) -> p k s n", p=P, s=3)
            kvd = strip[5][:, :, 256:512].rearrange("p k (s n) -> p k s n", s=4)
            mld = strip[0][:, :, 0:384].rearrange("p k (s n) -> p k s n", s=3)
            with sp.Fori(0, GROUPS) as g:
                r.enter(g, {0: (1, 4), 1: (1, 1), 5: (1, 5)})
                r.load(0, *[(mld[:, :, s, :], ml[:, :, s, bass.ds(g * 128, 128)]) for s in range(3)],
                       (strip[0][:, :, 384:512], w2c[:, :, bass.ds(g * 128 + O0, 128)]))
                r.load(5, (strip[5][:, :, 0:256], w2c[:, :, bass.ds(g * 256, 256)]),
                       *[(kvd[:, :, n, :], kv[:, :, s, bass.ds(g * HD, HD)]) for n, s in enumerate((2, 4, 3, 5))])
                r.load(1, (slot[1][:, 0:D].rearrange("p (k n) -> p k n", k=KC),
                           w2c[:, :, bass.ds(g * 128 + MEMQ0, 128)]))
                r.leave(GROUPS)
            gm = w_in2[:, MERGE0:MERGE0 + 3 * D].rearrange("(k p) (b n) -> p k b n", p=P, b=3)
            pn, pl, pe_ = (chunks(a[n][0]) for n in ("w_proj_nsa_2", "w_proj_ml_2", "w_proj_mem_2"))
            with sp.Fori(0, 4) as i:
                r.enter(i, {s: (1, 3) for s in (2, 3, 4, 5)})
                for u in range(2):
                    c = bass.ds(i * 256 + u * 128, 128)
                    gd = slot[2 + 2 * u][:, 0:3072].rearrange("p (k b n) -> p k b n", k=KC, b=3)
                    pd = slot[3 + 2 * u][:, 0:2048].rearrange("p (k n) -> p k n", k=16)
                    r.load(2 + 2 * u, *[(gd[:, :, b, :], gm[:, :, b, c]) for b in range(3)])
                    r.load(3 + 2 * u, (pd[:, 0:8, :], pn[:, :, c]), (pd[:, 8:12, :], pl[:, :, c]),
                           (pd[:, 12:16, :], pe_[:, :, c]))
                r.leave(4)
            r.load(0, *halves(0, a["w_out_2"][0], 0))
            r.load(1, *halves(1, a["w_out_2"][0], 512))
            gu = a["w_ffn_in_2"][0].rearrange("(k p) (m n) -> p k m n", p=P, m=2)
            dn_ = a["w_ffn_down_2"][0]

            def ff(s, par):
                A_ = strip[2 + 2 * par].rearrange("p k (m n) -> p k m n", m=2)
                B_ = slot[3 + 2 * par][:, 0:2 * D].rearrange("p (k n) -> p k n", k=2)
                r.load(2 + 2 * par, *[(A_[:, :, m, :], gu[:, :, m, bass.ds(s * 256, 256)]) for m in range(2)])
                r.load(3 + 2 * par, (B_, chunks(dn_[bass.ds(s * 256, 256), :])))

            ff(0, 0)
            ff(1, 1)
            with sp.Fori(0, 4) as i:
                r.enter(i, {2: (1, 2), 3: (1, 1), 4: (1, 2), 5: (1, 1)})
                ff(i * 2 + 2, 0)
                ff(i * 2 + 3, 1)
                r.leave(4)
            ff(10, 0)
            for t in range(NT):
                sp.wait_ge(x4_done, 3 + t)
                sp.dma_start(out[0][t * P:(t + 1) * P, :], x[:, t, :]).then_inc(out_done, 16)
            sp.wait_ge(out_done, 16 * NT)

        @block.gpsimd
        def _(g_):
            g_.dma_start(wp[:, :], a["w_pool"][0, 0]).then_inc(in_wp, 16)
            g_.dma_start(poolm[:, :, :, :], a["pool"].rearrange("p (t g s) -> p t g s", t=NT, g=4)).then_inc(in_pool, 16)
            g_.wait_ge(qknA, 1)
            g_.dma_start(mx[:, :, :], a["mem_2"][0].rearrange("(t p) d -> p t d", p=P)).then_inc(in_mem, 16)
            g_.dma_start(small[:, :], a["small"]).then_inc(in_mem, 16)
            g_.dma_start(hgrow[:, :], a["ml_head_g_2"][0].partition_broadcast(P)).then_inc(in_mem, 16)
            for j in range(1, PAIRS):
                g_.wait_ge(wp_used, j)
                g_.dma_start(wp[:, :], a["w_pool"][0, j]).then_inc(in_wp, 16)
            g_.wait_ge(sel_done, 2)
            with g_.Fori(0, EXPERTS) as e:
                g_.tensor_copy(sele_flat, selflat[:, bass.ds(e * 128, 128)]).then_inc(sele_sb, 1)
                g_.wait_ge(gt_ps, e + 1)
            g_.wait_ge(in_mem, 48)
            g_.wait_ge(st_sb, 2)
            g_.wait_ge(ga_sb, 1)
            g_.wait_ge(kc_sb, 2)
            with g_.Fori(0, GROUPS) as g:
                for dst, src, n in ((cst, vec[:, CONV:CONV + 40], 10), (lst, stall, 4), (hgg, hgrow[:, :], P),
                                    (kcg, kcall, 16), (vcg, vcall, HD), (gst, gball, 24)):
                    g_.tensor_copy(dst, src[:, bass.ds(g * n, n)]).then_inc(staged, 1)
                g_.tensor_copy(vmg, vm[:, :, bass.ds(g * P, P)]).then_inc(staged, 1)
                g_.wait_ge(ynsa_done, g * 2 + 2)
                g_.wait_ge(yml_done, g + 1)
                g_.wait_ge(ymem_done, g + 1)

        @block.scalar
        def _(act):
            chain = Chain(act, act_chain)
            act.dma_start(consts[:, :], a["consts"]).then_inc(in_consts, 16)
            act.dma_start(vecs[:, :], a["vecs"]).then_inc(in_consts, 16)

            def bias_rows(half):
                src = bass.AP(a["rpb"].tensor, (5 - half) * 8 * RPB_C + WIN_COLS - GRID_W,
                              [[1, GRID_W], [RPB_C, 6 * 8], [1, GRID_W]])
                act.dma_start(slot[5][half * 64:half * 64 + 64, 0:6 * 8 * GRID_W].rearrange("p (n c) -> p n c", n=48), src)\
                   .then_inc(in_bias, 16)

            act.wait_ge(exp_warm, 1)
            act.activation(nt_[:, 33:34], nt_[:, 32:33], ACT.Exp)

            def tile_squares(c, src, t):
                if 2 * c + t:
                    act.wait_ge(ssq_done, 2 * c + t)
                act.activation(junk, src[:, t, :], ACT.Square, accum_out=stat[:, 2 * c + t:2 * c + t + 1])\
                   .then_inc(ssq_done, 1)

            def squares(c, src):
                for t in range(NT):
                    tile_squares(c, src, t)

            for t in range(NT):
                act.wait_ge((in_x, in_x1)[t], 16)
                tile_squares(0, x, t)

            def projected(j):
                for t in range(NT):
                    act.wait_ge(zA_ps, j * 2 + t + 1)
                    act.activation(zA[:, t, 0:384], bank[t][:, 0:384], ACT.Copy).then_inc(zA_sb, 1)

            def projected_v(j):
                act.activation(zA[:, :, 384:512], ps[:, 0:2, 384:512], ACT.Copy).then_inc(vA_sb, 1)

            def pair(j, more):
                act.wait_ge(poolA_ps, j + 1)
                act.activation(dT, bank[3][:, 0:T], ACT.Copy).then_inc(dT_sb, 1)
                for h in range(2):
                    act.wait_ge(maxA, j * 2 + h + 1)
                    for t in range(NT):
                        e = act.activation(sA[:, h, t, :], sA[:, h, t, :], ACT.Exp,
                                           bias=nmA[:, 2 * h + t:2 * h + t + 1],
                                           accum_out=sumA[:, 2 * h + t:2 * h + t + 1])
                    e.then_inc(expA, 1)
                if more:
                    projected(j + 1)
                for h in range(2):
                    act.wait_ge(ptA_ps, j * 2 + h + 1)
                    act.activation(PTA[:, h, :, :], bank[6 + h].rearrange("p (k q) -> p k q", k=NT), ACT.Copy)\
                       .then_inc(ptA_sb, 1)
                act.wait_ge(oA_ps, j * 2 + 2)
                act.nop(nofuse=True)
                act.activation(yT[:, bass.ds(j + 4, 1), :].rearrange("p a t -> p (a t)"), bank[4][:, 0:T], ACT.Copy)\
                   .then_inc(yA_attn, 1)
                if more:
                    projected_v(j + 1)

            projected(0)
            projected_v(0)
            bias_rows(0)
            bias_rows(1)
            with act.Fori(0, PAIRS - 1) as j:
                pair(j, True)
            pair(PAIRS - 1, False)

            for c, n in enumerate(("norm_ple_post", "g_post_mix_2", "g_post_ffn_2")):
                act.dma_start(grows[:, c, :], a[n][0].partition_broadcast(P)).then_inc(in_rows, 16)
            act.wait_ge(in_mem, 48)
            squares(1, mx)
            for t in range(NT):
                act.wait_ge(x1_done, 3 + t)
                tile_squares(2, x, t)
            act.wait_ge(lg_max, 1)
            for t in range(NT):
                e = act.activation(lgE[:, t, :], bank[4][:, t * 16:t * 16 + 16], ACT.Exp, bias=nmE[:, t:t + 1],
                                   accum_out=smE[:, t:t + 1])
            e.then_inc(lg_exp, 1)

            act.wait_ge(ssq_done, 6)
            act.dma_start(pin[:, :, :], a["p"][0, 0].rearrange("(t p) d -> p t d", p=P)).then_inc(in_p, 16)

            def expert(e):
                act.wait_ge(gt_ps, e + 1)
                act.activation(gT, bank[2][:, 0:T], ACT.Copy).then_inc(gt_sb, 1)
                act.wait_ge(gate_ps, e + 1)
                act.activation(thE, bank[0], ACT.Tanh, scale=0.5).then_inc(gate_th, 1)
                act.wait_ge(ht_ps, e + 1)
                act.activation(hTe.rearrange("p c n -> p (c n)"), bank[2], ACT.Copy).then_inc(ht_sb, 1)
                act.wait_ge(y_ps, e + 1)
                act.activation(ysb[:, 0:512], bank[4], ACT.Copy).then_inc(y_sb, 1)
                act.wait_ge(sc_ps, e * 4 + 4)

            def experts(part):
                with act.Fori(0, PARTS[part]) as i:
                    expert(i + sum(PARTS[:part]))

            expert(0)
            experts(1)
            act.wait_ge(pT_ps, 1)
            act.activation(pT.rearrange("p k t -> p (k t)"), bank[6], ACT.Copy).then_inc(pT_sb, 1)
            for b in range(4):
                act.wait_ge(e_ps, b + 1)
                act.activation(uP[:, b // 2, (b % 2) * 512:(b % 2) * 512 + 512], bank[4 + b], ACT.Copy)\
                   .then_inc(e_sb, 1)
            act.wait_ge(e_sb, 4)
            for t in range(NT):
                if t:
                    act.wait_ge(e_sq, t)
                act.activation(junk, uP[:, t, :], ACT.Square, accum_out=stat[:, 12 + t:13 + t]).then_inc(e_sq, 1)
            for b in range(2):
                act.wait_ge(mkv_ps, b + 1)
                act.activation(kTm[:, b * 512:(b + 1) * 512], bank[b], ACT.Copy).then_inc(mkv_sb, 1)
            experts(2)
            for b in range(2):
                act.wait_ge(mkv_ps, b + 3)
                act.activation(vm[:, b, :], bank[2 + b], ACT.Copy).then_inc(mkv_sb, 1)
            experts(3)

            act.wait_ge(e_sq, 2)
            for t in range(NT):
                act.wait_ge(x_acc, 4 * EXPERTS - 2 + 2 * t)
                tile_squares(3, x, t)
            for t in range(NT):
                for h in range(2):
                    act.wait_ge(g_ps, 2 * t + h + 1)
                    act.activation(thP[:, t, h * 512:(h + 1) * 512], bank[4 + 2 * t + h], ACT.Tanh, scale=0.5)\
                       .then_inc(g_th, 1)
                act.wait_ge(x3_done, t + 1)
                tile_squares(4, x, t)

            act.wait_ge(ga_ps, 1)
            gates = bank[4][:, 0:2 * 56].rearrange("p (t n) -> p t n", t=NT)
            act.activation(ifT, gates[:, :, 48:56], ACT.Copy).then_inc(ga_th, 1)
            act.activation(gth, gates[:, :, 0:48], ACT.Tanh, scale=0.5).then_inc(ga_th, 1)
            for b in range(2):
                act.wait_ge(kvc_ps, b + 1)
                act.activation(kvc[:, 2 * b:2 * b + 2, :], bank[6 + b].rearrange("p (g t) -> p g t", g=2), ACT.Copy)\
                   .then_inc(kvc_sb, 1)
            act.wait_ge(hid_pre, 1)
            act.activation(hth, hpre, ACT.Tanh, scale=0.5).then_inc(hid_th, 1)
            act.wait_ge(ab_sb, 1)
            chain(act.activation(lnR, abR, ACT.Exp, scale=-1.0))
            act.activation(lnR, lnR, ACT.Ln, bias=1.0).then_inc(ab_ln, 1)
            act.wait_ge(em_in, 1)
            act.activation(emR, mR, ACT.Exp, scale=-1.0).then_inc(em_sb, 1)
            act.activation(nt_[:, 33:34], nt_[:, 32:33], ACT.Tanh)

            def heads_exp(n, i):
                act.wait_ge(ns_max, n + i + 1)
                o = i % 2
                for b in range(2):
                    for t, c in ((0, slice(0, 128)), (1, slice(128, 384))):
                        e = act.activation(Pn[:, o, b, c], bank[2 * o + b][:, c], ACT.Exp,
                                           bias=nmN[:, o, b, t:t + 1], accum_out=smN[:, o, b, t:t + 1])
                e.then_inc(ns_exp, 1)

            def heads_turned(n, i):
                act.wait_ge(nt_ps, n + i + 1)
                act.activation(PTn, ps[:, 4:6, 0:384], ACT.Copy).then_inc(nt_sb, 1)

            def nsa_out(n, g, pair):
                act.wait_ge(no_ps, n + 2 * pair + 2)
                act.nop(nofuse=True)
                act.activation(yT[:, bass.ds(g * 2 + pair, 1), :].rearrange("p a t -> p (a t)"),
                               bank[6 + pair][:, 0:T], ACT.Copy).then_inc(ynsa_done, 1)

            with act.Fori(0, GROUPS) as g:
                n4 = g * 4
                act.wait_ge(proj_ps, g * 6 + 1)
                act.activation(zp[:, :, 3:259], bank[5].rearrange("p (m t) -> p m t", m=2), ACT.Copy)\
                   .then_inc(proj_sb, 1)
                act.wait_ge(c_conv, g + 1)
                act.activation(thc, yc, ACT.Tanh, scale=0.5).then_inc(c_th, 1)
                act.wait_ge(proj_ps, g * 6 + 2)
                act.activation(qs, bank[0].rearrange("p (m t) -> p m t", m=2), ACT.Copy, scale=HD ** -0.5)\
                   .then_inc(proj_sb, 1)
                act.wait_ge(proj_ps, g * 6 + 3)
                act.activation(kxy[:, 0, :], bank[1][:, 0:T], ACT.Copy).then_inc(proj_sb, 1)
                act.wait_ge(proj_sb, g * 7 + 3)
                act.nop(nofuse=True)
                act.dma_start(kxy[0:64, 1, :], kxy[64:128, 0, :]).then_inc(kx_swap, 16)
                act.dma_start(kxy[64:128, 1, :], kxy[0:64, 0, :]).then_inc(kx_swap, 16)
                act.wait_ge(staged, g * 7 + 7)
                act.wait_ge(d_in, g + 1)
                act.activation(tm[:, 0:256], tm[:, 0:256], ACT.Exp, bias=lst[:, 0:1])
                act.activation(tm[:, 256:384], tm[:, 256:384], ACT.Exp, bias=lst[:, 1:2]).then_inc(d_exp, 1)
                act.wait_ge(proj_ps, g * 6 + 4)
                vo = bank[4].rearrange("p (t n) -> p t n", t=NT)
                act.activation(v1[:, :, 0:128], vo[:, :, 0:128], ACT.Copy).then_inc(proj_sb, 1)
                act.activation(so, vo[:, :, 128:256], ACT.Tanh, scale=0.5).then_inc(proj_sb, 1)
                heads_exp(n4, 0)
                act.wait_ge(proj_ps, g * 6 + 5)
                act.activation(qm, bank[7][:, 0:T], ACT.Copy, scale=ML_DH ** -0.5).then_inc(proj_sb, 1)
                heads_exp(n4, 1)
                act.wait_ge(xs_max, g + 1)
                for t in range(NT):
                    e = act.activation(Pm[:, t, :], bank[4][:, t * T:t * T + T], ACT.Exp, bias=nmM[:, t:t + 1],
                                       accum_out=smM[:, t:t + 1])
                e.then_inc(xs_exp, 1)
                act.wait_ge(cs_in, g + 1)
                act.activation(sc[:, :, 0:N_CMP], sc[:, :, 0:N_CMP], ACT.Exp).then_inc(cs_exp, 1)
                act.wait_ge(proj_ps, g * 6 + 6)
                act.activation(vsb, bank[5][:, 0:256].rearrange("p (t n) -> p t n", t=NT), ACT.Copy)\
                   .then_inc(proj_sb, 1)
                act.wait_ge(ct_ps, g + 1)
                act.activation(PTc, bank[6][:, T:2 * T], ACT.Copy).then_inc(ct_sb, 1)
                heads_turned(n4, 0)
                act.wait_ge(xt_ps, g + 1)
                act.activation(PTm, bank[7].rearrange("p (k q) -> p k q", k=NT), ACT.Copy).then_inc(xt_sb, 1)
                act.wait_ge(h_div, g + 1)
                for t in range(NT):
                    e = act.activation(y1[:, t, :], hh[:, t, :], ACT.Square, accum_out=ssM[:, t:t + 1])
                e.then_inc(h_sq, 1)
                heads_exp(n4, 2)
                heads_turned(n4, 1)
                nsa_out(n4, g, 0)
                heads_turned(n4, 2)
                heads_exp(n4, 3)
                act.wait_ge(xo_ps, g + 1)
                act.nop(nofuse=True)
                act.activation(ymem[:, bass.ds(g, 1), :].rearrange("p a t -> p (a t)"), bank[0][:, 0:T], ACT.Copy)\
                   .then_inc(ymem_done, 1)
                heads_turned(n4, 3)
                act.wait_ge(ym_ps, g + 1)
                act.nop(nofuse=True)
                act.activation(yml[:, bass.ds(g, 1), :].rearrange("p a t -> p (a t)"), bank[2][:, 0:T], ACT.Copy,
                               scale=0.5).then_inc(yml_done, 1)
                nsa_out(n4, g, 1)

            with act.Fori(0, 4) as i:
                for u in range(2):
                    m = i * 2 + u
                    act.wait_ge(mg_free, m + 1)
                    act.wait_ge(mg_ps, m + 1)
                    act.activation(thG[:, u, 0:512], bank[4 * u], ACT.Tanh, scale=0.5)
                    act.activation(thG[:, u, 512:768], bank[4 * u + 1][:, 0:T], ACT.Tanh, scale=0.5)\
                       .then_inc(mg_th, 1)

            def post(base, dst, scale, then=None):
                for t in range(NT):
                    for h in range(2):
                        act.wait_ge((out2_ps, ffo_ps)[base], 2 * t + h + 1)
                        act.activation(dst[:, t, h * 512:(h + 1) * 512], bank[2 * t + h], ACT.Copy,
                                       scale=scale).then_inc(y_evac, 1)
                    act.wait_ge(y_evac, 4 * base + 2 * t + 2)
                    act.wait_ge(ssq_done, 12 if base else 10 + t)
                    if base and t:
                        act.wait_ge(y_sq, 3)
                    act.activation(junk, dst[:, t, :], ACT.Square,
                                   accum_out=stat[:, 14 - 2 * base + t:15 - 2 * base + t]).then_inc(y_sq, 1)
                    if then is not None:
                        act.wait_ge(y_sq, t + 1)
                        act.wait_ge(x4_done, t + 1)
                        tile_squares(then, x, t)

            post(0, ysF, 0.5, then=5)

            def ff(s, par):
                for f in range(2):
                    act.wait_ge(ff_ps, s * 2 + f + 1)
                    act.activation(thF[:, par, f, :], bank[4 + 2 * par + f][:, 0:T], ACT.Tanh, scale=0.5)\
                       .then_inc(ff_th, 1)

            ff(0, 0)
            ff(1, 1)
            with act.Fori(0, 4) as i:
                ff(i * 2 + 2, 0)
                ff(i * 2 + 3, 1)
            ff(10, 0)
            post(1, ysF, 1.0)

        @block.tensor
        def _(pe):
            r = Ring(pe, full, free)

            def mm(o, l, rr, start=True, stop=True):
                return pe.matmul(o, l, rr, start=start, stop=stop)

            def turn(c, src, b0):
                for t in range(NT):
                    pe.wait_ge(xn_done, 2 * c + t + 1)
                    for h in range(2):
                        for k in range(4):
                            kk = 4 * h + k
                            ins = pe.transpose(bank[b0 + 2 * t + h][:, k * P:(k + 1) * P],
                                               src[:, t, kk * P:(kk + 1) * P], ident)
                        ins.then_inc(tr_done, 1)

            def product(o, w, n=KC, src=None, l0=0):
                for k in range(n):
                    ins = mm(o, w(k), (hT if src is None else src)[:, k, :], k == 0, k == n - 1)
                return ins

            pe.wait_ge(in_consts, 32)
            turn(0, xn, 0)
            pe.wait_ge(hT_done, 4)

            def project(j, w):
                for t in range(NT):
                    for k in range(KC):
                        ins = mm(bank[t], hT[:, k, t * P:(t + 1) * P], w(k), k == 0, k == KC - 1)
                    ins.then_inc(zA_ps, 1)

            def pair_scores(j):
                pe.wait_ge(zA_sb, j * 2 + 2)
                for t in range(NT):
                    ins = mm(bank[3][:, 0:T], zA[:, t, 0:P], poolm[:, t, bass.ds(j, 1), :].rearrange("p a s -> p (a s)"),
                             t == 0, t == NT - 1)
                ins.then_inc(poolA_ps, 1)
                pe.wait_ge(qknA, j + 1)
                for m in range(2):
                    for t in range(NT):
                        ins = pe.transpose(bank[2][:, m * T + t * P:m * T + (t + 1) * P],
                                           qkn[:, t, m * P:(m + 1) * P], ident)
                ins.then_inc(qkT_ps, 1)
                pe.wait_ge(in_wp, j * 16 + 16)
                pe.wait_ge(dT_sb, j + 1)
                mm(bank[3][:, T:2 * T], wp[:, :], dT).then_inc(poolY_ps, 1)
                pe.wait_ge(qkT_sb, j * 2 + 2)
                pe.nop(nofuse=True)
                for h in range(2):
                    for t in range(NT):
                        ins = mm(bank[4 + h][:, t * T:(t + 1) * T], qkT[64 * h:64 * h + 64, 0, t * P:(t + 1) * P],
                                 qkT[64 * h:64 * h + 64, 1, :])
                        if h == 0 and t == 0:
                            ins.then_inc(wp_used, 1)
                    ins.then_inc(sA_ps, 1)

            def pair_values(j):
                for h in range(2):
                    pe.wait_ge(pA, j * 2 + h + 1)
                    for k in range(NT):
                        for t in range(NT):
                            ins = pe.transpose(bank[6 + h][:, k * T + t * P:k * T + (t + 1) * P],
                                               sA[:, h, t, k * P:(k + 1) * P], ident)
                    ins.then_inc(ptA_ps, 1)
                for h in range(2):
                    pe.wait_ge(ptA_sb, j * 2 + h + 1)
                    for k in range(NT):
                        ins = mm(bank[4][64 * h:64 * h + 64, 0:T], zA[:, k, 384 + 64 * h:448 + 64 * h],
                                 PTA[:, h, k, :], k == 0, k == NT - 1)
                    ins.then_inc(oA_ps, 1)

            r.arrived(0, 4)
            project(0, lambda k: strip[0][:, k, :])
            pe.wait_ge(in_pool, 16)
            pe.wait_ge(zA_sb, 2)
            pe.sem_inc(free[0], 1)
            for s in range(1, PAIRS):
                r.arrived(s, 4)
            with pe.Fori(0, PAIRS - 1) as j:
                pair_scores(j)
                pe.wait_ge(vA_sb, j + 1)
                project(j + 1, lambda k: ring[:, bass.ds((j + 1) * SLOT + k * 512, 512)])
                pair_values(j)
            for s in range(1, PAIRS):
                pe.sem_inc(free[s], 1)
            last = PAIRS - 1
            pair_scores(last)

            r.count(5, 0)
            r.arrived(4, 2)
            pe.wait_ge(vA_sb, PAIRS)
            pe.wait_ge(yA_pool, PAIRS)
            pe.wait_ge(yA_attn, PAIRS - 1)
            for t in range(NT):
                for k in range(KC - 1):
                    mm(bank[t], yT[:, k, t * P:(t + 1) * P], strip[4][:, k, :], k == 0, False)
            pair_values(last)
            r.arrived(5, 2)
            pe.wait_ge(yA_attn, PAIRS)
            for t in range(NT):
                mm(bank[t], yT[:, KC - 1, t * P:(t + 1) * P], strip[4][:, KC - 1, :], False, True).then_inc(out1_ps, 1)
            for t in range(NT):
                for k in range(KC):
                    ins = mm(bank[2 + t], yT[:, k, t * P:(t + 1) * P], strip[5][:, k, :], k == 0, k == KC - 1)
                    if t == 0 and k == 0:
                        ins.then_inc(free[4], 1)
                ins.then_inc(out1_ps, 1)
            turn(2, xn, 0)
            pe.wait_ge(hT_done, 8)
            pe.wait_ge(in_mem, 48)
            for t in range(NT):
                for k in range(KC):
                    ins = mm(bank[4][:, t * 16:t * 16 + 16], hT[:, k, t * P:(t + 1) * P], wr[:, k, :], k == 0, k == KC - 1)
                    if t == 0 and k == 0:
                        ins.then_inc(free[5], 1)
            ins.then_inc(lg_ps, 1)
            pe.wait_ge(aff_sb, 1)
            for t in range(NT):
                ins = pe.transpose(bank[5][0:EXPERTS, t * P:(t + 1) * P], lgE[:, t, :], ident)
            ins.then_inc(aff_ps, 1)
            pe.wait_ge(pos_sb, 1)
            for t in range(NT):
                ins = pe.transpose(bank[6][:, t * 16:t * 16 + 16], cumT[:, t * P:(t + 1) * P], ident[0:EXPERTS, 0:EXPERTS])
            ins.then_inc(pos_ps, 1)

            wide = [s.rearrange("p (k n) -> p k n", k=2) for s in slot]
            tall = [s.rearrange("p (k n) -> p k n", k=4) for s in slot]

            def expert(e, slots):
                pe.wait_ge(sele_sb, e + 1)
                for k in range(KC):
                    for t in range(NT):
                        ins = mm(bank[3][:, k * CAP:(k + 1) * CAP], xn[:, t, k * P:(k + 1) * P], sele[:, t, 0, :],
                                 t == 0, t == NT - 1)
                ins.then_inc(xe_ps, 1)
                for t in range(NT):
                    for c in range(4):
                        ins = mm(bank[2][32 * c:32 * c + 32, t * P:(t + 1) * P], sele[:, t, 1, :], ident)
                ins.then_inc(gt_ps, 1)
                pe.wait_ge(xe_sb, e + 1)
                for n in range(8):
                    s = slots[n]
                    r.arrived(s, 1)
                    for k in (2 * (n % 4), 2 * (n % 4) + 1):
                        for c in range(4):
                            ins = mm(bank[n // 4][32 * c:32 * c + 32, :], xeT[:, k, :],
                                     wide[s][:, k % 2, c * 512:(c + 1) * 512], k == 0, k == KC - 1)
                            if k % 2 and c == 3 and n % 4 != 3 and s < SLOTS:
                                ins.then_inc(free[s], 1)
                            if n == 4 and k == 0 and c == 0:
                                ins.then_inc(free[slots[3]], 1)
                    if n % 4 == 3:
                        ins.then_inc((gate_ps, up_ps)[n // 4], 1)
                pe.wait_ge(h_sb, e + 1)
                pe.wait_ge(gt_sb, e + 1)
                for c in range(4):
                    ins = pe.transpose(bank[2][:, c * P:(c + 1) * P], hE[:, c * P:(c + 1) * P], ident)
                    if c == 0 and slots[7] < SLOTS:
                        ins.then_inc(free[slots[7]], 1)
                ins.then_inc(ht_ps, 1)
                pe.wait_ge(ht_sb, e + 1)
                for i in range(4):
                    s = slots[8 + i]
                    r.arrived(s, 1)
                    for h in range(2):
                        for c in range(4):
                            ins = mm(bank[4 + h][32 * c:32 * c + 32, :], hTe[:, c, 32 * i:32 * i + 32],
                                     tall[s][:, c, h * 512:(h + 1) * 512], i == 0, i == 3)
                    if i < 3:
                        ins.then_inc(free[s], 1)
                ins.then_inc(y_ps, 1)
                pe.wait_ge(y_sb, e * 2 + 2)
                for t in range(NT):
                    for h in range(2):
                        ins = mm(bank[(6, 4)[t] + h], gT[:, t * P:(t + 1) * P], ysb[:, h * 512:(h + 1) * 512])
                        ins.then_inc(sc_ps, 1)
                pe.wait_ge(sc_ps, e * 4 + 4)
                pe.sem_inc(free[slots[11]], 1)

            def experts(part, rot):
                with pe.Fori(0, PARTS[part]) as i:
                    r.enter(i, {s: (2, 2) for s in range(SLOTS)})
                    expert(i + sum(PARTS[:part]), around(rot))
                    r.leave(PARTS[part])

            expert(0, FIRST_SLOTS)
            experts(1, 4)
            pe.wait_ge(in_p, 16)
            pe.wait_ge(x_acc, 4 * sum(PARTS[:2]))
            for k in range(2):
                for t in range(NT):
                    ins = pe.transpose(bank[6][:, k * T + t * P:k * T + (t + 1) * P], pin[:, t, k * P:(k + 1) * P], ident)
            ins.then_inc(pT_ps, 1)
            turn(1, mx, 0)
            pe.wait_ge(pT_sb, 1)
            r.arrived(4, 1)
            wple = slot[4][:, 0:2 * D].rearrange("p (k n) -> p k n", k=2)
            for t in range(NT):
                for h in range(2):
                    for k in range(2):
                        ins = mm(bank[4 + 2 * t + h], pT[:, k, t * P:(t + 1) * P], wple[:, k, h * 512:(h + 1) * 512], k == 0, k == 1)
                    ins.then_inc(e_ps, 1)
            pe.wait_ge(hT_done, 12)
            r.arrived(5, 2)
            for h in range(4):
                for k in range(KC):
                    ins = mm(bank[h // 2][:, (h % 2) * T:(h % 2) * T + T], strip[5][:, k, h * P:(h + 1) * P],
                             hT[:, k, :], k == 0, k == KC - 1)
                    if h == 0 and k == 0:
                        ins.then_inc(free[4], 1)
                if h % 2:
                    ins.then_inc(mkv_ps, 1)
            pe.wait_ge(mkv_sb, 2)
            pe.wait_ge(e_sb, 4)
            pe.sem_inc(free[5], 1)
            experts(2, 0)
            r.arrived(0, 2)
            for t in range(NT):
                for k in range(KC):
                    ins = mm(bank[2 + t], hT[:, k, t * P:(t + 1) * P], strip[0][:, k, :], k == 0, k == KC - 1)
                ins.then_inc(mkv_ps, 1)
            pe.wait_ge(mkv_sb, 4)
            pe.sem_inc(free[0], 1)
            experts(3, 3)

            pe.wait_ge(x_acc, 4 * EXPERTS)
            turn(3, xn, 0)
            pe.wait_ge(hT_done, 16)
            r.arrived(3, 2)
            r.arrived(4, 2)
            for t in range(NT):
                for h in range(2):
                    for k in range(KC):
                        ins = mm(bank[4 + 2 * t + h], hT[:, k, t * P:(t + 1) * P], strip[3 + h][:, k, :], k == 0, k == KC - 1)
                    ins.then_inc(g_ps, 1)

            turn(4, xn, 0)
            pe.wait_ge(hT_done, 20)
            for t in range(NT):
                for k in range(KC):
                    ins = mm(bank[4][:, t * 56:t * 56 + 56], hT[:, k, t * P:(t + 1) * P], wsm[:, k, :], k == 0, k == KC - 1)
                    if t == 0 and k < 2:
                        ins.then_inc(free[3 + k], 1)
            ins.then_inc(ga_ps, 1)
            r.arrived(5, 2)
            for g in range(GROUPS):
                o = bank[6 + g // 2][:, (g % 2) * T:(g % 2) * T + T]
                for k in range(KC):
                    for m in range(2):
                        ins = mm(o[64 * m:64 * m + 64, :], strip[5][:, k, m * 256 + g * HD:m * 256 + g * HD + HD],
                                 hT[:, k, :], k == 0, k == KC - 1)
                if g % 2:
                    ins.then_inc(kvc_ps, 1)
                if g == 0:
                    pe.wait_ge(ga_th, 1)
                    for m in range(2):
                        for t in range(NT):
                            ins = pe.transpose(bank[5][0:4, m * T + t * P:m * T + (t + 1) * P],
                                               ifT[:, t, 4 * m:4 * m + 4], ident)
                    ins.then_inc(if_ps, 1)
            pe.wait_ge(kvc_sb, 3)
            r.arrived(2, 2)
            w1 = slot[2].rearrange("p (l h) -> p l h", l=CMP_L)
            for l in range(CMP_L):
                for m in range(2):
                    ins = mm(bank[m][:, 0:75].rearrange("p (g n) -> p g n", g=5), w1[64 * m:64 * m + 64, l, :],
                             kvc[64 * m:64 * m + 64, :, l:l + CMP_STRIDE * (N_CMP - 1) + 1:CMP_STRIDE],
                             l == 0, l == CMP_L - 1)
                    if l == 0 and m == 0:
                        ins.then_inc(free[5], 1)
            ins.then_inc(hid_ps, 1)
            pe.wait_ge(hid_sb, 1)
            for m in range(2):
                mm(bank[2][64 * m:64 * m + 64, 0:60], w2[:, 0:HD], hidk)
            for g in range(GROUPS):
                for i in range(4):
                    ins = mm(bank[3][32 * i:32 * i + 32, g * HD:(g + 1) * HD], hidv[:, g, :], w2[:, HD:2 * HD])
            ins.then_inc(kc_ps, 1)
            pe.wait_ge(em_sb, 1)
            for n, row in enumerate((aR, emR)):
                for t in range(NT):
                    ins = pe.transpose(bank[7][:, (n * 2 + t) * 4:(n * 2 + t) * 4 + 4], row[:, t * P:(t + 1) * P],
                                       ident[0:4, 0:4])
                    if n == 0 and t == 0:
                        ins.then_inc(free[2], 1)
            ins.then_inc(st_ps, 1)
            pe.wait_ge(st_sb, 2)
            pe.wait_ge(kc_sb, 2)

            def scores(g, i):
                par, hp = i % 2, i // 2
                for b in range(2):
                    key = kxy[64 * par:64 * par + 64, b ^ par, :]
                    q = qs[64 * par:64 * par + 64, hp, :]
                    o = bank[2 * par + b]
                    mm(o[:, 0:128], q[:, 0:128], key[:, 0:128])
                    ins = mm(o[:, 128:384], q[:, 128:256], key)
                ins.then_inc(ns_ps, 1)

            def turned(n4, i):
                pe.wait_ge(np_sb, n4 + i + 1)
                for b in range(2):
                    for c in range(3):
                        ins = pe.transpose(bank[4 + b][:, c * P:(c + 1) * P], Pn[:, i % 2, b, c * P:(c + 1) * P], ident)
                ins.then_inc(nt_ps, 1)

            def values(n4, i):
                pe.wait_ge(nt_sb, n4 + i + 1)
                par, hp = i % 2, i // 2
                o = bank[6 + hp][64 * par:64 * par + 64, :]
                mm(o[:, 0:T], vsb[:, 0, 0:64], PTn[:, 0, 0:256], True, False)
                mm(o[:, 0:T], vsb[:, 0, 64:128], PTn[:, 1, 0:256], False, False)
                mm(o[:, 128:256], vsb[:, 1, 0:64], PTn[:, 0, 256:384], False, False)
                mm(o[:, 128:256], vsb[:, 1, 64:128], PTn[:, 1, 256:384], False, False)
                mm(o[:, 0:T], vcg[32 * i:32 * i + 32, :], PTc[32 * i:32 * i + 32, :], False, True).then_inc(no_ps, 1)

            memq = slot[1][:, 0:D].rearrange("p (k n) -> p k n", k=KC)
            with pe.Fori(0, GROUPS) as g:
                r.enter(g, {0: (1, 4), 1: (1, 1), 5: (1, 5)})
                n4 = g * 4
                r.arrived(0, 4)
                for m in range(2):
                    ins = product(bank[5][:, m * T:(m + 1) * T], lambda k: strip[0][:, k, m * P:(m + 1) * P])
                ins.then_inc(proj_ps, 1)
                r.arrived(5, 5)
                for m in range(2):
                    ins = product(bank[0][:, m * T:(m + 1) * T], lambda k: strip[5][:, k, m * P:(m + 1) * P])
                ins.then_inc(proj_ps, 1)
                product(bank[1][:, 0:T], lambda k: strip[5][:, k, 256:384]).then_inc(proj_ps, 1)
                pe.wait_ge(proj_sb, g * 7 + 1)
                pe.nop(nofuse=True)
                mm(bank[7][:, T:2 * T], const("ones", 4), negMd[:, bass.ds(g * T, T)]).then_inc(d_ps, 1)
                for t in range(NT):
                    for k in range(KC):
                        ins = mm(bank[4][:, t * T:(t + 1) * T], hT[:, k, t * P:(t + 1) * P], strip[0][:, k, 256:512],
                                 k == 0, k == KC - 1)
                ins.then_inc(proj_ps, 1)
                pe.wait_ge(proj_sb, g * 7 + 3)
                pe.wait_ge(kx_swap, g * 32 + 32)
                pe.nop(nofuse=True)
                scores(g, 0)
                pe.wait_ge(d_in, g + 1)
                r.arrived(1, 1)
                for k in range(KC):
                    ins = mm(bank[7][:, 0:T], memq[:, k, :], hT[:, k, :], k == 0, k == KC - 1)
                    if k == 0:
                        ins.then_inc(free[0], 1)
                ins.then_inc(proj_ps, 1)
                scores(g, 1)
                pe.wait_ge(proj_sb, g * 7 + 6)
                for t in range(NT):
                    ins = mm(bank[4][:, t * T:(t + 1) * T], qm[:, t * P:(t + 1) * P], kTm[:, bass.ds(g * T, T)])
                    if t == 0:
                        ins.then_inc(free[1], 1)
                ins.then_inc(xs_ps, 1)
                pe.wait_ge(c_qk, g + 1)
                mm(bank[6][:, 0:T], yc[:, 1, 0:P], yc[:, 0, :])
                mm(bank[6][:, T:T + P], yc[:, 1, P:T], yc[:, 0, P:T])
                pe.wait_ge(staged, g * 7 + 7)
                pe.nop(nofuse=True)
                for par in range(2):
                    for hp in range(2):
                        for t in range(NT):
                            c = 384 + (hp * 2 + t) * 16
                            ins = mm(bank[6 + par][:, c:c + N_CMP], qs[64 * par:64 * par + 64, hp, t * P:(t + 1) * P],
                                     kcg[64 * par:64 * par + 64, 0:N_CMP])
                ins.then_inc(cs_ps, 1)
                for t in range(NT):
                    for k in range(KC):
                        ins = mm(bank[5][:, t * P:(t + 1) * P], hT[:, k, t * P:(t + 1) * P], strip[5][:, k, 384:512],
                                 k == 0, k == KC - 1)
                ins.then_inc(proj_ps, 1)
                pe.wait_ge(w_sb, g + 1)
                mm(bank[7][:, 0:129], Wm[:, 0:128], v1[:, 0, 0:129]).then_inc(free[5], 1)
                mm(bank[7][:, 132:261], Wm[:, 128:256], v1[:, 0, 0:129], True, False)
                mm(bank[7][:, 132:261], Wm[:, 256:384], v1[:, 1, 0:129], False, True).then_inc(n_ps, 1)
                pe.wait_ge(cp_sb, g + 1)
                pe.wait_ge(cs_in, g + 1)
                for t in range(NT):
                    ins = pe.transpose(bank[6][:, T + t * P:T + (t + 1) * P], Pc[:, t, :, :].rearrange("p i n -> p (i n)"), ident)
                ins.then_inc(ct_ps, 1)
                pe.wait_ge(proj_sb, g * 7 + 7)
                turned(n4, 0)
                pe.wait_ge(xp_sb, g + 1)
                pe.wait_ge(h_div, g + 1)
                for k in range(NT):
                    for t in range(NT):
                        ins = pe.transpose(bank[7][:, k * T + t * P:k * T + (t + 1) * P], Pm[:, t, k * P:(k + 1) * P], ident)
                ins.then_inc(xt_ps, 1)
                scores(g, 2)
                pe.wait_ge(ct_sb, g + 1)
                values(n4, 0)
                turned(n4, 1)
                scores(g, 3)
                values(n4, 1)
                turned(n4, 2)
                pe.wait_ge(xt_sb, g + 1)
                for k in range(NT):
                    ins = mm(bank[0][:, 0:T], vmg[:, k, :], PTm[:, k, :], k == 0, k == NT - 1)
                ins.then_inc(xo_ps, 1)
                values(n4, 2)
                turned(n4, 3)
                pe.wait_ge(ym_sb, g + 1)
                for t in range(NT):
                    ins = pe.transpose(bank[2][:, t * P:(t + 1) * P], y1[:, t, :], ident)
                ins.then_inc(ym_ps, 1)
                values(n4, 3)
                pe.wait_ge(ymem_done, g + 1)
                r.leave(GROUPS)

            pe.wait_ge(ynsa_done, 8)
            pe.wait_ge(yml_done, 4)
            pe.wait_ge(ymem_done, 4)
            with pe.Fori(0, 4) as i:
                r.enter(i, {s: (1, 3) for s in (2, 3, 4, 5)})
                for u in range(2):
                    gs = slot[2 + 2 * u][:, 0:3072].rearrange("p (k n) -> p k n", k=KC)
                    pj = slot[3 + 2 * u][:, 0:2048].rearrange("p (k n) -> p k n", k=16)
                    pe.wait_ge(mg_free, i * 2 + u + 1)
                    r.arrived(2 + 2 * u, 3)
                    for b in range(3):
                        ins = product(bank[4 * u + b // 2][:, (b % 2) * T:(b % 2) * T + T],
                                      lambda k: gs[:, k, b * P:(b + 1) * P])
                    ins.then_inc(mg_ps, 1)
                    r.arrived(3 + 2 * u, 3)
                    ins = product(bank[4 * u + 2][:, 0:T], lambda k: pj[:, k, :], KC, yT)
                    ins.then_inc(free[2 + 2 * u], 1)
                    product(bank[4 * u + 2][:, T:2 * T], lambda k: pj[:, 8 + k, :], 4, yml)
                    ins = product(bank[4 * u + 3][:, 0:T], lambda k: pj[:, 12 + k, :], 4, ymem)
                    ins.then_inc(mp_ps, 1)
                    pe.wait_ge(mp_ps, i * 2 + u + 1)
                    pe.sem_inc(free[3 + 2 * u], 1)
                r.leave(4)
            pe.wait_ge(mg_free, 10)
            r.arrived(0, 2)
            r.arrived(1, 2)
            for t in range(NT):
                for h in range(2):
                    for k in range(KC):
                        ins = mm(bank[2 * t + h], yT2[:, k, t * P:(t + 1) * P], strip[h][:, k, :], k == 0, k == KC - 1)
                    ins.then_inc(out2_ps, 1)
            turn(5, xF, 4)
            pe.wait_ge(hT_done, 24)

            def ff_in(s, par):
                r.arrived(2 + 2 * par, 2)
                for f in range(2):
                    o = bank[4 + 2 * par + f]
                    for m in range(2):
                        ins = product(o[:, m * T:(m + 1) * T],
                                      lambda k: strip[2 + 2 * par][:, k, m * 256 + f * P:m * 256 + (f + 1) * P])
                    ins.then_inc(ff_ps, 1)

            def ff_down(s, par, first=False, last=False):
                r.arrived(3 + 2 * par, 1)
                w = slot[3 + 2 * par][:, 0:2 * D].rearrange("p (k n) -> p k n", k=2)
                pe.wait_ge(ff_h, s * 2 + 2)
                order = [(k, t, h) for k in range(2) for t in range(NT) for h in range(2)]
                if last:
                    order.sort(key=lambda o: o[1])
                for k, t, h in order:
                            ins = mm(bank[2 * t + h], hF[:, par, k, t * P:(t + 1) * P], w[:, k, h * 512:(h + 1) * 512],
                                     first and k == 0, last and k == 1)
                            if last and k == 1:
                                ins.then_inc(ffo_ps, 1)
                            elif k == 0 and t == 0 and h == 0:
                                ins.then_inc(free[4 - 2 * par], 1)
                if not last:
                    ins.then_inc(free[3 + 2 * par], 1)

            ff_in(0, 0)
            pe.wait_ge(ff_ps, 2)
            pe.sem_inc(free[2], 1)
            ff_in(1, 1)
            ff_down(0, 0, first=True)
            with pe.Fori(0, 4) as i:
                r.enter(i, {2: (1, 2), 3: (1, 1), 4: (1, 2), 5: (1, 1)})
                ff_in(i * 2 + 2, 0)
                ff_down(i * 2 + 1, 1)
                ff_in(i * 2 + 3, 1)
                ff_down(i * 2 + 2, 0)
                r.leave(4)
            ff_in(10, 0)
            ff_down(9, 1)
            ff_down(10, 0, last=True)

        @block.vector
        def _(dve):
            chain = Chain(dve, dve_chain)
            RS = 12

            def rsqrt(o, ss, n, w):
                v, y, q = nt_[:, 0:w], nt_[:, 8:8 + w], nt_[:, 16:16 + w]
                chain(dve.tensor_scalar(v, ss, 1.0 / n, EPS, ALU.mult, ALU.add))
                chain(dve.tensor_scalar(y.bitcast(I32), v.bitcast(I32), 1, None, ALU.logical_shift_right))
                chain(dve.tensor_scalar(y.bitcast(I32), y.bitcast(I32), -1.0, RSQRT_SEED, ALU.mult, ALU.add))
                for it in range(3):
                    chain(dve.tensor_tensor(q, y, y, ALU.mult))
                    chain(dve.scalar_tensor_tensor(out=q, in0=q, scalar=-0.5, in1=v, op0=ALU.mult, op1=ALU.mult))
                    chain(dve.scalar_tensor_tensor(out=y if it < 2 else o, in0=q, scalar=1.5, in1=y, op0=ALU.add,
                                                   op1=ALU.mult))

            def tile_normed(c, src, dst, t):
                dve.wait_ge(ssq_done, 2 * c + t + 1)
                rsqrt(rst[:, 2 * c + t:2 * c + t + 1], stat[:, 2 * c + t:2 * c + t + 1], D, 1)
                dve.tensor_scalar(dst[:, t, :], src[:, t, :], rst[:, 2 * c + t:2 * c + t + 1], None, ALU.mult)\
                   .then_inc(xn_done, 1)

            def normed(c, src, dst):
                for t in range(NT):
                    tile_normed(c, src, dst, t)

            def gained(c, b0):
                for t in range(NT):
                    for h in range(2):
                        n = 4 * TURNS[c] + 2 * t + h
                        dve.wait_ge(tr_done, n + 1)
                        gain = vec[:, GAIN(c) + 4 * h:GAIN(c) + 4 * h + 4].unsqueeze(2).broadcast_to([P, 4, P])
                        dve.tensor_tensor(hT[:, 4 * h:4 * h + 4, t * P:(t + 1) * P],
                                          bank[b0 + 2 * t + h].rearrange("p (k t) -> p k t", k=4), gain, ALU.mult)\
                           .then_inc(hT_done, 1)

            dve.memset(nt_[:, 32:33], 0.0).then_inc(exp_warm, 1)
            normed(0, x, xn)
            dve.wait_ge(in_consts, 32)
            gained(0, 0)
            def qk_normed(j):
                dve.wait_ge(zA_sb, j * 2 + 2)
                chain(dve.tensor_tensor(sqA, zA[:, :, 128:384], zA[:, :, 128:384], ALU.mult))
                chain(dve.tensor_reduce(ssA, sqA.rearrange("p t (h d) -> p (t h) d", d=HD), AX, ALU.add))
                rsqrt(rsA, ssA, HD, 8)
                for t in range(NT):
                    ins = dve.tensor_tensor(qkn[:, t, :].rearrange("p (h d) -> p h d", d=HD),
                                            zA[:, t, 128:384].rearrange("p (h d) -> p h d", d=HD),
                                            rsA[:, 4 * t:4 * t + 4].unsqueeze(2).broadcast_to([P, 4, HD]), ALU.mult)
                ins.then_inc(qknA, 1)

            def bias_table():
                dve.wait_ge(in_bias, 2 * 16)
                mask = const("wmask").unsqueeze(1).broadcast_to([P, 6, GRID_W])
                for h in range(8):
                    ins = dve.tensor_tensor(btab[:, h, :, :], braw[:, h, :, ::-1], mask, ALU.add)
                ins.then_inc(bias_sb, 1)
                dve.wait_ge(bias_sb, 1)
                dve.memset(nt_[:, 35:36], 0.0).then_inc(free[5], 1)

            def pair(j, first=False):
                dve.wait_ge(qkT_ps, j + 1)
                dve.tensor_scalar(qkT[:, 0, :], bank[2][:, 0:T], vec[:, QN:QN + 1], HD ** -0.5, ALU.mult, ALU.mult)\
                   .then_inc(qkT_sb, 1)
                dve.tensor_scalar(qkT[:, 1, :], bank[2][:, T:2 * T], vec[:, KN:KN + 1], None, ALU.mult)\
                   .then_inc(qkT_sb, 1)
                dve.wait_ge(poolY_ps, j + 1)
                dve.tensor_scalar(yT[:, bass.ds(j, 1), :].rearrange("p a t -> p (a t)"), bank[3][:, T:2 * T],
                                  vec[:, bass.ds(j + PSCALE, 1)], None, ALU.mult).then_inc(yA_pool, 1)
                if first:
                    bias_table()
                for h in range(2):
                    dve.wait_ge(sA_ps, j * 2 + h + 1)
                    for t in range(NT):
                        bias = btab[:, bass.ds(j * 2 + h, 1), 2 - 2 * t:6 - 2 * t, :].rearrange("p a r c -> p (a r c)")
                        ins = dve.tensor_tensor(sA[:, h, t, :], bank[4 + h][:, t * T:(t + 1) * T], bias, ALU.add)
                    chain(ins)
                    dve.tensor_reduce(nmA[:, 2 * h:2 * h + 2], sA[:, h, :, :], AX, ALU.max, negate=True).then_inc(maxA, 1)
                for h in range(2):
                    dve.wait_ge(expA, j * 2 + h + 1)
                    chain(dve.reciprocal(rcA[:, 2 * h:2 * h + 2], sumA[:, 2 * h:2 * h + 2]))
                    for t in range(NT):
                        ins = dve.tensor_scalar(sA[:, h, t, :], sA[:, h, t, :], rcA[:, 2 * h + t:2 * h + t + 1], None,
                                                ALU.mult)
                    ins.then_inc(pA, 1)

            qk_normed(0)
            pair(0, first=True)
            qk_normed(1)
            with dve.Fori(0, PAIRS - 2) as i:
                chain.enter(i, 2 + RS + 2 + 2)
                pair(i + 1)
                qk_normed(i + 2)
                chain.leave(PAIRS - 2)
            pair(PAIRS - 1)

            normed(1, mx, mx)
            for n in range(2):
                for t in range(NT):
                    dve.wait_ge(out1_ps, 2 * n + t + 1)
                    dve.tensor_tensor(x[:, t, n * 512:(n + 1) * 512], x[:, t, n * 512:(n + 1) * 512],
                                      bank[2 * n + t], ALU.add).then_inc(x1_done, 1)
                    if n == 1:
                        tile_normed(2, x, xn, t)
            gained(2, 0)

            dve.wait_ge(lg_ps, 1)
            dve.tensor_reduce(nmE, bank[4][:, 0:32].rearrange("p (t e) -> p t e", t=NT), AX, ALU.max, negate=True)\
               .then_inc(lg_max, 1)
            dve.memset(onesT, 1.0)
            dve.wait_ge(lg_exp, 1)
            chain(dve.reciprocal(smE, smE))
            dve.tensor_tensor(lgE, lgE, smE.unsqueeze(2).broadcast_to([P, NT, EXPERTS]), ALU.mult).then_inc(aff_sb, 1)
            dve.wait_ge(aff_ps, 1)
            chain(dve.tensor_copy(affT, bank[5][0:EXPERTS, 0:T]))
            for it in range(CAP // 8):
                chain(dve.max(m8, affT))
                chain(dve.match_replace(affT, m8, affT, -1.0))
            chain(dve.tensor_scalar(selT, affT, 0.0, None, ALU.is_lt))
            chain(dve.tensor_tensor_scan(cumT, onesT, selT, 0.0, ALU.mult, ALU.add))
            dve.tensor_tensor(cumT, cumT, selT, ALU.mult).then_inc(pos_sb, 1)
            dve.wait_ge(pos_ps, 1)
            chain(dve.tensor_copy(posT, bank[6][:, 0:32].rearrange("p (t e) -> p t e", t=NT)))
            for t in range(NT):
                pos = posT[:, t, :].unsqueeze(2).broadcast_to([P, EXPERTS, CAP])
                aff = lgE[:, t, :].unsqueeze(2).broadcast_to([P, EXPERTS, CAP])
                place = const("iota1").unsqueeze(1).broadcast_to([P, EXPERTS, CAP])
                chain(dve.tensor_tensor(selall[:, :, t, 0, :], pos, place, ALU.is_equal))
                dve.tensor_tensor(selall[:, :, t, 1, :], selall[:, :, t, 0, :], aff, ALU.mult).then_inc(sel_done, 1)

            gain = vec[:, GAIN(2):GAIN(2) + 8].unsqueeze(2).broadcast_to([P, KC, CAP])
            def expert(e):
                dve.wait_ge(xe_ps, e + 1)
                dve.tensor_tensor(xeT, bank[3][:, 0:KC * CAP].rearrange("p (k s) -> p k s", k=KC), gain, ALU.mult)\
                   .then_inc(xe_sb, 1)
                dve.wait_ge(gate_th, e + 1)
                chain(dve.scalar_tensor_tensor(out=thE, in0=thE, scalar=1.0, in1=bank[0], op0=ALU.add, op1=ALU.mult))
                dve.wait_ge(up_ps, e + 1)
                dve.scalar_tensor_tensor(out=hE, in0=thE, scalar=0.5, in1=bank[1], op0=ALU.mult, op1=ALU.mult)\
                   .then_inc(h_sb, 1)
                dve.wait_ge(y_ps, e + 1)
                dve.tensor_copy(ysb[:, 512:1024], bank[5]).then_inc(y_sb, 1)
                for t in range(NT):
                    for h in range(2):
                        dve.wait_ge(sc_ps, e * 4 + 2 * t + h + 1)
                        dve.tensor_tensor(x[:, t, h * 512:(h + 1) * 512], x[:, t, h * 512:(h + 1) * 512],
                                          bank[(6, 4)[t] + h], ALU.add).then_inc(x_acc, 1)

            def experts(part):
                with dve.Fori(0, PARTS[part]) as i:
                    chain.enter(i, 1)
                    expert(i + sum(PARTS[:part]))
                    chain.leave(PARTS[part])

            expert(0)
            experts(1)
            gained(1, 0)
            dve.wait_ge(e_sq, 2)
            dve.wait_ge(in_rows, 16 * 3)
            rsqrt(rst[:, 12:14], stat[:, 12:14], D, 2)
            for t in range(NT):
                chain(dve.scalar_tensor_tensor(out=uP[:, t, :], in0=uP[:, t, :], scalar=rst[:, 12 + t:13 + t],
                                               in1=grows[:, 0, :], op0=ALU.mult, op1=ALU.mult))
            experts(2)
            experts(3)

            normed(3, x, xn)
            gained(3, 0)
            for t in range(NT):
                dve.wait_ge(g_th, 2 * t + 2)
                chain(dve.scalar_tensor_tensor(out=uP[:, t, :], in0=thP[:, t, :], scalar=1.0, in1=uP[:, t, :],
                                               op0=ALU.add, op1=ALU.mult))
                dve.scalar_tensor_tensor(out=x[:, t, :], in0=uP[:, t, :], scalar=0.5, in1=x[:, t, :],
                                         op0=ALU.mult, op1=ALU.add).then_inc(x3_done, 1)
                tile_normed(4, x, xn, t)
            gained(4, 0)

            dve.memset(kvc[:, 4, :], 0.0)
            dve.memset(hidv, 0.0)
            dve.memset(zp[:, :, 0:3], 0.0)
            dve.memset(v1[:, :, 128:132], 1.0)
            chain(dve.memset(Pc, 0.0))
            dve.wait_ge(kvc_sb, 2)
            dve.tensor_copy(kvc[:, 4, 0:CMP_L], peT[:, :]).then_inc(kvc_sb, 1)
            dve.wait_ge(if_ps, 1)
            chain(dve.tensor_scalar(iR, bank[5][0:4, 0:T], ifb[0:4, 0:1], None, ALU.add))
            chain(dve.tensor_scalar(fR, bank[5][0:4, T:2 * T], ifb[0:4, 1:2], None, ALU.add))
            chain(dve.tensor_scalar(mnR, fR, 0.0, None, ALU.min))
            chain(dve.tensor_scalar(MR, fR, -1.0, None, ALU.mult))
            dve.tensor_tensor(abR, fR, MR, ALU.max).then_inc(ab_sb, 1)
            dve.wait_ge(ga_th, 2)
            for b in range(3):
                for q in range(2):
                    o = gball.rearrange("p (g b q i t) -> p g b q i t", g=4, b=3, q=2, i=2)[:, :, b, q, :, :]
                    for t in range(NT):
                        src = gth[:, t, :].rearrange("p (g i q b) -> p g i q b", g=4, i=2, q=2)[:, :, :, q, b]
                        ins = dve.tensor_scalar(o[:, :, :, t], src, 1.0, 0.5, ALU.add, ALU.mult)
            ins.then_inc(ga_sb, 1)
            dve.wait_ge(hid_ps, 1)
            for m in range(2):
                chain(dve.tensor_copy(hidb[:, m:m + 1], bank[m][:, 60:61]))
            for m in range(2):
                ins = dve.tensor_scalar(hpre[:, m, :], bank[m][:, 0:60], hidb[:, m:m + 1], None, ALU.add)
            ins.then_inc(hid_pre, 1)
            dve.wait_ge(hid_pre, 1)
            dve.wait_ge(hid_th, 1)
            chain(dve.scalar_tensor_tensor(out=hth, in0=hth, scalar=1.0, in1=hpre, op0=ALU.add, op1=ALU.mult))
            dve.tensor_scalar(hidk, hth[:, 0, :], 0.5, None, ALU.mult)
            dve.tensor_scalar(hidv[:, :, 0:N_CMP], hth[:, 1, :].rearrange("p (g n) -> p g n", g=4), 0.5, None, ALU.mult)\
               .then_inc(hid_sb, 1)
            dve.wait_ge(ab_ln, 1)
            chain(dve.tensor_tensor(mnR, mnR, lnR, ALU.subtract))
            chain(dve.tensor_scalar(MR, mnR, 0.0, 1.0, ALU.mult, ALU.add))
            chain(dve.tensor_tensor_scan(BR, MR, mnR, 0.0, ALU.mult, ALU.add))
            chain(dve.tensor_tensor(aR, iR, BR, ALU.subtract))
            chain(dve.tensor_tensor_scan(MR, aR, aR, 0.0, ALU.max, ALU.max))
            dve.tensor_tensor(mR, BR, MR, ALU.add).then_inc(em_in, 1)
            chain(dve.tensor_scalar(nMR, MR, -1.0, None, ALU.mult))
            dve.tensor_tensor(negMd.rearrange("p (h t) -> p h t", h=4), nMR.unsqueeze(1).broadcast_to([4, 4, T]),
                              const("eye4", 4).unsqueeze(2).broadcast_to([4, 4, T]), ALU.mult).then_inc(st_sb, 1)
            dve.wait_ge(kc_ps, 1)
            dve.tensor_copy(kcall.rearrange("p (g n) -> p g n", g=4)[:, :, 0:N_CMP],
                            bank[2][:, 0:60].rearrange("p (g n) -> p g n", g=4)).then_inc(kc_sb, 1)
            dve.memset(kcall.rearrange("p (g n) -> p g n", g=4)[:, :, N_CMP:16], 0.0)
            dve.tensor_copy(vcall, bank[3][:, 0:256]).then_inc(kc_sb, 1)
            dve.wait_ge(st_ps, 1)
            dve.tensor_copy(stall.rearrange("p (h n) -> p h n", h=4),
                            bank[7][:, 0:16].rearrange("p (n h) -> p h n", h=4)).then_inc(st_sb, 1)

            cadd = const("cmpadd").rearrange("p (t n) -> p t n", t=NT)[:, :, 0:N_CMP].unsqueeze(1)\
                .broadcast_to([P, 2, NT, N_CMP])
            cmul = const("cmpmul").rearrange("p (t n) -> p t n", t=NT)[:, :, 0:N_CMP].unsqueeze(1)\
                .broadcast_to([P, 2, NT, N_CMP])
            gv = gst.rearrange("p (b q i t) -> p b q i t", b=3, q=2, i=2)

            def head_max(n4, i):
                par = i % 2
                dve.wait_ge(ns_ps, n4 + i + 1)
                s = ps[:, 2 * par:2 * par + 2, 0:384].rearrange("p b (c k) -> p b c k", c=3)
                chain(dve.tensor_tensor(s[:, :, 0, :], s[:, :, 0, :], caus.unsqueeze(1).broadcast_to([P, 2, P]), ALU.add))
                chain(dve.tensor_tensor(s[:, :, 2, :], s[:, :, 2, :], caus.unsqueeze(1).broadcast_to([P, 2, P]), ALU.add))
                dve.tensor_reduce(nmN[:, par, :, 0], s[:, :, 0, :], AX, ALU.max, negate=True)
                dve.tensor_reduce(nmN[:, par, :, 1], ps[:, 2 * par:2 * par + 2, 128:384], AX, ALU.max, negate=True)\
                   .then_inc(ns_max, 1)

            def head_probs(n4, i):
                par, hp = i % 2, i // 2
                dve.wait_ge(ns_exp, n4 + i + 1)
                chain(dve.reciprocal(rcN[:, par, :, :], smN[:, par, :, :]))
                chain(dve.tensor_tensor(rcN[:, par, :, :], rcN[:, par, :, :], gv[:, 1:3, par, hp, :], ALU.mult))
                for b in range(2):
                    for t, c in ((0, slice(0, 128)), (1, slice(128, 384))):
                        ins = dve.tensor_scalar(Pn[:, par, b, c], Pn[:, par, b, c], rcN[:, par, b, t:t + 1], None, ALU.mult)
                ins.then_inc(np_sb, 1)

            with dve.Fori(0, GROUPS) as g:
                n4 = g * 4
                chain.enter(g, 7 + 1 + 2 + 4 + 4 + 4 * 2 + 4 * 2 + RS + 2)
                dve.wait_ge(staged, g * 7 + 7)
                dve.wait_ge(proj_sb, g * 7 + 1)
                for j in range(4):
                    for m in range(2):
                        w = cst[:, 5 * m + j:5 * m + j + 1]
                        if j == 0:
                            ins = dve.tensor_scalar(yc[:, m, :], zp[:, m, 0:T], w, cst[:, 5 * m + 4:5 * m + 5],
                                                    ALU.mult, ALU.add)
                        else:
                            ins = dve.scalar_tensor_tensor(out=yc[:, m, :], in0=zp[:, m, j:j + T], scalar=w,
                                                           in1=yc[:, m, :], op0=ALU.mult, op1=ALU.add)
                        if j < 3:
                            chain(ins)
                        elif m == 0:
                            chain(ins)
                        else:
                            ins.then_inc(c_conv, 1)
                dve.wait_ge(c_th, g + 1)
                dve.scalar_tensor_tensor(out=yc, in0=thc, scalar=1.0, in1=yc, op0=ALU.add, op1=ALU.mult).then_inc(c_qk, 1)
                dve.wait_ge(d_ps, g + 1)
                dve.tensor_tensor(tm[:, 0:T], bank[7][:, T:2 * T], causTz, ALU.add)
                dve.tensor_tensor(tm[:, T:384], bank[7][:, T + P:2 * T], causT, ALU.add).then_inc(d_in, 1)
                head_max(n4, 0)
                head_probs(n4, 0)
                head_max(n4, 1)
                dve.wait_ge(xs_ps, g + 1)
                dve.tensor_reduce(nmM, bank[4].rearrange("p (t k) -> p t k", t=NT), AX, ALU.max, negate=True)\
                   .then_inc(xs_max, 1)
                dve.wait_ge(cs_ps, g + 1)
                for par in range(2):
                    ins = dve.tensor_tensor(
                        sc[:, 4 * par:4 * par + 4, 0:N_CMP].rearrange("p (i t) n -> p i t n", i=2),
                        bank[6 + par][:, 384:448].rearrange("p (i t n) -> p i t n", i=2, t=NT)[:, :, :, 0:N_CMP],
                        cadd, ALU.add)
                chain(ins)
                chain(dve.tensor_reduce(nmC, sc[:, :, 0:N_CMP], AX, ALU.max, negate=True))
                dve.tensor_tensor(sc[:, :, 0:N_CMP], sc[:, :, 0:N_CMP], nmC.unsqueeze(2).broadcast_to([P, 8, N_CMP]),
                                  ALU.add).then_inc(cs_in, 1)
                dve.wait_ge(d_exp, g + 1)
                dve.scalar_tensor_tensor(out=Wm, in0=bank[6][:, 0:384], scalar=0.25 * ML_DH ** -0.5, in1=tm,
                                         op0=ALU.mult, op1=ALU.mult).then_inc(w_sb, 1)
                head_probs(n4, 1)
                dve.wait_ge(xs_exp, g + 1)
                chain(dve.reciprocal(rcM, smM))
                for t in range(NT):
                    ins = dve.tensor_scalar(Pm[:, t, :], Pm[:, t, :], rcM[:, t:t + 1], None, ALU.mult)
                ins.then_inc(xp_sb, 1)
                dve.wait_ge(cs_exp, g + 1)
                chain(dve.tensor_reduce(smC, sc[:, :, 0:N_CMP], AX, ALU.add))
                chain(dve.reciprocal(rcC, smC))
                chain(dve.tensor_tensor(rcC, rcC, gst[:, 0:8], ALU.mult))
                chain(dve.tensor_tensor(sc[:, :, 0:N_CMP], sc[:, :, 0:N_CMP],
                                        rcC.unsqueeze(2).broadcast_to([P, 8, N_CMP]), ALU.mult))
                pcv = Pc.rearrange("p t (i q) n -> p q i t n", q=2)
                for par in range(2):
                    ins = dve.tensor_tensor(pcv[:, par, :, :, 0:N_CMP],
                                            sc[:, 4 * par:4 * par + 4, 0:N_CMP].rearrange("p (i t) n -> p i t n", i=2),
                                            cmul, ALU.mult)
                ins.then_inc(cp_sb, 1)
                dve.wait_ge(n_ps, g + 1)
                num = bank[7][:, 0:264].rearrange("p (t e) -> p t e", t=NT)
                chain(dve.tensor_copy(dn, num[:, :, 128]))
                chain(dve.scalar_tensor_tensor(out=ab, in0=dn, scalar=-1.0, in1=dn, op0=ALU.mult, op1=ALU.max))
                chain(dve.tensor_tensor(ab, ab, lst[:, 2:4], ALU.max))
                chain(dve.reciprocal(rd, ab))
                for t in range(NT):
                    ins = dve.tensor_scalar(hh[:, t, :], num[:, t, 0:128], rd[:, t:t + 1], None, ALU.mult)
                ins.then_inc(h_div, 1)
                head_max(n4, 2)
                dve.wait_ge(h_sq, g + 1)
                rsqrt(rd, ssM, ML_DH, 2)
                head_probs(n4, 2)
                head_max(n4, 3)
                for t in range(NT):
                    ins = dve.scalar_tensor_tensor(out=y1[:, t, :], in0=hh[:, t, :], scalar=rd[:, t:t + 1], in1=hgg,
                                                   op0=ALU.mult, op1=ALU.mult)
                    chain(ins)
                dve.scalar_tensor_tensor(out=y1, in0=so, scalar=1.0, in1=y1, op0=ALU.add, op1=ALU.mult).then_inc(ym_sb, 1)
                head_probs(n4, 3)
                chain.leave(GROUPS)

            dve.wait_ge(ynsa_done, 8)
            dve.wait_ge(yml_done, 4)
            dve.memset(nt_[:, 34:35], 0.0).then_inc(mg_free, 2)
            with dve.Fori(0, 4) as i:
                chain.enter(i, 6)
                for u in range(2):
                    m = i * 2 + u
                    dve.wait_ge(mg_th, m + 1)
                    dve.wait_ge(mp_ps, m + 1)
                    chain(dve.scalar_tensor_tensor(out=yG[:, u, 0:512], in0=thG[:, u, 0:512], scalar=1.0,
                                                   in1=bank[4 * u + 2], op0=ALU.add, op1=ALU.mult))
                    chain(dve.scalar_tensor_tensor(out=yG[:, u, 512:768], in0=thG[:, u, 512:768], scalar=1.0,
                                                   in1=bank[4 * u + 3][:, 0:T], op0=ALU.add, op1=ALU.mult))
                    chain(dve.tensor_tensor(yG[:, u, 0:T], yG[:, u, 0:T], yG[:, u, T:512], ALU.add))
                    dve.tensor_tensor(yT2[:, bass.ds(m, 1), :].rearrange("p a t -> p (a t)"), yG[:, u, 0:T],
                                      yG[:, u, 512:768], ALU.add).then_inc(mg_free, 1)
                chain.leave(4)

            def post(base):
                for t in range(NT):
                    dve.wait_ge(y_sq, 2 * base + t + 1)
                    c = 14 - 2 * base
                    rsqrt(rst[:, c + t:c + t + 1], stat[:, c + t:c + t + 1], D, 1)
                    chain(dve.scalar_tensor_tensor(out=ysF[:, t, :], in0=ysF[:, t, :], scalar=rst[:, c + t:c + t + 1],
                                                   in1=grows[:, 1 + base, :], op0=ALU.mult, op1=ALU.mult))
                    dve.tensor_tensor(x[:, t, :], x[:, t, :], ysF[:, t, :], ALU.add).then_inc(x4_done, 1)
                    if not base:
                        tile_normed(5, x, xF, t)

            post(0)
            gained(5, 4)

            def ff(s, par):
                for f in range(2):
                    b = bank[4 + 2 * par + f]
                    dve.wait_ge(ff_th, s * 2 + f + 1)
                    chain(dve.scalar_tensor_tensor(out=vF[:, par, f, :], in0=thF[:, par, f, :], scalar=1.0,
                                                   in1=b[:, 0:T], op0=ALU.add, op1=ALU.mult))
                    dve.scalar_tensor_tensor(out=hF[:, par, f, :], in0=vF[:, par, f, :], scalar=0.5, in1=b[:, T:2 * T],
                                             op0=ALU.mult, op1=ALU.mult).then_inc(ff_h, 1)

            ff(0, 0)
            ff(1, 1)
            with dve.Fori(0, 4) as i:
                chain.enter(i, 4)
                ff(i * 2 + 2, 0)
                ff(i * 2 + 3, 1)
                chain.leave(4)
            ff(10, 0)
            post(1)


_NAMES = ["x", "p", "norm_mix", "w_in", "w_pool", "pool_scale", "q_norm", "k_norm", "rpb", "w_out", "norm_ffn",
          "w_router", "w_gate", "w_up", "w_down", "norm_ple", "w_ple_gate", "w_ple_proj", "norm_ple_post", "mem_2",
          "g_pre_mix_2", "w_in_2", "cmp_pe_k_2", "cmp_w1_k_2", "cmp_w2_k_2", "cmp_pe_v_2", "cmp_w1_v_2",
          "cmp_w2_v_2", "ml_conv_w_2", "ml_conv_b_2", "ml_gate_b_2", "ml_head_g_2", "g_mem_2", "w_mem_kv_2",
          "w_proj_nsa_2", "w_proj_ml_2", "w_proj_mem_2", "w_out_2", "g_post_mix_2", "g_pre_ffn_2", "w_ffn_in_2",
          "w_ffn_down_2", "g_post_ffn_2"]


def laid_out(name, value):
    value = np.asarray(value)
    if name == "rpb":
        value = value[0].transpose(1, 0, 2)[..., ::-1]
    return np.ascontiguousarray(value)


def packed_vectors(inputs):
    v = np.zeros((P, NVEC + CMP_L + 2), np.float32)
    get = lambda n: np.asarray(inputs[n])[0]
    for c, n in enumerate(("norm_mix", "g_mem_2", "norm_ffn", "norm_ple", "g_pre_mix_2", "g_pre_ffn_2")):
        v[:, GAIN(c):GAIN(c) + 8] = get(n).reshape(8, P).T
    v[:, PSCALE:PSCALE + 4] = get("pool_scale").reshape(4, P).T
    taps, bias = get("ml_conv_w_2").reshape(4, 2, 4, P), get("ml_conv_b_2").reshape(2, 4, P)
    for m in range(2):
        for j in range(4):
            v[:, CONV + 5 * m + j:CONV + 40:10] = taps[j, m].T
        v[:, CONV + 5 * m + 4:CONV + 40:10] = bias[m].T
    for n, c in (("q_norm", QN), ("k_norm", KN)):
        v[0:HD, c] = v[HD:P, c] = get(n)
    v[0:HD, NVEC:NVEC + CMP_L] = get("cmp_pe_k_2").T
    v[HD:P, NVEC:NVEC + CMP_L] = get("cmp_pe_v_2").T
    v[0:4, NVEC + CMP_L:] = get("ml_gate_b_2").reshape(2, 4).T
    return v


def packed_weights(inputs):
    get = lambda n: np.asarray(inputs[n])[0]
    rows = lambda w: w.reshape(KC, P, -1).transpose(1, 0, 2).reshape(P, -1)
    w_in = get("w_in_2")
    gates = np.concatenate([w_in[:, GATE0:GATE0 + 48], w_in[:, IF0:IF0 + 8]], 1)
    return np.ascontiguousarray(np.concatenate([rows(get("w_router")), rows(gates), get("cmp_w2_k_2"),
                                                get("cmp_w2_v_2")], 1))


def kernel(**inputs):
    import concourse.bacc as _bacc
    from concourse.bass_utils import run_bass_kernel_spmd as _run

    nc = _bacc.Bacc("TRN2", target_bir_lowering=False, num_devices=1)
    arrays, aps = {}, {}
    masks, pool = constants()
    packed = [("vecs", packed_vectors(inputs)), ("small", packed_weights(inputs))]
    for name, value in [(n, laid_out(n, inputs[n])) for n in _NAMES] + packed + [("consts", masks), ("pool", pool)]:
        arrays[f"in_{name}"] = value
        aps[name] = nc.dram_tensor(f"in_{name}", value.shape, mybir.dt.from_np(value.dtype), kind="ExternalInput").ap()
    out = nc.dram_tensor("out_0", (1, T, D), F32, kind="ExternalOutput").ap()
    two_blocks(nc, aps, out)
    r = _run(nc, [arrays], core_ids=[0])
    return r.results[0]["out_0"]
```

```python
from contextlib import ExitStack

import numpy as np
import concourse.bass as bass
from concourse import mybir

F32 = mybir.dt.float32
I32 = mybir.dt.int32
ALU = mybir.AluOpType
ACT = mybir.ActivationFunctionType
AX = mybir.AxisListType.X

P = 128
T = 256
NT = T // P
D = 1024
KC = D // P
EPS = 1e-6
NEG = -1e30
SLOTS = 6
SLOT = 4096
RSQRT_SEED = float(0x5F3759DF)

PAIRS = 4
HD = 64
GRID_W, WIN_COLS, RPB_R, RPB_C = 64, 16, 15, 31
POOL_WINDOWS = (2, 4, 8, 16)
EXPERTS, CAP, DE = 16, 32, 2048
PARTS = (1, 5, 5, 5)
PLE = 256

GROUPS = 4
N_CMP, CMP_L, CMP_STRIDE = 15, 32, 16
ML_DH = 128
D_FF = 2816
FF_STEPS = D_FF // 256

Q0 = 0
KV0 = 1024
GATE0 = KV0 + 6 * 256
ML0 = GATE0 + 48
IF0 = ML0 + 3 * 512
O0 = IF0 + 8
MEMQ0 = O0 + 512
MERGE0 = MEMQ0 + 512

GAIN = lambda c: 8 * c
PSCALE = 48
CONV = 52
QN, KN = 92, 93
NVEC = 94
NSMALL = KC * (EXPERTS + 56) + 2 * HD

CONSTS = [("ident", 128), ("caus", 128), ("causTz", 256), ("wmask", 64), ("cmpadd", 32),
          ("cmpmul", 32), ("iota1", 32), ("ones", 128), ("eye4", 4)]
COFF = {}
_n = 0
for _name, _w in CONSTS:
    COFF[_name] = _n
    _n += _w
NCONST = _n


def constants():
    c = np.zeros((P, NCONST), np.float32)

    def put(name, a):
        a = np.asarray(a, np.float32)
        c[:a.shape[0], COFF[name]:COFF[name] + a.shape[1]] = a

    i = np.arange(P)
    put("ident", np.eye(P))
    put("caus", np.where(i[None, :] <= i[:, None], 0.0, NEG))
    put("causTz", np.concatenate([np.where(i[:, None] <= i[None, :], 0.0, NEG), np.zeros((P, P))], 1))
    col = i % GRID_W
    start = np.clip(col - WIN_COLS // 2, 0, GRID_W - WIN_COLS)
    kc = np.arange(GRID_W)
    put("wmask", np.where((kc[None] >= start[:, None]) & (kc[None] < start[:, None] + WIN_COLS), 0.0, NEG))
    t = np.arange(NT)[None, :, None] * P + i[:, None, None]
    n = np.arange(16)[None, None, :]
    seen = n * CMP_STRIDE + CMP_L - 1 <= t
    put("cmpadd", np.where(seen, 0.0, NEG).reshape(P, 32))
    put("cmpmul", np.where(seen, 1.0, 0.0).reshape(P, 32))
    put("iota1", np.tile(np.arange(1, CAP + 1), (P, 1)))
    put("ones", np.ones((P, P)))
    put("eye4", np.eye(4))
    pool = np.zeros((len(POOL_WINDOWS), T, T), np.float32)
    for g, w in enumerate(POOL_WINDOWS):
        for s in range(T):
            lo = min(max(s - w // 2, 0), T - 1)
            hi = min(max(s + (w - w // 2) - 1, 0), T - 1)
            pool[g, lo:hi + 1, s] += 1.0 / (hi - lo + 1)
            pool[g, s, s] -= 1.0
    return c, np.ascontiguousarray(pool.reshape(4, NT, P, T).transpose(2, 1, 0, 3).reshape(P, NT * 4 * T))


FIRST_SLOTS = [0, 1, 2, 3, 6, 8, 4, 5, 7, 0, 1, 2]


def around(rot):
    return [(n + rot) % SLOTS for n in range(12)]


class Chain:

    def __init__(self, eng, sem):
        self.eng, self.sem, self.base, self.n = eng, sem, 0, 0

    def __call__(self, ins):
        ins.then_inc(self.sem, 1)
        self.n += 1
        self.eng.wait_ge(self.sem, self.base + self.n)

    def enter(self, i, per):
        self.before, self.per = self.n, per
        self.base, self.n = i * per + self.before, 0

    def leave(self, times):
        assert self.n == self.per, (self.n, self.per)
        self.base, self.n = 0, self.before + times * self.per


class Ring:

    def __init__(self, eng, full, free):
        self.eng, self.full, self.free = eng, full, free
        self.rounds, self.incs = [0] * len(full), [0] * len(full)

    def load(self, slot, *copies):
        r = self.rounds[slot]
        if not (isinstance(r, int) and r == 0):
            self.eng.wait_ge(self.free[slot], r)
            if not isinstance(r, int):
                self.eng.nop(nofuse=True)
        for dst, src in copies:
            self.eng.dma_start(dst, src).then_inc(self.full[slot], 16)
        self.count(slot, len(copies))

    def count(self, slot, copies):
        self.rounds[slot] = self.rounds[slot] + 1
        self.incs[slot] = self.incs[slot] + 16 * copies

    def arrived(self, slot, copies):
        self.count(slot, copies)
        self.eng.wait_ge(self.full[slot], self.incs[slot])

    def enter(self, i, per):
        self.before, self.per = (list(self.rounds), list(self.incs)), per
        for s, (loads, copies) in per.items():
            self.rounds[s] = i * loads + self.rounds[s]
            self.incs[s] = i * (16 * copies) + self.incs[s]

    def leave(self, times):
        self.rounds, self.incs = list(self.before[0]), list(self.before[1])
        for s, (loads, copies) in self.per.items():
            self.rounds[s] += times * loads
            self.incs[s] += 16 * times * copies


def two_blocks(nc, a, out):
    ctx = ExitStack()
    with ctx:
        def sb(name, n, parts=P):
            return ctx.enter_context(nc.sbuf_tensor(name, [parts, n], F32))

        def sem(name):
            return ctx.enter_context(nc.semaphore(name))

        ring = sb("ring", SLOTS * SLOT)
        slot = [ring[:, s * SLOT:(s + 1) * SLOT] for s in range(SLOTS)]
        strip = [s.rearrange("p (k n) -> p k n", k=KC) for s in slot]
        x = sb("x", NT * D)[:, :].rearrange("p (t d) -> p t d", t=NT)
        xn = sb("xn", NT * D)[:, :].rearrange("p (t d) -> p t d", t=NT)
        turned_T = sb("turned_T", 2 * KC * T)
        hT = turned_T[:, 0:KC * T].rearrange("p (k t) -> p k t", k=KC)
        yT = turned_T[:, KC * T:].rearrange("p (k t) -> p k t", k=KC)
        later = sb("later", SLOT)
        yml = later[:, 0:1024].rearrange("p (k t) -> p k t", k=4)
        ymem = later[:, 1024:2048].rearrange("p (k t) -> p k t", k=4)
        kTm = later[:, 2048:3072]
        vm = later[:, 3072:4096].rearrange("p (t n) -> p t n", t=NT)
        gains = sb("gains", SLOT)
        grows = gains[:, 0:3 * D].rearrange("p (c d) -> p c d", c=3)
        hgrow = gains[:, 3 * D:3 * D + 512]
        slot += [later[:, :], turned_T[:, :], gains[:, :]]
        consts = sb("consts", NCONST)
        vecs = sb("vecs", NVEC + CMP_L + 2)
        vec = vecs[:, 0:NVEC]
        peT = vecs[:, NVEC:NVEC + CMP_L]
        ifb = vecs[:, NVEC + CMP_L:NVEC + CMP_L + 2]
        small = sb("small", NSMALL)
        wr = small[:, 0:128].rearrange("p (k e) -> p k e", k=KC)
        wsm = small[:, 128:576].rearrange("p (k e) -> p k e", k=KC)
        w2 = small[:, 576:704]
        sq = sb("sq", 24 + 2 + 8)
        stat = sb("stat", 16)
        rst = sb("rst", 16)
        nt_ = sb("nt_", 40)
        scr = sb("scr", 10420)

        class Area:

            def __init__(self, at=0):
                self.at = at

            def __call__(self, n, pat=None, parts=P, **kw):
                v = scr[0:parts, self.at:self.at + n]
                self.at += n
                assert self.at <= 10420, self.at
                return v.rearrange(pat, **kw) if pat else v

        def const(name, parts=P):
            w = dict(CONSTS)[name]
            return consts[0:parts, COFF[name]:COFF[name] + w]

        ident, caus, causTz = const("ident"), const("caus"), const("causTz")
        causT = causTz[:, 0:P]

        ps = ctx.enter_context(nc.psum_tensor("ps", [P, 8, 512], F32))
        bank = [ps[:, b, :] for b in range(8)]

        A = Area()
        poolm = A(NT * 4 * T, "p (t g s) -> p t g s", t=NT, g=4)
        mx = A(NT * D, "p (t d) -> p t d", t=NT)
        zA = A(NT * 512, "p (t n) -> p t n", t=NT)
        sqA = A(NT * T, "p (t n) -> p t n", t=NT)
        qkn = A(NT * T, "p (t n) -> p t n", t=NT)
        qkT = A(2 * T, "p (m t) -> p m t", m=2)
        sA = A(2 * NT * T, "p (a t k) -> p a t k", a=2, t=NT)
        PTA = A(2 * NT * T, "p (a k q) -> p a k q", a=2, k=NT)
        dT = A(T)
        junk = A(D)
        wp = A(P)
        ssA, rsA, nmA, sumA, rcA = A(8), A(8), A(4), A(4), A(4)
        braw = slot[5][:, 0:6 * 8 * GRID_W].rearrange("p (r h c) -> p h r c", h=8, r=6)
        btab = grows.rearrange("p c d -> p (c d)").rearrange("p (h r c) -> p h r c", h=8, r=6)

        B = Area(at=NT * 4 * T + NT * D)
        lgE = B(32, "p (t e) -> p t e", t=NT)
        nmE, smE = B(2), B(2)
        affT, selT, cumT, onesT = (B(T, parts=EXPERTS) for _ in range(4))
        m8 = B(8, parts=EXPERTS)
        posT = B(32, "p (t e) -> p t e", t=NT)
        selall = B(EXPERTS * 128, "p (e t w s) -> p e t w s", e=EXPERTS, t=NT, w=2)
        selflat = scr[:, B.at - EXPERTS * 128:B.at]
        gT = B(T)
        ysb = B(D)
        pin = B(NT * PLE, "p (t n) -> p t n", t=NT)
        pT = B(2 * T, "p (k t) -> p k t", k=2)
        B = Area()
        sele = B(128, "p (t w s) -> p t w s", t=NT, w=2)
        sele_flat = scr[:, 0:128]
        xeT = B(KC * CAP, "p (k s) -> p k s", k=KC)
        thE = B(512)
        hE = B(512)
        hTe = B(512, "p (c n) -> p c n", c=4)
        assert B.at <= NT * 4 * T

        uP = mx
        C = Area(at=NT * 4 * T + NT * D)
        thP = C(NT * D, "p (t d) -> p t d", t=NT)

        E = Area()
        gball = E(96)
        stall = E(16)
        kcall = E(4 * 16)
        vcall = E(4 * HD)
        negMd = E(4 * T, parts=4)
        gst, lst, cst, kcg, vcg = E(24), E(4), E(10), E(16), E(HD)
        vmg = E(NT * P, "p (t d) -> p t d", t=NT)
        hgg = E(P)
        zp = E(2 * 259, "p (m t) -> p m t", m=2)
        v1 = E(NT * 132, "p (t e) -> p t e", t=NT)
        Pc = E(NT * 4 * 32, "p (t i n) -> p t i n", t=NT, i=4)
        loop_at = E.at
        qs = E(2 * T, "p (m t) -> p m t", m=2)
        kxy = E(2 * T, "p (m t) -> p m t", m=2)
        vsb = E(NT * P, "p (t d) -> p t d", t=NT)
        yc = E(2 * T, "p (m t) -> p m t", m=2)
        thc = E(2 * T, "p (m t) -> p m t", m=2)
        so = E(NT * P, "p (t d) -> p t d", t=NT)
        tm = E(384)
        Wm = E(384)
        hh = E(NT * P, "p (t d) -> p t d", t=NT)
        y1 = E(NT * P, "p (t d) -> p t d", t=NT)
        qm = E(T)
        Pm = E(NT * T, "p (t k) -> p t k", t=NT)
        PTm = E(NT * T, "p (k q) -> p k q", k=NT)
        sc = E(8 * 16, "p (j n) -> p j n", j=8)
        PTc = E(T)
        Pn = xn.rearrange("p t d -> p (t d)")[:, 0:1536].rearrange("p (a b n) -> p a b n", a=2, b=2)
        PTn = E(2 * 384, "p (b n) -> p b n", b=2)
        nmC, smC, rcC = E(8), E(8), E(8)
        nmN, smN, rcN = (E(8, "p (a b t) -> p a b t", a=2, b=2) for _ in range(3))
        nmM, smM, rcM, dn, ab, rd, ssM = (E(2) for _ in range(7))
        E2 = Area(at=loop_at)
        kvc = E2(5 * T, "p (g t) -> p g t", g=5)
        hidb = E2(2)
        hpre = E2(2 * 60, "p (m n) -> p m n", m=2)
        hth = E2(2 * 60, "p (m n) -> p m n", m=2)
        hidk = E2(60)
        hidv = E2(4 * 32, "p (g n) -> p g n", g=4)
        gth = E2(NT * 48, "p (t n) -> p t n", t=NT)
        ifT = E2(NT * 8, "p (t n) -> p t n", t=NT)
        iR, fR, mnR, abR, lnR, BR, aR, MR, mR, emR, nMR = (E2(T, parts=4) for _ in range(11))
        G = Area(at=0)
        thG = G(2 * 768, "p (u n) -> p u n", u=2)
        yG = G(2 * 768, "p (u n) -> p u n", u=2)
        yT2 = xn.rearrange("p t d -> p (t d)").rearrange("p (k t) -> p k t", k=KC)
        thF = G(4 * T, "p (u f t) -> p u f t", u=2, f=2)
        vF = G(4 * T, "p (u f t) -> p u f t", u=2, f=2)
        hF = G(4 * T, "p (u f t) -> p u f t", u=2, f=2)
        ysF = G(NT * D, "p (t d) -> p t d", t=NT)
        xF = Area(at=0)(NT * D, "p (t d) -> p t d", t=NT)

        full = [sem(f"slot{s}_full") for s in range(SLOTS + 3)]
        free = [sem(f"slot{s}_free") for s in range(SLOTS)]
        in_x, in_x1, in_consts, in_pool, in_bias, in_mem, in_p, in_wp = (
            sem(n) for n in ("in_x", "in_x1", "in_consts", "in_pool", "in_bias", "in_mem",
                             "in_p", "in_wp"))
        out_done = sem("out_done")
        dve_chain, act_chain, pool_chain = sem("dve_chain"), sem("act_chain"), sem("pool_chain")
        exp_warm = sem("exp_warm")
        bias_sb, in_rows = sem("bias_sb"), sem("in_rows")
        ssq_done, xn_done, tr_done, hT_done = sem("ssq_done"), sem("xn_done"), sem("tr_done"), sem("hT_done")
        zA_ps, zA_sb, qknA, qkT_ps, qkT_sb, poolA_ps, dT_sb, poolY_ps, yA_pool = (
            sem(n) for n in ("zA_ps", "zA_sb", "qknA", "qkT_ps", "qkT_sb", "poolA_ps", "dT_sb", "poolY_ps", "yA_pool"))
        sA_ps, maxA, expA, pA, ptA_ps, ptA_sb, oA_ps, yA_attn, wp_used = (
            sem(n) for n in ("sA_ps", "maxA", "expA", "pA", "ptA_ps", "ptA_sb", "oA_ps", "yA_attn", "wp_used"))
        vA_sb = sem("vA_sb")
        out1_ps, x1_done, mkv_ps, mkv_sb = sem("out1_ps"), sem("x1_done"), sem("mkv_ps"), sem("mkv_sb")
        lg_ps, lg_max, lg_exp, aff_sb, aff_ps, pos_sb, pos_ps, sel_done = (
            sem(n) for n in ("lg_ps", "lg_max", "lg_exp", "aff_sb", "aff_ps", "pos_sb", "pos_ps", "sel_done"))
        sele_sb, xe_ps, xe_sb, gt_ps, gt_sb, gate_ps, up_ps, gate_th, h_sb, ht_ps, ht_sb, y_ps, y_sb, sc_ps, x_acc = (
            sem(n) for n in ("sele_sb", "xe_ps", "xe_sb", "gt_ps", "gt_sb", "gate_ps", "up_ps", "gate_th", "h_sb",
                             "ht_ps", "ht_sb", "y_ps", "y_sb", "sc_ps", "x_acc"))
        pT_ps, pT_sb, g_ps, g_th, e_ps, e_sb, e_sq, x3_done = (
            sem(n) for n in ("pT_ps", "pT_sb", "g_ps", "g_th", "e_ps", "e_sb", "e_sq", "x3_done"))
        pe_sb, ga_ps, if_ps, ga_th, ga_sb, ab_sb, ab_ln, em_in, em_sb, st_sb, st_ps = (
            sem(n) for n in ("pe_sb", "ga_ps", "if_ps", "ga_th", "ga_sb", "ab_sb", "ab_ln", "em_in", "em_sb",
                             "st_sb", "st_ps"))
        kvc_ps, kvc_sb, hid_ps, hid_pre, hid_th, hid_sb, kc_ps, kc_sb = (
            sem(n) for n in ("kvc_ps", "kvc_sb", "hid_ps", "hid_pre", "hid_th", "hid_sb", "kc_ps", "kc_sb"))
        staged, proj_ps, proj_sb, c_conv, c_th, c_qk, d_ps, d_in, d_exp, w_sb, n_ps, h_div, h_sq, ym_sb, ym_ps = (
            sem(n) for n in ("staged", "proj_ps", "proj_sb", "c_conv", "c_th", "c_qk", "d_ps", "d_in", "d_exp",
                             "w_sb", "n_ps", "h_div", "h_sq", "ym_sb", "ym_ps"))
        xs_ps, xs_max, xs_exp, xp_sb, xt_ps, xt_sb, xo_ps, ymem_done, yml_done, ynsa_done = (
            sem(n) for n in ("xs_ps", "xs_max", "xs_exp", "xp_sb", "xt_ps", "xt_sb", "xo_ps", "ymem_done",
                             "yml_done", "ynsa_done"))
        kx_swap = sem("kx_swap")
        cs_ps, cs_in, cs_exp, cp_sb, ct_ps, ct_sb, ns_ps, ns_max, ns_exp, np_sb, nt_ps, nt_sb, no_ps = (
            sem(n) for n in ("cs_ps", "cs_in", "cs_exp", "cp_sb", "ct_ps", "ct_sb", "ns_ps", "ns_max", "ns_exp",
                             "np_sb", "nt_ps", "nt_sb", "no_ps"))
        mg_ps, mp_ps, mg_th, mg_free, out2_ps, y_sq, x4_done = (
            sem(n) for n in ("mg_ps", "mp_ps", "mg_th", "mg_free", "out2_ps", "y_sq", "x4_done"))
        ff_ps, ff_th, ff_h, ffo_ps = sem("ff_ps"), sem("ff_th"), sem("ff_h"), sem("ffo_ps")

        TURNS = {0: 0, 2: 1, 1: 2, 3: 3, 4: 4, 5: 5}
        block = ctx.enter_context(nc.Block())

        def chunks(w):
            return w.rearrange("(k p) n -> p k n", p=P)

        @block.sync
        def _(sp):
            r = Ring(sp, full, free)
            w_in1, w_in2 = a["w_in"][0], a["w_in_2"][0]

            def pair_strip(j, s):
                src = w_in1.rearrange("(k p) (m n) -> p k m n", p=P, m=4)
                dst = strip[s].rearrange("p k (m n) -> p k m n", m=4)
                return [(dst[:, :, m, :], src[:, :, m, bass.ds(j * 128, 128)]) for m in range(4)]

            def halves(s, w, c0):
                src = chunks(w)
                return [(strip[s][:, h:h + 4, :], src[:, h:h + 4, c0:c0 + 512]) for h in (0, 4)]

            for t in range(NT):
                sp.dma_start(x[:, t, :], a["x"][0][t * P:(t + 1) * P, :]).then_inc((in_x, in_x1)[t], 16)
            for j in range(PAIRS):
                r.load(j, *pair_strip(j, j))
            r.load(4, *halves(4, a["w_out"][0], 0))
            r.count(5, 0)
            r.load(5, *halves(5, a["w_out"][0], 512))

            wide = [s.rearrange("p (k n) -> p k n", k=2) for s in slot]
            tall = [s.rearrange("p (k n) -> p k n", k=4) for s in slot]
            gate = a["w_gate"][0].rearrange("e k f -> (e k) f")
            up = a["w_up"][0].rearrange("e k f -> (e k) f")
            down = a["w_down"][0].rearrange("e k f -> (e k) f")

            def expert(e, slots):
                for n in range(8):
                    w, i, s = (gate, up)[n // 4], n % 4, slots[n]
                    if s == 8:
                        sp.wait_ge(maxA, 2 * PAIRS)
                    src = w[bass.ds(e * D + i * 256, 256), :].rearrange("(k p) f -> p k f", p=P)
                    r.load(s, (wide[s], src))
                for n in range(8, 12):
                    i, s = n - 8, slots[n]
                    if s == 7:
                        sp.wait_ge(lg_ps, 1)
                    src = down[bass.ds(e * DE + i * 512, 512), :].rearrange("(k p) f -> p k f", p=P)
                    r.load(s, (tall[s], src))

            def experts(part, rot):
                with sp.Fori(0, PARTS[part]) as i:
                    r.enter(i, {s: (2, 2) for s in range(SLOTS)})
                    expert(i + sum(PARTS[:part]), around(rot))
                    r.leave(PARTS[part])

            expert(0, FIRST_SLOTS)
            experts(1, 3)
            r.load(3, (slot[3][:, 0:2 * D].rearrange("p (k n) -> p k n", k=2), chunks(a["w_ple_proj"][0])))
            r.load(4, *halves(4, a["w_mem_kv_2"][0], 0))
            experts(2, 5)
            r.load(2, *halves(2, a["w_mem_kv_2"][0], 512))
            experts(3, 3)

            r.load(3, *halves(3, a["w_ple_gate"][0], 0))
            r.load(4, *halves(4, a["w_ple_gate"][0], 512))
            r.load(5, *halves(5, w_in2, KV0))
            r.load(2, *[(slot[2][h * HD:h * HD + HD, :].rearrange("p (l h) -> p l h", l=CMP_L),
                         a[n][0].rearrange("l d h -> d l h")) for h, n in enumerate(("cmp_w1_k_2", "cmp_w1_v_2"))])
            w2c = chunks(w_in2)
            kv = w_in2[:, KV0:KV0 + 1536].rearrange("(k p) (s n) -> p k s n", p=P, s=6)
            ml = w_in2[:, ML0:ML0 + 1536].rearrange("(k p) (s n) -> p k s n", p=P, s=3)
            kvd = strip[5][:, :, 256:512].rearrange("p k (s n) -> p k s n", s=4)
            mld = strip[0][:, :, 0:384].rearrange("p k (s n) -> p k s n", s=3)
            with sp.Fori(0, GROUPS) as g:
                r.enter(g, {0: (1, 4), 1: (1, 1), 5: (1, 5)})
                r.load(0, *[(mld[:, :, s, :], ml[:, :, s, bass.ds(g * 128, 128)]) for s in range(3)],
                       (strip[0][:, :, 384:512], w2c[:, :, bass.ds(g * 128 + O0, 128)]))
                r.load(5, (strip[5][:, :, 0:256], w2c[:, :, bass.ds(g * 256, 256)]),
                       *[(kvd[:, :, n, :], kv[:, :, s, bass.ds(g * HD, HD)]) for n, s in enumerate((2, 4, 3, 5))])
                r.load(1, (slot[1][:, 0:D].rearrange("p (k n) -> p k n", k=KC),
                           w2c[:, :, bass.ds(g * 128 + MEMQ0, 128)]))
                r.leave(GROUPS)
            gm = w_in2[:, MERGE0:MERGE0 + 3 * D].rearrange("(k p) (b n) -> p k b n", p=P, b=3)
            pn, pl, pe_ = (chunks(a[n][0]) for n in ("w_proj_nsa_2", "w_proj_ml_2", "w_proj_mem_2"))
            with sp.Fori(0, 4) as i:
                r.enter(i, {s: (1, 3) for s in (2, 3, 4, 5)})
                for u in range(2):
                    c = bass.ds(i * 256 + u * 128, 128)
                    gd = slot[2 + 2 * u][:, 0:3072].rearrange("p (k b n) -> p k b n", k=KC, b=3)
                    pd = slot[3 + 2 * u][:, 0:2048].rearrange("p (k n) -> p k n", k=16)
                    r.load(2 + 2 * u, *[(gd[:, :, b, :], gm[:, :, b, c]) for b in range(3)])
                    r.load(3 + 2 * u, (pd[:, 0:8, :], pn[:, :, c]), (pd[:, 8:12, :], pl[:, :, c]),
                           (pd[:, 12:16, :], pe_[:, :, c]))
                r.leave(4)
            r.load(0, *halves(0, a["w_out_2"][0], 0))
            r.load(1, *halves(1, a["w_out_2"][0], 512))
            gu = a["w_ffn_in_2"][0].rearrange("(k p) (m n) -> p k m n", p=P, m=2)
            dn_ = a["w_ffn_down_2"][0]

            def ff(s, par):
                A_ = strip[2 + 2 * par].rearrange("p k (m n) -> p k m n", m=2)
                B_ = slot[3 + 2 * par][:, 0:2 * D].rearrange("p (k n) -> p k n", k=2)
                r.load(2 + 2 * par, *[(A_[:, :, m, :], gu[:, :, m, bass.ds(s * 256, 256)]) for m in range(2)])
                r.load(3 + 2 * par, (B_, chunks(dn_[bass.ds(s * 256, 256), :])))

            ff(0, 0)
            ff(1, 1)
            with sp.Fori(0, 4) as i:
                r.enter(i, {2: (1, 2), 3: (1, 1), 4: (1, 2), 5: (1, 1)})
                ff(i * 2 + 2, 0)
                ff(i * 2 + 3, 1)
                r.leave(4)
            ff(10, 0)
            for t in range(NT):
                for h in range(2):
                    sp.wait_ge(x4_done, 4 + 2 * t + h + 1)
                    sp.dma_start(out[0][t * P:(t + 1) * P, h * 512:(h + 1) * 512], x[:, t, h * 512:(h + 1) * 512])\
                      .then_inc(out_done, 16)
            sp.wait_ge(out_done, 16 * 2 * NT)

        @block.gpsimd
        def _(g_):
            g_.dma_start(wp, a["w_pool"][0, 0]).then_inc(in_wp, 16)
            g_.dma_start(poolm[:, :, :, :], a["pool"].rearrange("p (t g s) -> p t g s", t=NT, g=4)).then_inc(in_pool, 16)
            g_.wait_ge(qknA, 1)
            g_.dma_start(mx[:, :, :], a["mem_2"][0].rearrange("(t p) d -> p t d", p=P)).then_inc(in_mem, 16)
            g_.dma_start(small[:, :], a["small"]).then_inc(in_mem, 16)
            for j in range(1, PAIRS):
                g_.wait_ge(wp_used, j)
                g_.dma_start(wp, a["w_pool"][0, j]).then_inc(in_wp, 16)
            g_.wait_ge(sel_done, 2)
            g_.tensor_copy(sele_flat, selflat[:, 0:128]).then_inc(sele_sb, 1)
            g_.wait_ge(gt_ps, 1)
            g_.wait_ge(sel_done, 4)
            with g_.Fori(0, EXPERTS - 1) as i:
                g_.tensor_copy(sele_flat, selflat[:, bass.ds(i * 128 + 128, 128)]).then_inc(sele_sb, 1)
                g_.wait_ge(gt_ps, i + 2)
            g_.wait_ge(in_rows, 16 * 4)
            g_.wait_ge(st_sb, 2)
            g_.wait_ge(ga_sb, 1)
            g_.wait_ge(kc_sb, 2)
            with g_.Fori(0, GROUPS) as g:
                for dst, src, n in ((cst, vec[:, CONV:CONV + 40], 10), (lst, stall, 4), (hgg, hgrow, P),
                                    (kcg, kcall, 16), (vcg, vcall, HD), (gst, gball, 24)):
                    g_.tensor_copy(dst, src[:, bass.ds(g * n, n)]).then_inc(staged, 1)
                g_.tensor_copy(vmg, vm[:, :, bass.ds(g * P, P)]).then_inc(staged, 1)
                g_.wait_ge(ynsa_done, g * 2 + 2)
                g_.wait_ge(yml_done, g + 1)
                g_.wait_ge(ymem_done, g + 1)

        @block.scalar
        def _(act):
            chain = Chain(act, act_chain)
            act.dma_start(consts[:, :], a["consts"]).then_inc(in_consts, 16)
            act.dma_start(vecs[:, :], a["vecs"]).then_inc(in_consts, 16)

            def bias_rows(half):
                src = bass.AP(a["rpb"].tensor, (5 - half) * 8 * RPB_C + WIN_COLS - GRID_W,
                              [[1, GRID_W], [RPB_C, 6 * 8], [1, GRID_W]])
                act.dma_start(slot[5][half * 64:half * 64 + 64, 0:6 * 8 * GRID_W].rearrange("p (n c) -> p n c", n=48), src)\
                   .then_inc(in_bias, 16)

            act.wait_ge(exp_warm, 1)
            act.activation(nt_[:, 33:34], nt_[:, 32:33], ACT.Exp)

            def half_squares(c, src, t, h):
                n = 4 * c + 2 * t + h
                if n > 1:
                    act.wait_ge(ssq_done, n - 1)
                act.activation(junk[:, h * 512:(h + 1) * 512], src[:, t, h * 512:(h + 1) * 512], ACT.Square,
                               accum_out=sq[:, n:n + 1]).then_inc(ssq_done, 1)

            for t in range(NT):
                act.wait_ge((in_x, in_x1)[t], 16)
                for h in range(2):
                    half_squares(0, x, t, h)

            def projected(j):
                for t in range(NT):
                    act.wait_ge(zA_ps, j * 2 + t + 1)
                    act.activation(zA[:, t, 0:384], bank[t][:, 0:384], ACT.Copy).then_inc(zA_sb, 1)

            def projected_v(j):
                act.activation(zA[:, :, 384:512], ps[:, 0:2, 384:512], ACT.Copy).then_inc(vA_sb, 1)

            def pair(j, more):
                act.wait_ge(poolA_ps, j + 1)
                act.activation(dT, bank[3][:, 0:T], ACT.Copy).then_inc(dT_sb, 1)
                for h in range(2):
                    act.wait_ge(maxA, j * 2 + h + 1)
                    for t in range(NT):
                        e = act.activation(sA[:, h, t, :], sA[:, h, t, :], ACT.Exp,
                                           bias=nmA[:, 2 * h + t:2 * h + t + 1],
                                           accum_out=sumA[:, 2 * h + t:2 * h + t + 1])
                    e.then_inc(expA, 1)
                if more:
                    projected(j + 1)
                for h in range(2):
                    act.wait_ge(ptA_ps, j * 2 + h + 1)
                    act.activation(PTA[:, h, :, :], bank[6 + h].rearrange("p (k q) -> p k q", k=NT), ACT.Copy)\
                       .then_inc(ptA_sb, 1)
                act.wait_ge(oA_ps, j * 2 + 2)
                act.nop(nofuse=True)
                act.activation(yT[:, bass.ds(j + 4, 1), :].rearrange("p a t -> p (a t)"), bank[4][:, 0:T], ACT.Copy)\
                   .then_inc(yA_attn, 1)
                if more:
                    projected_v(j + 1)

            projected(0)
            projected_v(0)
            bias_rows(0)
            bias_rows(1)
            with act.Fori(0, PAIRS - 1) as j:
                pair(j, True)
            pair(PAIRS - 1, False)

            act.wait_ge(in_mem, 32)
            for t in range(NT):
                for h in range(2):
                    half_squares(1, mx, t, h)
            for t in range(NT):
                for h in range(2):
                    act.wait_ge(x1_done, 2 * t + h + 1)
                    half_squares(2, x, t, h)
            act.wait_ge(lg_max, 1)
            for t in range(NT):
                e = act.activation(lgE[:, t, :], bank[4][:, t * 16:t * 16 + 16], ACT.Exp, bias=nmE[:, t:t + 1],
                                   accum_out=smE[:, t:t + 1])
            e.then_inc(lg_exp, 1)

            act.wait_ge(ssq_done, 12)
            act.dma_start(pin[:, :, :], a["p"][0, 0].rearrange("(t p) d -> p t d", p=P)).then_inc(in_p, 16)

            def expert(e):
                act.wait_ge(gt_ps, e + 1)
                act.activation(gT, bank[2][:, 0:T], ACT.Copy).then_inc(gt_sb, 1)
                act.wait_ge(gate_ps, e + 1)
                act.activation(thE, bank[0], ACT.Tanh, scale=0.5).then_inc(gate_th, 1)
                act.wait_ge(ht_ps, e + 1)
                act.activation(hTe.rearrange("p c n -> p (c n)"), bank[2], ACT.Copy).then_inc(ht_sb, 1)
                act.wait_ge(y_ps, e + 1)
                act.activation(ysb[:, 0:512], bank[4], ACT.Copy).then_inc(y_sb, 1)
                act.wait_ge(sc_ps, e * 4 + 4)

            def experts(part):
                with act.Fori(0, PARTS[part]) as i:
                    expert(i + sum(PARTS[:part]))

            expert(0)
            for c, n in enumerate(("norm_ple_post", "g_post_mix_2", "g_post_ffn_2")):
                act.dma_start(grows[:, c, :], a[n][0].partition_broadcast(P)).then_inc(in_rows, 16)
            act.dma_start(hgrow, a["ml_head_g_2"][0].partition_broadcast(P)).then_inc(in_rows, 16)
            experts(1)
            act.wait_ge(pT_ps, 1)
            act.activation(pT.rearrange("p k t -> p (k t)"), bank[6], ACT.Copy).then_inc(pT_sb, 1)
            for b in range(4):
                act.wait_ge(e_ps, b + 1)
                act.activation(uP[:, b // 2, (b % 2) * 512:(b % 2) * 512 + 512], bank[4 + b], ACT.Copy)\
                   .then_inc(e_sb, 1)
            act.wait_ge(e_sb, 4)
            for t in range(NT):
                if t:
                    act.wait_ge(e_sq, t)
                act.activation(junk, uP[:, t, :], ACT.Square, accum_out=sq[:, 24 + t:25 + t]).then_inc(e_sq, 1)
            for b in range(2):
                act.wait_ge(mkv_ps, b + 1)
                act.activation(kTm[:, b * 512:(b + 1) * 512], bank[b], ACT.Copy).then_inc(mkv_sb, 1)
            experts(2)
            for b in range(2):
                act.wait_ge(mkv_ps, b + 3)
                act.activation(vm[:, b, :], bank[2 + b], ACT.Copy).then_inc(mkv_sb, 1)
            experts(3)

            act.wait_ge(e_sq, 2)
            for t in range(NT):
                for h in range(2):
                    act.wait_ge(x_acc, 4 * EXPERTS - 3 + 2 * t + h)
                    half_squares(3, x, t, h)
            for t in range(NT):
                for h in range(2):
                    act.wait_ge(g_ps, 2 * t + h + 1)
                    act.activation(thP[:, t, h * 512:(h + 1) * 512], bank[4 + 2 * t + h], ACT.Tanh, scale=0.5)\
                       .then_inc(g_th, 1)
                for h in range(2):
                    act.wait_ge(x3_done, 2 * t + h + 1)
                    half_squares(4, x, t, h)

            act.wait_ge(ga_ps, 1)
            gates = bank[4][:, 0:2 * 56].rearrange("p (t n) -> p t n", t=NT)
            act.activation(ifT, gates[:, :, 48:56], ACT.Copy).then_inc(ga_th, 1)
            act.activation(gth, gates[:, :, 0:48], ACT.Tanh, scale=0.5).then_inc(ga_th, 1)
            act.wait_ge(ab_sb, 1)
            chain(act.activation(lnR, abR, ACT.Exp, scale=-1.0))
            act.activation(lnR, lnR, ACT.Ln, bias=1.0).then_inc(ab_ln, 1)
            for b in range(2):
                act.wait_ge(kvc_ps, b + 1)
                act.activation(kvc[:, 2 * b:2 * b + 2, :], bank[6 + b].rearrange("p (g t) -> p g t", g=2), ACT.Copy)\
                   .then_inc(kvc_sb, 1)
            act.wait_ge(em_in, 1)
            act.activation(emR, mR, ACT.Exp, scale=-1.0).then_inc(em_sb, 1)
            act.wait_ge(hid_pre, 1)
            act.activation(hth, hpre, ACT.Tanh, scale=0.5).then_inc(hid_th, 1)

            def heads_exp(n, i):
                act.wait_ge(ns_max, n + i + 1)
                o = i % 2
                for b in range(2):
                    for t, c in ((0, slice(0, 128)), (1, slice(128, 384))):
                        e = act.activation(Pn[:, o, b, c], bank[2 * o + b][:, c], ACT.Exp,
                                           bias=nmN[:, o, b, t:t + 1], accum_out=smN[:, o, b, t:t + 1])
                e.then_inc(ns_exp, 1)

            def heads_turned(n, i):
                act.wait_ge(nt_ps, n + i + 1)
                act.activation(PTn, ps[:, 4:6, 0:384], ACT.Copy).then_inc(nt_sb, 1)

            def nsa_out(n, g, pair):
                act.wait_ge(no_ps, n + 2 * pair + 2)
                act.nop(nofuse=True)
                act.activation(yT[:, bass.ds(g * 2 + pair, 1), :].rearrange("p a t -> p (a t)"),
                               bank[6 + pair][:, 0:T], ACT.Copy).then_inc(ynsa_done, 1)

            with act.Fori(0, GROUPS) as g:
                n4 = g * 4
                act.wait_ge(proj_ps, g * 6 + 1)
                act.activation(zp[:, :, 3:259], bank[5].rearrange("p (m t) -> p m t", m=2), ACT.Copy)\
                   .then_inc(proj_sb, 1)
                act.wait_ge(c_conv, g + 1)
                act.activation(thc, yc, ACT.Tanh, scale=0.5).then_inc(c_th, 1)
                act.wait_ge(proj_ps, g * 6 + 2)
                act.activation(qs, bank[0].rearrange("p (m t) -> p m t", m=2), ACT.Copy, scale=HD ** -0.5)\
                   .then_inc(proj_sb, 1)
                act.wait_ge(proj_ps, g * 6 + 3)
                act.activation(kxy[:, 0, :], bank[1][:, 0:T], ACT.Copy).then_inc(proj_sb, 1)
                act.wait_ge(proj_sb, g * 7 + 3)
                act.nop(nofuse=True)
                act.dma_start(kxy[0:64, 1, :], kxy[64:128, 0, :]).then_inc(kx_swap, 16)
                act.dma_start(kxy[64:128, 1, :], kxy[0:64, 0, :]).then_inc(kx_swap, 16)
                act.wait_ge(staged, g * 7 + 7)
                act.wait_ge(d_in, g + 1)
                act.activation(tm[:, 0:256], tm[:, 0:256], ACT.Exp, bias=lst[:, 0:1])
                act.activation(tm[:, 256:384], tm[:, 256:384], ACT.Exp, bias=lst[:, 1:2]).then_inc(d_exp, 1)
                act.wait_ge(proj_ps, g * 6 + 4)
                vo = bank[4].rearrange("p (t n) -> p t n", t=NT)
                act.activation(v1[:, :, 0:128], vo[:, :, 0:128], ACT.Copy).then_inc(proj_sb, 1)
                act.activation(so, vo[:, :, 128:256], ACT.Tanh, scale=0.5).then_inc(proj_sb, 1)
                heads_exp(n4, 0)
                act.wait_ge(proj_ps, g * 6 + 5)
                act.activation(qm, bank[7][:, 0:T], ACT.Copy, scale=ML_DH ** -0.5).then_inc(proj_sb, 1)
                heads_exp(n4, 1)
                act.wait_ge(xs_max, g + 1)
                for t in range(NT):
                    e = act.activation(Pm[:, t, :], bank[4][:, t * T:t * T + T], ACT.Exp, bias=nmM[:, t:t + 1],
                                       accum_out=smM[:, t:t + 1])
                e.then_inc(xs_exp, 1)
                act.wait_ge(cs_in, g + 1)
                act.activation(sc[:, :, 0:N_CMP], sc[:, :, 0:N_CMP], ACT.Exp).then_inc(cs_exp, 1)
                act.wait_ge(proj_ps, g * 6 + 6)
                act.activation(vsb, bank[5][:, 0:256].rearrange("p (t n) -> p t n", t=NT), ACT.Copy)\
                   .then_inc(proj_sb, 1)
                act.wait_ge(ct_ps, g + 1)
                act.activation(PTc, bank[6][:, T:2 * T], ACT.Copy).then_inc(ct_sb, 1)
                act.wait_ge(h_div, g + 1)
                for t in range(NT):
                    e = act.activation(y1[:, t, :], hh[:, t, :], ACT.Square, accum_out=ssM[:, t:t + 1])
                e.then_inc(h_sq, 1)
                heads_turned(n4, 0)
                heads_exp(n4, 2)
                heads_turned(n4, 1)
                act.wait_ge(xt_ps, g + 1)
                act.activation(PTm, bank[7].rearrange("p (k q) -> p k q", k=NT), ACT.Copy).then_inc(xt_sb, 1)
                nsa_out(n4, g, 0)
                heads_turned(n4, 2)
                heads_exp(n4, 3)
                act.wait_ge(xo_ps, g + 1)
                act.nop(nofuse=True)
                act.activation(ymem[:, bass.ds(g, 1), :].rearrange("p a t -> p (a t)"), bank[0][:, 0:T], ACT.Copy)\
                   .then_inc(ymem_done, 1)
                heads_turned(n4, 3)
                act.wait_ge(ym_ps, g + 1)
                act.nop(nofuse=True)
                act.activation(yml[:, bass.ds(g, 1), :].rearrange("p a t -> p (a t)"), bank[2][:, 0:T], ACT.Copy,
                               scale=0.5).then_inc(yml_done, 1)
                nsa_out(n4, g, 1)

            with act.Fori(0, 4) as i:
                for u in range(2):
                    m = i * 2 + u
                    act.wait_ge(mg_free, m + 1)
                    act.wait_ge(mg_ps, m + 1)
                    act.activation(thG[:, u, 0:512], bank[4 * u], ACT.Tanh, scale=0.5)
                    act.activation(thG[:, u, 512:768], bank[4 * u + 1][:, 0:T], ACT.Tanh, scale=0.5)\
                       .then_inc(mg_th, 1)

            def post(base, scale):
                for t in range(NT):
                    for h in range(2):
                        n = 4 * base + 2 * t + h
                        act.wait_ge((out2_ps, ffo_ps)[base], 2 * t + h + 1)
                        act.wait_ge(ssq_done, 24 if base else 20 + 2 * t)
                        if n > 1:
                            act.wait_ge(y_sq, n - 1)
                        act.activation(junk[:, h * 512:(h + 1) * 512], bank[2 * t + h], ACT.Square, scale=scale,
                                       accum_out=sq[:, 26 + n:27 + n]).then_inc(y_sq, 1)
                    if base == 0:
                        for h in range(2):
                            act.wait_ge(y_sq, 2 * t + h + 1)
                            act.wait_ge(x4_done, 2 * t + h + 1)
                            half_squares(5, x, t, h)

            post(0, 0.5)

            def ff(s, par):
                for f in range(2):
                    act.wait_ge(ff_ps, s * 2 + f + 1)
                    act.activation(thF[:, par, f, :], bank[4 + 2 * par + f][:, 0:T], ACT.Tanh, scale=0.5)\
                       .then_inc(ff_th, 1)

            ff(0, 0)
            ff(1, 1)
            with act.Fori(0, 4) as i:
                ff(i * 2 + 2, 0)
                ff(i * 2 + 3, 1)
            ff(10, 0)
            post(1, 1.0)

        @block.tensor
        def _(pe):
            r = Ring(pe, full, free)

            def mm(o, l, rr, start=True, stop=True):
                return pe.matmul(o, l, rr, start=start, stop=stop)

            def tile_turn(c, src, b0, t):
                pe.wait_ge(xn_done, 2 * c + t + 1)
                for h in range(2):
                    for k in range(4):
                        kk = 4 * h + k
                        ins = pe.transpose(bank[b0 + 2 * t + h][:, k * P:(k + 1) * P],
                                           src[:, t, kk * P:(kk + 1) * P], ident)
                    ins.then_inc(tr_done, 1)

            def turn(c, src, b0):
                for t in range(NT):
                    tile_turn(c, src, b0, t)

            def product(o, w, n=KC, src=None, l0=0):
                for k in range(n):
                    ins = mm(o, w(k), (hT if src is None else src)[:, k, :], k == 0, k == n - 1)
                return ins

            pe.wait_ge(in_consts, 32)
            turn(0, xn, 0)
            pe.wait_ge(hT_done, 4)

            def project(j, w):
                for t in range(NT):
                    for k in range(KC):
                        ins = mm(bank[t], hT[:, k, t * P:(t + 1) * P], w(k), k == 0, k == KC - 1)
                    ins.then_inc(zA_ps, 1)

            def pair_scores(j):
                pe.wait_ge(zA_sb, j * 2 + 2)
                for t in range(NT):
                    ins = mm(bank[3][:, 0:T], zA[:, t, 0:P], poolm[:, t, bass.ds(j, 1), :].rearrange("p a s -> p (a s)"),
                             t == 0, t == NT - 1)
                ins.then_inc(poolA_ps, 1)
                pe.wait_ge(qknA, j + 1)
                for m in range(2):
                    for t in range(NT):
                        ins = pe.transpose(bank[2][:, m * T + t * P:m * T + (t + 1) * P],
                                           qkn[:, t, m * P:(m + 1) * P], ident)
                ins.then_inc(qkT_ps, 1)
                pe.wait_ge(in_wp, j * 16 + 16)
                pe.wait_ge(dT_sb, j + 1)
                mm(bank[3][:, T:2 * T], wp, dT).then_inc(poolY_ps, 1)
                pe.wait_ge(qkT_sb, j * 2 + 2)
                pe.nop(nofuse=True)
                for h in range(2):
                    for t in range(NT):
                        ins = mm(bank[4 + h][:, t * T:(t + 1) * T], qkT[64 * h:64 * h + 64, 0, t * P:(t + 1) * P],
                                 qkT[64 * h:64 * h + 64, 1, :])
                        if h == 0 and t == 0:
                            ins.then_inc(wp_used, 1)
                    ins.then_inc(sA_ps, 1)

            def pair_values(j):
                for h in range(2):
                    pe.wait_ge(pA, j * 2 + h + 1)
                    for k in range(NT):
                        for t in range(NT):
                            ins = pe.transpose(bank[6 + h][:, k * T + t * P:k * T + (t + 1) * P],
                                               sA[:, h, t, k * P:(k + 1) * P], ident)
                    ins.then_inc(ptA_ps, 1)
                for h in range(2):
                    pe.wait_ge(ptA_sb, j * 2 + h + 1)
                    for k in range(NT):
                        ins = mm(bank[4][64 * h:64 * h + 64, 0:T], zA[:, k, 384 + 64 * h:448 + 64 * h],
                                 PTA[:, h, k, :], k == 0, k == NT - 1)
                    ins.then_inc(oA_ps, 1)

            r.arrived(0, 4)
            project(0, lambda k: strip[0][:, k, :])
            pe.wait_ge(in_pool, 16)
            pe.wait_ge(zA_sb, 2)
            pe.sem_inc(free[0], 1)
            for s in range(1, PAIRS):
                r.arrived(s, 4)
            with pe.Fori(0, PAIRS - 1) as j:
                pair_scores(j)
                pe.wait_ge(vA_sb, j + 1)
                project(j + 1, lambda k: ring[:, bass.ds((j + 1) * SLOT + k * 512, 512)])
                pair_values(j)
            for s in range(1, PAIRS):
                pe.sem_inc(free[s], 1)
            last = PAIRS - 1
            pair_scores(last)

            r.count(5, 0)
            r.arrived(4, 2)
            r.arrived(5, 2)
            pe.wait_ge(vA_sb, PAIRS)
            pe.wait_ge(yA_pool, PAIRS)
            pe.wait_ge(yA_attn, PAIRS - 1)
            for h in range(2):
                for k in range(KC - 1):
                    mm(bank[h], yT[:, k, 0:P], strip[4 + h][:, k, :], k == 0, False)
            pair_values(last)
            pe.wait_ge(yA_attn, PAIRS)
            for h in range(2):
                mm(bank[h], yT[:, KC - 1, 0:P], strip[4 + h][:, KC - 1, :], False, True).then_inc(out1_ps, 1)
            for h in range(2):
                for k in range(KC):
                    ins = mm(bank[2 + h], yT[:, k, P:T], strip[4 + h][:, k, :], k == 0, k == KC - 1)
                    if h == 1 and k == 0:
                        ins.then_inc(free[4], 1)
                ins.then_inc(out1_ps, 1)
            for t in range(NT):
                tile_turn(2, xn, 0, t)
                pe.wait_ge(hT_done, 6 + 2 * t)
                if t == 0:
                    pe.wait_ge(in_mem, 32)
                for k in range(KC):
                    ins = mm(bank[4][:, t * 16:t * 16 + 16], hT[:, k, t * P:(t + 1) * P], wr[:, k, :], k == 0, k == KC - 1)
                    if t == 0 and k == 0:
                        ins.then_inc(free[5], 1)
            ins.then_inc(lg_ps, 1)
            pe.wait_ge(aff_sb, 1)
            for t in range(NT):
                ins = pe.transpose(bank[5][0:EXPERTS, t * P:(t + 1) * P], lgE[:, t, :], ident)
            ins.then_inc(aff_ps, 1)
            pe.wait_ge(pos_sb, 1)
            for t in range(NT):
                ins = pe.transpose(bank[6][:, t * 16:t * 16 + 16], cumT[:, t * P:(t + 1) * P], ident[0:EXPERTS, 0:EXPERTS])
            ins.then_inc(pos_ps, 1)

            wide = [s.rearrange("p (k n) -> p k n", k=2) for s in slot]
            tall = [s.rearrange("p (k n) -> p k n", k=4) for s in slot]

            def expert(e, slots):
                pe.wait_ge(sele_sb, e + 1)
                for k in range(KC):
                    for t in range(NT):
                        ins = mm(bank[3][:, k * CAP:(k + 1) * CAP], xn[:, t, k * P:(k + 1) * P], sele[:, t, 0, :],
                                 t == 0, t == NT - 1)
                ins.then_inc(xe_ps, 1)
                for t in range(NT):
                    for c in range(4):
                        ins = mm(bank[2][32 * c:32 * c + 32, t * P:(t + 1) * P], sele[:, t, 1, :], ident)
                ins.then_inc(gt_ps, 1)
                pe.wait_ge(xe_sb, e + 1)
                for n in range(8):
                    s = slots[n]
                    r.arrived(s, 1)
                    for k in (2 * (n % 4), 2 * (n % 4) + 1):
                        for c in range(4):
                            ins = mm(bank[n // 4][32 * c:32 * c + 32, :], xeT[:, k, :],
                                     wide[s][:, k % 2, c * 512:(c + 1) * 512], k == 0, k == KC - 1)
                            if k % 2 and c == 3 and n % 4 != 3 and s < SLOTS:
                                ins.then_inc(free[s], 1)
                            if n == 4 and k == 0 and c == 0:
                                ins.then_inc(free[slots[3]], 1)
                    if n % 4 == 3:
                        ins.then_inc((gate_ps, up_ps)[n // 4], 1)
                pe.wait_ge(h_sb, e + 1)
                pe.wait_ge(gt_sb, e + 1)
                for c in range(4):
                    ins = pe.transpose(bank[2][:, c * P:(c + 1) * P], hE[:, c * P:(c + 1) * P], ident)
                    if c == 0:
                        ins.then_inc(free[slots[7]], 1)
                ins.then_inc(ht_ps, 1)
                pe.wait_ge(ht_sb, e + 1)
                for i in range(4):
                    s = slots[8 + i]
                    r.arrived(s, 1)
                    for h in range(2):
                        for c in range(4):
                            ins = mm(bank[4 + h][32 * c:32 * c + 32, :], hTe[:, c, 32 * i:32 * i + 32],
                                     tall[s][:, c, h * 512:(h + 1) * 512], i == 0, i == 3)
                    if i < 3 and s < SLOTS:
                        ins.then_inc(free[s], 1)
                ins.then_inc(y_ps, 1)
                pe.wait_ge(y_sb, e * 2 + 2)
                for t in range(NT):
                    for h in range(2):
                        ins = mm(bank[(6, 4)[t] + h], gT[:, t * P:(t + 1) * P], ysb[:, h * 512:(h + 1) * 512])
                        ins.then_inc(sc_ps, 1)
                pe.wait_ge(sc_ps, e * 4 + 4)
                pe.sem_inc(free[slots[11]], 1)

            def experts(part, rot):
                with pe.Fori(0, PARTS[part]) as i:
                    r.enter(i, {s: (2, 2) for s in range(SLOTS)})
                    expert(i + sum(PARTS[:part]), around(rot))
                    r.leave(PARTS[part])

            expert(0, FIRST_SLOTS)
            experts(1, 3)
            pe.wait_ge(in_p, 16)
            pe.wait_ge(x_acc, 4 * sum(PARTS[:2]))
            for k in range(2):
                for t in range(NT):
                    ins = pe.transpose(bank[6][:, k * T + t * P:k * T + (t + 1) * P], pin[:, t, k * P:(k + 1) * P], ident)
            ins.then_inc(pT_ps, 1)
            turn(1, mx, 0)
            pe.wait_ge(pT_sb, 1)
            r.arrived(3, 1)
            wple = slot[3][:, 0:2 * D].rearrange("p (k n) -> p k n", k=2)
            for t in range(NT):
                for h in range(2):
                    for k in range(2):
                        ins = mm(bank[4 + 2 * t + h], pT[:, k, t * P:(t + 1) * P], wple[:, k, h * 512:(h + 1) * 512], k == 0, k == 1)
                    ins.then_inc(e_ps, 1)
            pe.wait_ge(hT_done, 12)
            r.arrived(4, 2)
            for h in range(4):
                for k in range(KC):
                    ins = mm(bank[h // 2][:, (h % 2) * T:(h % 2) * T + T], strip[4][:, k, h * P:(h + 1) * P],
                             hT[:, k, :], k == 0, k == KC - 1)
                    if h == 0 and k == 0:
                        ins.then_inc(free[3], 1)
                if h % 2:
                    ins.then_inc(mkv_ps, 1)
            pe.wait_ge(mkv_sb, 2)
            pe.wait_ge(e_sb, 4)
            pe.sem_inc(free[4], 1)
            experts(2, 5)
            r.arrived(2, 2)
            for t in range(NT):
                for k in range(KC):
                    ins = mm(bank[2 + t], hT[:, k, t * P:(t + 1) * P], strip[2][:, k, :], k == 0, k == KC - 1)
                ins.then_inc(mkv_ps, 1)
            pe.wait_ge(mkv_sb, 4)
            pe.sem_inc(free[2], 1)
            experts(3, 3)

            r.arrived(3, 2)
            r.arrived(4, 2)
            for t in range(NT):
                tile_turn(3, xn, 0, t)
                pe.wait_ge(hT_done, 14 + 2 * t)
                for h in range(2):
                    for k in range(KC):
                        ins = mm(bank[4 + 2 * t + h], hT[:, k, t * P:(t + 1) * P], strip[3 + h][:, k, :], k == 0, k == KC - 1)
                    ins.then_inc(g_ps, 1)

            pe.wait_ge(g_th, 4)
            for t in range(NT):
                tile_turn(4, xn, 0, t)
                pe.wait_ge(hT_done, 18 + 2 * t)
                for k in range(KC):
                    ins = mm(bank[4][:, t * 56:t * 56 + 56], hT[:, k, t * P:(t + 1) * P], wsm[:, k, :], k == 0, k == KC - 1)
                    if t == 0 and k < 2:
                        ins.then_inc(free[3 + k], 1)
                if t == 0:
                    r.arrived(5, 2)
                else:
                    ins.then_inc(ga_ps, 1)
                for g in range(GROUPS):
                    o = bank[6 + g // 2][:, (g % 2) * T + t * P:(g % 2) * T + (t + 1) * P]
                    for k in range(KC):
                        for m in range(2):
                            ins = mm(o[64 * m:64 * m + 64, :], strip[5][:, k, m * 256 + g * HD:m * 256 + g * HD + HD],
                                     hT[:, k, t * P:(t + 1) * P], k == 0, k == KC - 1)
                    if t == 1 and g % 2:
                        ins.then_inc(kvc_ps, 1)
                    if t == 1 and g == 0:
                        pe.wait_ge(ga_th, 1)
                        for m in range(2):
                            for u in range(NT):
                                ins = pe.transpose(bank[5][0:4, m * T + u * P:m * T + (u + 1) * P],
                                                   ifT[:, u, 4 * m:4 * m + 4], ident)
                        ins.then_inc(if_ps, 1)
            pe.wait_ge(pe_sb, 1)
            pe.wait_ge(kvc_sb, 2)
            r.arrived(2, 2)
            w1 = slot[2].rearrange("p (l h) -> p l h", l=CMP_L)
            for l in range(CMP_L):
                for m in range(2):
                    ins = mm(bank[m][:, 0:75].rearrange("p (g n) -> p g n", g=5), w1[64 * m:64 * m + 64, l, :],
                             kvc[64 * m:64 * m + 64, :, l:l + CMP_STRIDE * (N_CMP - 1) + 1:CMP_STRIDE],
                             l == 0, l == CMP_L - 1)
                    if l == 0 and m == 0:
                        ins.then_inc(free[5], 1)
            ins.then_inc(hid_ps, 1)
            pe.wait_ge(em_sb, 1)
            for n, row in enumerate((aR, emR)):
                for t in range(NT):
                    ins = pe.transpose(bank[7][:, (n * 2 + t) * 4:(n * 2 + t) * 4 + 4], row[:, t * P:(t + 1) * P],
                                       ident[0:4, 0:4])
                    if n == 0 and t == 0:
                        ins.then_inc(free[2], 1)
            ins.then_inc(st_ps, 1)
            pe.wait_ge(hid_sb, 1)
            for m in range(2):
                mm(bank[2][64 * m:64 * m + 64, 0:60], w2[:, 0:HD], hidk)
            for g in range(GROUPS):
                for i in range(4):
                    ins = mm(bank[3][32 * i:32 * i + 32, g * HD:(g + 1) * HD], hidv[:, g, :], w2[:, HD:2 * HD])
            ins.then_inc(kc_ps, 1)
            pe.wait_ge(st_sb, 2)
            pe.wait_ge(kc_sb, 2)

            def scores(g, i):
                par, hp = i % 2, i // 2
                for b in range(2):
                    key = kxy[64 * par:64 * par + 64, b ^ par, :]
                    q = qs[64 * par:64 * par + 64, hp, :]
                    o = bank[2 * par + b]
                    mm(o[:, 0:128], q[:, 0:128], key[:, 0:128])
                    ins = mm(o[:, 128:384], q[:, 128:256], key)
                ins.then_inc(ns_ps, 1)

            def turned(n4, i):
                pe.wait_ge(np_sb, n4 + i + 1)
                for b in range(2):
                    for c in range(3):
                        ins = pe.transpose(bank[4 + b][:, c * P:(c + 1) * P], Pn[:, i % 2, b, c * P:(c + 1) * P], ident)
                ins.then_inc(nt_ps, 1)

            def values(n4, i):
                pe.wait_ge(nt_sb, n4 + i + 1)
                par, hp = i % 2, i // 2
                o = bank[6 + hp][64 * par:64 * par + 64, :]
                mm(o[:, 0:T], vsb[:, 0, 0:64], PTn[:, 0, 0:256], True, False)
                mm(o[:, 0:T], vsb[:, 0, 64:128], PTn[:, 1, 0:256], False, False)
                mm(o[:, 128:256], vsb[:, 1, 0:64], PTn[:, 0, 256:384], False, False)
                mm(o[:, 128:256], vsb[:, 1, 64:128], PTn[:, 1, 256:384], False, False)
                mm(o[:, 0:T], vcg[32 * i:32 * i + 32, :], PTc[32 * i:32 * i + 32, :], False, True).then_inc(no_ps, 1)

            memq = slot[1][:, 0:D].rearrange("p (k n) -> p k n", k=KC)
            with pe.Fori(0, GROUPS) as g:
                r.enter(g, {0: (1, 4), 1: (1, 1), 5: (1, 5)})
                n4 = g * 4
                r.arrived(0, 4)
                for m in range(2):
                    ins = product(bank[5][:, m * T:(m + 1) * T], lambda k: strip[0][:, k, m * P:(m + 1) * P])
                ins.then_inc(proj_ps, 1)
                r.arrived(5, 5)
                for m in range(2):
                    ins = product(bank[0][:, m * T:(m + 1) * T], lambda k: strip[5][:, k, m * P:(m + 1) * P])
                ins.then_inc(proj_ps, 1)
                product(bank[1][:, 0:T], lambda k: strip[5][:, k, 256:384]).then_inc(proj_ps, 1)
                pe.wait_ge(proj_sb, g * 7 + 1)
                pe.nop(nofuse=True)
                mm(bank[7][:, T:2 * T], const("ones", 4), negMd[:, bass.ds(g * T, T)]).then_inc(d_ps, 1)
                for t in range(NT):
                    for k in range(KC):
                        ins = mm(bank[4][:, t * T:(t + 1) * T], hT[:, k, t * P:(t + 1) * P], strip[0][:, k, 256:512],
                                 k == 0, k == KC - 1)
                ins.then_inc(proj_ps, 1)
                pe.wait_ge(proj_sb, g * 7 + 3)
                pe.wait_ge(kx_swap, g * 32 + 32)
                pe.nop(nofuse=True)
                scores(g, 0)
                pe.wait_ge(d_in, g + 1)
                r.arrived(1, 1)
                for k in range(KC):
                    ins = mm(bank[7][:, 0:T], memq[:, k, :], hT[:, k, :], k == 0, k == KC - 1)
                    if k == 0:
                        ins.then_inc(free[0], 1)
                ins.then_inc(proj_ps, 1)
                scores(g, 1)
                pe.wait_ge(proj_sb, g * 7 + 6)
                for t in range(NT):
                    ins = mm(bank[4][:, t * T:(t + 1) * T], qm[:, t * P:(t + 1) * P], kTm[:, bass.ds(g * T, T)])
                    if t == 0:
                        ins.then_inc(free[1], 1)
                ins.then_inc(xs_ps, 1)
                pe.wait_ge(c_qk, g + 1)
                mm(bank[6][:, 0:T], yc[:, 1, 0:P], yc[:, 0, :])
                mm(bank[6][:, T:T + P], yc[:, 1, P:T], yc[:, 0, P:T])
                pe.wait_ge(staged, g * 7 + 7)
                pe.nop(nofuse=True)
                for par in range(2):
                    for hp in range(2):
                        for t in range(NT):
                            c = 384 + (hp * 2 + t) * 16
                            ins = mm(bank[6 + par][:, c:c + N_CMP], qs[64 * par:64 * par + 64, hp, t * P:(t + 1) * P],
                                     kcg[64 * par:64 * par + 64, 0:N_CMP])
                ins.then_inc(cs_ps, 1)
                for t in range(NT):
                    for k in range(KC):
                        ins = mm(bank[5][:, t * P:(t + 1) * P], hT[:, k, t * P:(t + 1) * P], strip[5][:, k, 384:512],
                                 k == 0, k == KC - 1)
                ins.then_inc(proj_ps, 1)
                pe.wait_ge(w_sb, g + 1)
                mm(bank[7][:, 0:129], Wm[:, 0:128], v1[:, 0, 0:129]).then_inc(free[5], 1)
                mm(bank[7][:, 132:261], Wm[:, 128:256], v1[:, 0, 0:129], True, False)
                mm(bank[7][:, 132:261], Wm[:, 256:384], v1[:, 1, 0:129], False, True).then_inc(n_ps, 1)
                pe.wait_ge(cp_sb, g + 1)
                pe.wait_ge(cs_in, g + 1)
                for t in range(NT):
                    ins = pe.transpose(bank[6][:, T + t * P:T + (t + 1) * P], Pc[:, t, :, :].rearrange("p i n -> p (i n)"), ident)
                ins.then_inc(ct_ps, 1)
                pe.wait_ge(proj_sb, g * 7 + 7)
                turned(n4, 0)
                scores(g, 2)
                pe.wait_ge(xp_sb, g + 1)
                pe.wait_ge(h_div, g + 1)
                for k in range(NT):
                    for t in range(NT):
                        ins = pe.transpose(bank[7][:, k * T + t * P:k * T + (t + 1) * P], Pm[:, t, k * P:(k + 1) * P], ident)
                ins.then_inc(xt_ps, 1)
                pe.wait_ge(ct_sb, g + 1)
                values(n4, 0)
                turned(n4, 1)
                scores(g, 3)
                values(n4, 1)
                turned(n4, 2)
                pe.wait_ge(xt_sb, g + 1)
                for k in range(NT):
                    ins = mm(bank[0][:, 0:T], vmg[:, k, :], PTm[:, k, :], k == 0, k == NT - 1)
                ins.then_inc(xo_ps, 1)
                values(n4, 2)
                turned(n4, 3)
                values(n4, 3)
                pe.wait_ge(ym_sb, g + 1)
                for t in range(NT):
                    ins = pe.transpose(bank[2][:, t * P:(t + 1) * P], y1[:, t, :], ident)
                ins.then_inc(ym_ps, 1)
                pe.wait_ge(ymem_done, g + 1)
                r.leave(GROUPS)

            pe.wait_ge(ynsa_done, 8)
            pe.wait_ge(yml_done, 4)
            pe.wait_ge(ymem_done, 4)
            with pe.Fori(0, 4) as i:
                r.enter(i, {s: (1, 3) for s in (2, 3, 4, 5)})
                for u in range(2):
                    gs = slot[2 + 2 * u][:, 0:3072].rearrange("p (k n) -> p k n", k=KC)
                    pj = slot[3 + 2 * u][:, 0:2048].rearrange("p (k n) -> p k n", k=16)
                    pe.wait_ge(mg_free, i * 2 + u + 1)
                    r.arrived(2 + 2 * u, 3)
                    for b in range(3):
                        for k in range(KC):
                            ins = mm(bank[4 * u + b // 2][:, (b % 2) * T:(b % 2) * T + T], gs[:, k, b * P:(b + 1) * P],
                                     hT[:, k, :], k == 0, k == KC - 1)
                            if u == 1 and b == 0 and k == 0:
                                ins.then_inc(free[3], 1)
                    ins.then_inc(mg_ps, 1)
                    r.arrived(3 + 2 * u, 3)
                    ins = product(bank[4 * u + 2][:, 0:T], lambda k: pj[:, k, :], KC, yT)
                    ins.then_inc(free[2 + 2 * u], 1)
                    product(bank[4 * u + 2][:, T:2 * T], lambda k: pj[:, 8 + k, :], 4, yml)
                    ins = product(bank[4 * u + 3][:, 0:T], lambda k: pj[:, 12 + k, :], 4, ymem)
                    ins.then_inc(mp_ps, 1)
                    if u == 1:
                        pe.wait_ge(mp_ps, i * 2 + 2)
                        pe.sem_inc(free[5], 1)
                r.leave(4)
            pe.wait_ge(mg_free, 9)
            r.arrived(0, 2)
            r.arrived(1, 2)
            for t in range(NT):
                for h in range(2):
                    for k in range(KC):
                        if (t, h, k) == (0, 0, KC - 1):
                            pe.wait_ge(mg_free, 10)
                        ins = mm(bank[2 * t + h], yT2[:, k, t * P:(t + 1) * P], strip[h][:, k, :], k == 0, k == KC - 1)
                    ins.then_inc(out2_ps, 1)

            def ff_in(s, par):
                r.arrived(2 + 2 * par, 2)
                for f in range(2):
                    o = bank[4 + 2 * par + f]
                    for m in range(2):
                        ins = product(o[:, m * T:(m + 1) * T],
                                      lambda k: strip[2 + 2 * par][:, k, m * 256 + f * P:m * 256 + (f + 1) * P])
                    ins.then_inc(ff_ps, 1)

            def ff_down(s, par, first=False, last=False):
                r.arrived(3 + 2 * par, 1)
                w = slot[3 + 2 * par][:, 0:2 * D].rearrange("p (k n) -> p k n", k=2)
                pe.wait_ge(ff_h, s * 2 + 2)
                order = [(k, t, h) for k in range(2) for t in range(NT) for h in range(2)]
                if last:
                    order.sort(key=lambda o: o[1])
                for k, t, h in order:
                    ins = mm(bank[2 * t + h], hF[:, par, k, t * P:(t + 1) * P], w[:, k, h * 512:(h + 1) * 512],
                             first and k == 0, last and k == 1)
                    if last and k == 1:
                        ins.then_inc(ffo_ps, 1)
                    elif k == 0 and t == 0 and h == 0:
                        ins.then_inc(free[4 - 2 * par], 1)
                if not last:
                    ins.then_inc(free[3 + 2 * par], 1)

            r.arrived(2, 2)
            for t in range(NT):
                tile_turn(5, xF, 4, t)
                pe.wait_ge(hT_done, 22 + 2 * t)
                for f in range(2):
                    for m in range(2):
                        for k in range(KC):
                            ins = mm(bank[4 + f][:, m * T + t * P:m * T + (t + 1) * P],
                                     strip[2][:, k, m * 256 + f * P:m * 256 + (f + 1) * P],
                                     hT[:, k, t * P:(t + 1) * P], k == 0, k == KC - 1)
                    if t == 1:
                        ins.then_inc(ff_ps, 1)
            pe.wait_ge(ff_ps, 2)
            pe.sem_inc(free[2], 1)
            ff_in(1, 1)
            ff_down(0, 0, first=True)
            with pe.Fori(0, 4) as i:
                r.enter(i, {2: (1, 2), 3: (1, 1), 4: (1, 2), 5: (1, 1)})
                ff_in(i * 2 + 2, 0)
                ff_down(i * 2 + 1, 1)
                ff_in(i * 2 + 3, 1)
                ff_down(i * 2 + 2, 0)
                r.leave(4)
            ff_in(10, 0)
            ff_down(9, 1)
            ff_down(10, 0, last=True)

        @block.vector
        def _(dve):
            chain = Chain(dve, dve_chain)
            RS = 12

            def rsqrt(o, ss, n, w):
                v, y, q = nt_[:, 0:w], nt_[:, 8:8 + w], nt_[:, 16:16 + w]
                chain(dve.tensor_scalar(v, ss, 1.0 / n, EPS, ALU.mult, ALU.add))
                chain(dve.tensor_scalar(y.bitcast(I32), v.bitcast(I32), 1, None, ALU.logical_shift_right))
                chain(dve.tensor_scalar(y.bitcast(I32), y.bitcast(I32), -1.0, RSQRT_SEED, ALU.mult, ALU.add))
                for it in range(3):
                    chain(dve.tensor_tensor(q, y, y, ALU.mult))
                    chain(dve.scalar_tensor_tensor(out=q, in0=q, scalar=-0.5, in1=v, op0=ALU.mult, op1=ALU.mult))
                    chain(dve.scalar_tensor_tensor(out=y if it < 2 else o, in0=q, scalar=1.5, in1=y, op0=ALU.add,
                                                   op1=ALU.mult))

            def tile_normed(c, src, dst, t):
                n = 4 * c + 2 * t
                dve.wait_ge(ssq_done, n + 2)
                chain(dve.tensor_tensor(stat[:, 2 * c + t:2 * c + t + 1], sq[:, n:n + 1], sq[:, n + 1:n + 2], ALU.add))
                rsqrt(rst[:, 2 * c + t:2 * c + t + 1], stat[:, 2 * c + t:2 * c + t + 1], D, 1)
                dve.tensor_scalar(dst[:, t, :], src[:, t, :], rst[:, 2 * c + t:2 * c + t + 1], None, ALU.mult)\
                   .then_inc(xn_done, 1)

            def normed(c, src, dst):
                for t in range(NT):
                    tile_normed(c, src, dst, t)

            def tile_gained(c, b0, t):
                for h in range(2):
                    n = 4 * TURNS[c] + 2 * t + h
                    dve.wait_ge(tr_done, n + 1)
                    gain = vec[:, GAIN(c) + 4 * h:GAIN(c) + 4 * h + 4].unsqueeze(2).broadcast_to([P, 4, P])
                    dve.tensor_tensor(hT[:, 4 * h:4 * h + 4, t * P:(t + 1) * P],
                                      bank[b0 + 2 * t + h].rearrange("p (k t) -> p k t", k=4), gain, ALU.mult)\
                       .then_inc(hT_done, 1)

            def gained(c, b0):
                for t in range(NT):
                    tile_gained(c, b0, t)

            dve.memset(nt_[:, 32:33], 0.0).then_inc(exp_warm, 1)
            normed(0, x, xn)
            dve.wait_ge(in_consts, 32)
            gained(0, 0)
            def qk_normed(j):
                for t in range(NT):
                    dve.wait_ge(zA_sb, j * 2 + t + 1)
                    chain(dve.tensor_tensor(sqA[:, t, :], zA[:, t, 128:384], zA[:, t, 128:384], ALU.mult))
                    chain(dve.tensor_reduce(ssA[:, 4 * t:4 * t + 4], sqA[:, t, :].rearrange("p (h d) -> p h d", d=HD), AX,
                                            ALU.add))
                rsqrt(rsA, ssA, HD, 8)
                for t in range(NT):
                    ins = dve.tensor_tensor(qkn[:, t, :].rearrange("p (h d) -> p h d", d=HD),
                                            zA[:, t, 128:384].rearrange("p (h d) -> p h d", d=HD),
                                            rsA[:, 4 * t:4 * t + 4].unsqueeze(2).broadcast_to([P, 4, HD]), ALU.mult)
                ins.then_inc(qknA, 1)

            def bias_table():
                dve.wait_ge(in_bias, 2 * 16)
                mask = const("wmask").unsqueeze(1).broadcast_to([P, 6, GRID_W])
                for h in range(8):
                    ins = dve.tensor_tensor(btab[:, h, :, :], braw[:, h, :, ::-1], mask, ALU.add)
                ins.then_inc(bias_sb, 1)
                dve.wait_ge(bias_sb, 1)
                dve.memset(nt_[:, 35:36], 0.0).then_inc(free[5], 1)

            def pair(j, first=False):
                dve.wait_ge(qkT_ps, j + 1)
                dve.tensor_scalar(qkT[:, 0, :], bank[2][:, 0:T], vec[:, QN:QN + 1], HD ** -0.5, ALU.mult, ALU.mult)\
                   .then_inc(qkT_sb, 1)
                dve.tensor_scalar(qkT[:, 1, :], bank[2][:, T:2 * T], vec[:, KN:KN + 1], None, ALU.mult)\
                   .then_inc(qkT_sb, 1)
                dve.wait_ge(poolY_ps, j + 1)
                dve.tensor_scalar(yT[:, bass.ds(j, 1), :].rearrange("p a t -> p (a t)"), bank[3][:, T:2 * T],
                                  vec[:, bass.ds(j + PSCALE, 1)], None, ALU.mult).then_inc(yA_pool, 1)
                if first:
                    bias_table()
                for h in range(2):
                    dve.wait_ge(sA_ps, j * 2 + h + 1)
                    for t in range(NT):
                        bias = btab[:, bass.ds(j * 2 + h, 1), 2 - 2 * t:6 - 2 * t, :].rearrange("p a r c -> p (a r c)")
                        ins = dve.tensor_tensor(sA[:, h, t, :], bank[4 + h][:, t * T:(t + 1) * T], bias, ALU.add)
                    chain(ins)
                    dve.tensor_reduce(nmA[:, 2 * h:2 * h + 2], sA[:, h, :, :], AX, ALU.max, negate=True).then_inc(maxA, 1)
                for h in range(2):
                    dve.wait_ge(expA, j * 2 + h + 1)
                    chain(dve.reciprocal(rcA[:, 2 * h:2 * h + 2], sumA[:, 2 * h:2 * h + 2]))
                    for t in range(NT):
                        ins = dve.tensor_scalar(sA[:, h, t, :], sA[:, h, t, :], rcA[:, 2 * h + t:2 * h + t + 1], None,
                                                ALU.mult)
                    ins.then_inc(pA, 1)

            qk_normed(0)
            pair(0, first=True)
            qk_normed(1)
            with dve.Fori(0, PAIRS - 2) as i:
                chain.enter(i, 4 + RS + 2 + 2)
                pair(i + 1)
                qk_normed(i + 2)
                chain.leave(PAIRS - 2)
            pair(PAIRS - 1)

            normed(1, mx, mx)
            for t in range(NT):
                for h in range(2):
                    dve.wait_ge(out1_ps, 2 * t + h + 1)
                    dve.tensor_tensor(x[:, t, h * 512:(h + 1) * 512], x[:, t, h * 512:(h + 1) * 512],
                                      bank[2 * t + h], ALU.add).then_inc(x1_done, 1)
                if t == 0:
                    tile_normed(2, x, xn, 0)
            tile_gained(2, 0, 0)
            tile_normed(2, x, xn, 1)
            tile_gained(2, 0, 1)

            dve.wait_ge(lg_ps, 1)
            dve.tensor_reduce(nmE, bank[4][:, 0:32].rearrange("p (t e) -> p t e", t=NT), AX, ALU.max, negate=True)\
               .then_inc(lg_max, 1)
            dve.memset(onesT, 1.0)
            dve.wait_ge(lg_exp, 1)
            chain(dve.reciprocal(smE, smE))
            dve.tensor_tensor(lgE, lgE, smE.unsqueeze(2).broadcast_to([P, NT, EXPERTS]), ALU.mult).then_inc(aff_sb, 1)
            dve.wait_ge(aff_ps, 1)
            chain(dve.tensor_copy(affT, bank[5][0:EXPERTS, 0:T]))
            for it in range(CAP // 8):
                chain(dve.max(m8, affT))
                chain(dve.match_replace(affT, m8, affT, -1.0))
            chain(dve.tensor_scalar(selT, affT, 0.0, None, ALU.is_lt))
            chain(dve.tensor_tensor_scan(cumT, onesT, selT, 0.0, ALU.mult, ALU.add))
            dve.tensor_tensor(cumT, cumT, selT, ALU.mult).then_inc(pos_sb, 1)
            dve.wait_ge(pos_ps, 1)
            chain(dve.tensor_copy(posT, bank[6][:, 0:32].rearrange("p (t e) -> p t e", t=NT)))
            for first, n in ((0, 2), (2, EXPERTS - 2)):
                e = slice(first, first + n)
                for t in range(NT):
                    pos = posT[:, t, e].unsqueeze(2).broadcast_to([P, n, CAP])
                    aff = lgE[:, t, e].unsqueeze(2).broadcast_to([P, n, CAP])
                    place = const("iota1").unsqueeze(1).broadcast_to([P, n, CAP])
                    chain(dve.tensor_tensor(selall[:, e, t, 0, :], pos, place, ALU.is_equal))
                    dve.tensor_tensor(selall[:, e, t, 1, :], selall[:, e, t, 0, :], aff, ALU.mult).then_inc(sel_done, 1)

            gain = vec[:, GAIN(2):GAIN(2) + 8].unsqueeze(2).broadcast_to([P, KC, CAP])
            def expert(e):
                dve.wait_ge(xe_ps, e + 1)
                dve.tensor_tensor(xeT, bank[3][:, 0:KC * CAP].rearrange("p (k s) -> p k s", k=KC), gain, ALU.mult)\
                   .then_inc(xe_sb, 1)
                dve.wait_ge(gate_th, e + 1)
                chain(dve.scalar_tensor_tensor(out=thE, in0=thE, scalar=1.0, in1=bank[0], op0=ALU.add, op1=ALU.mult))
                dve.wait_ge(up_ps, e + 1)
                dve.scalar_tensor_tensor(out=hE, in0=thE, scalar=0.5, in1=bank[1], op0=ALU.mult, op1=ALU.mult)\
                   .then_inc(h_sb, 1)
                dve.wait_ge(y_ps, e + 1)
                dve.tensor_copy(ysb[:, 512:1024], bank[5]).then_inc(y_sb, 1)
                for t in range(NT):
                    for h in range(2):
                        dve.wait_ge(sc_ps, e * 4 + 2 * t + h + 1)
                        dve.tensor_tensor(x[:, t, h * 512:(h + 1) * 512], x[:, t, h * 512:(h + 1) * 512],
                                          bank[(6, 4)[t] + h], ALU.add).then_inc(x_acc, 1)

            def experts(part):
                with dve.Fori(0, PARTS[part]) as i:
                    chain.enter(i, 1)
                    expert(i + sum(PARTS[:part]))
                    chain.leave(PARTS[part])

            expert(0)
            experts(1)
            gained(1, 0)
            dve.wait_ge(e_sq, 2)
            dve.wait_ge(in_rows, 16 * 4)
            rsqrt(rst[:, 12:14], sq[:, 24:26], D, 2)
            for t in range(NT):
                chain(dve.scalar_tensor_tensor(out=uP[:, t, :], in0=uP[:, t, :], scalar=rst[:, 12 + t:13 + t],
                                               in1=grows[:, 0, :], op0=ALU.mult, op1=ALU.mult))
            experts(2)
            experts(3)

            for t in range(NT):
                tile_normed(3, x, xn, t)
                tile_gained(3, 0, t)
            for t in range(NT):
                for h in range(2):
                    c = slice(h * 512, (h + 1) * 512)
                    dve.wait_ge(g_th, 2 * t + h + 1)
                    chain(dve.scalar_tensor_tensor(out=uP[:, t, c], in0=thP[:, t, c], scalar=1.0, in1=uP[:, t, c],
                                                   op0=ALU.add, op1=ALU.mult))
                    dve.scalar_tensor_tensor(out=x[:, t, c], in0=uP[:, t, c], scalar=0.5, in1=x[:, t, c],
                                             op0=ALU.mult, op1=ALU.add).then_inc(x3_done, 1)
                tile_normed(4, x, xn, t)
                if t == 0:
                    tile_gained(4, 0, 0)
            tile_gained(4, 0, 1)

            dve.memset(kvc[:, 4, :], 0.0)
            dve.memset(hidv, 0.0)
            dve.memset(zp[:, :, 0:3], 0.0)
            dve.memset(v1[:, :, 128:132], 1.0)
            chain(dve.memset(Pc, 0.0))
            dve.tensor_copy(kvc[:, 4, 0:CMP_L], peT[:, :]).then_inc(pe_sb, 1)
            dve.wait_ge(if_ps, 1)
            chain(dve.tensor_scalar(iR, bank[5][0:4, 0:T], ifb[0:4, 0:1], None, ALU.add))
            chain(dve.tensor_scalar(fR, bank[5][0:4, T:2 * T], ifb[0:4, 1:2], None, ALU.add))
            chain(dve.tensor_scalar(mnR, fR, 0.0, None, ALU.min))
            chain(dve.tensor_scalar(MR, fR, -1.0, None, ALU.mult))
            dve.tensor_tensor(abR, fR, MR, ALU.max).then_inc(ab_sb, 1)
            dve.wait_ge(ga_th, 2)
            for b in range(3):
                for q in range(2):
                    o = gball.rearrange("p (g b q i t) -> p g b q i t", g=4, b=3, q=2, i=2)[:, :, b, q, :, :]
                    for t in range(NT):
                        src = gth[:, t, :].rearrange("p (g i q b) -> p g i q b", g=4, i=2, q=2)[:, :, :, q, b]
                        ins = dve.tensor_scalar(o[:, :, :, t], src, 1.0, 0.5, ALU.add, ALU.mult)
            ins.then_inc(ga_sb, 1)
            dve.wait_ge(ab_ln, 1)
            chain(dve.tensor_tensor(mnR, mnR, lnR, ALU.subtract))
            chain(dve.tensor_scalar(MR, mnR, 0.0, 1.0, ALU.mult, ALU.add))
            chain(dve.tensor_tensor_scan(BR, MR, mnR, 0.0, ALU.mult, ALU.add))
            chain(dve.tensor_tensor(aR, iR, BR, ALU.subtract))
            chain(dve.tensor_tensor_scan(MR, aR, aR, 0.0, ALU.max, ALU.max))
            dve.tensor_tensor(mR, BR, MR, ALU.add).then_inc(em_in, 1)
            chain(dve.tensor_scalar(nMR, MR, -1.0, None, ALU.mult))
            dve.tensor_tensor(negMd.rearrange("p (h t) -> p h t", h=4), nMR.unsqueeze(1).broadcast_to([4, 4, T]),
                              const("eye4", 4).unsqueeze(2).broadcast_to([4, 4, T]), ALU.mult).then_inc(st_sb, 1)
            dve.wait_ge(hid_ps, 1)
            for m in range(2):
                chain(dve.tensor_copy(hidb[:, m:m + 1], bank[m][:, 60:61]))
            for m in range(2):
                ins = dve.tensor_scalar(hpre[:, m, :], bank[m][:, 0:60], hidb[:, m:m + 1], None, ALU.add)
            ins.then_inc(hid_pre, 1)
            dve.wait_ge(hid_pre, 1)
            dve.wait_ge(hid_th, 1)
            chain(dve.scalar_tensor_tensor(out=hth, in0=hth, scalar=1.0, in1=hpre, op0=ALU.add, op1=ALU.mult))
            dve.tensor_scalar(hidk, hth[:, 0, :], 0.5, None, ALU.mult)
            dve.tensor_scalar(hidv[:, :, 0:N_CMP], hth[:, 1, :].rearrange("p (g n) -> p g n", g=4), 0.5, None, ALU.mult)\
               .then_inc(hid_sb, 1)
            dve.wait_ge(kc_ps, 1)
            dve.tensor_copy(kcall.rearrange("p (g n) -> p g n", g=4)[:, :, 0:N_CMP],
                            bank[2][:, 0:60].rearrange("p (g n) -> p g n", g=4)).then_inc(kc_sb, 1)
            dve.memset(kcall.rearrange("p (g n) -> p g n", g=4)[:, :, N_CMP:16], 0.0)
            dve.tensor_copy(vcall, bank[3][:, 0:256]).then_inc(kc_sb, 1)
            dve.wait_ge(st_ps, 1)
            dve.tensor_copy(stall.rearrange("p (h n) -> p h n", h=4),
                            bank[7][:, 0:16].rearrange("p (n h) -> p h n", h=4)).then_inc(st_sb, 1)

            cadd = const("cmpadd").rearrange("p (t n) -> p t n", t=NT)[:, :, 0:N_CMP].unsqueeze(1)\
                .broadcast_to([P, 2, NT, N_CMP])
            cmul = const("cmpmul").rearrange("p (t n) -> p t n", t=NT)[:, :, 0:N_CMP].unsqueeze(1)\
                .broadcast_to([P, 2, NT, N_CMP])
            gv = gst.rearrange("p (b q i t) -> p b q i t", b=3, q=2, i=2)

            def head_max(n4, i):
                par = i % 2
                dve.wait_ge(ns_ps, n4 + i + 1)
                s = ps[:, 2 * par:2 * par + 2, 0:384].rearrange("p b (c k) -> p b c k", c=3)
                chain(dve.tensor_tensor(s[:, :, 0, :], s[:, :, 0, :], caus.unsqueeze(1).broadcast_to([P, 2, P]), ALU.add))
                chain(dve.tensor_tensor(s[:, :, 2, :], s[:, :, 2, :], caus.unsqueeze(1).broadcast_to([P, 2, P]), ALU.add))
                dve.tensor_reduce(nmN[:, par, :, 0], s[:, :, 0, :], AX, ALU.max, negate=True)
                dve.tensor_reduce(nmN[:, par, :, 1], ps[:, 2 * par:2 * par + 2, 128:384], AX, ALU.max, negate=True)\
                   .then_inc(ns_max, 1)

            def head_probs(n4, i):
                par, hp = i % 2, i // 2
                dve.wait_ge(ns_exp, n4 + i + 1)
                chain(dve.reciprocal(rcN[:, par, :, :], smN[:, par, :, :]))
                chain(dve.tensor_tensor(rcN[:, par, :, :], rcN[:, par, :, :], gv[:, 1:3, par, hp, :], ALU.mult))
                for b in range(2):
                    for t, c in ((0, slice(0, 128)), (1, slice(128, 384))):
                        ins = dve.tensor_scalar(Pn[:, par, b, c], Pn[:, par, b, c], rcN[:, par, b, t:t + 1], None, ALU.mult)
                ins.then_inc(np_sb, 1)

            with dve.Fori(0, GROUPS) as g:
                n4 = g * 4
                chain.enter(g, 7 + 1 + 2 + 4 + 4 + 4 * 2 + 4 * 2 + RS + 2)
                dve.wait_ge(staged, g * 7 + 7)
                dve.wait_ge(proj_sb, g * 7 + 1)
                for j in range(4):
                    for m in range(2):
                        w = cst[:, 5 * m + j:5 * m + j + 1]
                        if j == 0:
                            ins = dve.tensor_scalar(yc[:, m, :], zp[:, m, 0:T], w, cst[:, 5 * m + 4:5 * m + 5],
                                                    ALU.mult, ALU.add)
                        else:
                            ins = dve.scalar_tensor_tensor(out=yc[:, m, :], in0=zp[:, m, j:j + T], scalar=w,
                                                           in1=yc[:, m, :], op0=ALU.mult, op1=ALU.add)
                        if j < 3:
                            chain(ins)
                        elif m == 0:
                            chain(ins)
                        else:
                            ins.then_inc(c_conv, 1)
                dve.wait_ge(c_th, g + 1)
                dve.scalar_tensor_tensor(out=yc, in0=thc, scalar=1.0, in1=yc, op0=ALU.add, op1=ALU.mult).then_inc(c_qk, 1)
                dve.wait_ge(d_ps, g + 1)
                dve.tensor_tensor(tm[:, 0:T], bank[7][:, T:2 * T], causTz, ALU.add)
                dve.tensor_tensor(tm[:, T:384], bank[7][:, T + P:2 * T], causT, ALU.add).then_inc(d_in, 1)
                head_max(n4, 0)
                head_probs(n4, 0)
                head_max(n4, 1)
                dve.wait_ge(xs_ps, g + 1)
                dve.tensor_reduce(nmM, bank[4].rearrange("p (t k) -> p t k", t=NT), AX, ALU.max, negate=True)\
                   .then_inc(xs_max, 1)
                dve.wait_ge(cs_ps, g + 1)
                for par in range(2):
                    ins = dve.tensor_tensor(
                        sc[:, 4 * par:4 * par + 4, 0:N_CMP].rearrange("p (i t) n -> p i t n", i=2),
                        bank[6 + par][:, 384:448].rearrange("p (i t n) -> p i t n", i=2, t=NT)[:, :, :, 0:N_CMP],
                        cadd, ALU.add)
                chain(ins)
                chain(dve.tensor_reduce(nmC, sc[:, :, 0:N_CMP], AX, ALU.max, negate=True))
                dve.tensor_tensor(sc[:, :, 0:N_CMP], sc[:, :, 0:N_CMP], nmC.unsqueeze(2).broadcast_to([P, 8, N_CMP]),
                                  ALU.add).then_inc(cs_in, 1)
                dve.wait_ge(d_exp, g + 1)
                dve.scalar_tensor_tensor(out=Wm, in0=bank[6][:, 0:384], scalar=0.25 * ML_DH ** -0.5, in1=tm,
                                         op0=ALU.mult, op1=ALU.mult).then_inc(w_sb, 1)
                dve.wait_ge(xs_exp, g + 1)
                chain(dve.reciprocal(rcM, smM))
                for t in range(NT):
                    ins = dve.tensor_scalar(Pm[:, t, :], Pm[:, t, :], rcM[:, t:t + 1], None, ALU.mult)
                ins.then_inc(xp_sb, 1)
                dve.wait_ge(cs_exp, g + 1)
                chain(dve.tensor_reduce(smC, sc[:, :, 0:N_CMP], AX, ALU.add))
                chain(dve.reciprocal(rcC, smC))
                chain(dve.tensor_tensor(rcC, rcC, gst[:, 0:8], ALU.mult))
                chain(dve.tensor_tensor(sc[:, :, 0:N_CMP], sc[:, :, 0:N_CMP],
                                        rcC.unsqueeze(2).broadcast_to([P, 8, N_CMP]), ALU.mult))
                pcv = Pc.rearrange("p t (i q) n -> p q i t n", q=2)
                for par in range(2):
                    ins = dve.tensor_tensor(pcv[:, par, :, :, 0:N_CMP],
                                            sc[:, 4 * par:4 * par + 4, 0:N_CMP].rearrange("p (i t) n -> p i t n", i=2),
                                            cmul, ALU.mult)
                ins.then_inc(cp_sb, 1)
                dve.wait_ge(n_ps, g + 1)
                num = bank[7][:, 0:264].rearrange("p (t e) -> p t e", t=NT)
                chain(dve.tensor_copy(dn, num[:, :, 128]))
                chain(dve.scalar_tensor_tensor(out=ab, in0=dn, scalar=-1.0, in1=dn, op0=ALU.mult, op1=ALU.max))
                chain(dve.tensor_tensor(ab, ab, lst[:, 2:4], ALU.max))
                chain(dve.reciprocal(rd, ab))
                for t in range(NT):
                    ins = dve.tensor_scalar(hh[:, t, :], num[:, t, 0:128], rd[:, t:t + 1], None, ALU.mult)
                ins.then_inc(h_div, 1)
                head_probs(n4, 1)
                head_max(n4, 2)
                dve.wait_ge(h_sq, g + 1)
                rsqrt(rd, ssM, ML_DH, 2)
                head_probs(n4, 2)
                head_max(n4, 3)
                for t in range(NT):
                    ins = dve.scalar_tensor_tensor(out=y1[:, t, :], in0=hh[:, t, :], scalar=rd[:, t:t + 1], in1=hgg,
                                                   op0=ALU.mult, op1=ALU.mult)
                    chain(ins)
                dve.scalar_tensor_tensor(out=y1, in0=so, scalar=1.0, in1=y1, op0=ALU.add, op1=ALU.mult).then_inc(ym_sb, 1)
                head_probs(n4, 3)
                chain.leave(GROUPS)

            dve.wait_ge(ynsa_done, 8)
            dve.wait_ge(yml_done, 4)
            dve.memset(nt_[:, 34:35], 0.0).then_inc(mg_free, 2)
            with dve.Fori(0, 4) as i:
                chain.enter(i, 6)
                for u in range(2):
                    m = i * 2 + u
                    dve.wait_ge(mg_th, m + 1)
                    dve.wait_ge(mp_ps, m + 1)
                    chain(dve.scalar_tensor_tensor(out=yG[:, u, 0:512], in0=thG[:, u, 0:512], scalar=1.0,
                                                   in1=bank[4 * u + 2], op0=ALU.add, op1=ALU.mult))
                    chain(dve.scalar_tensor_tensor(out=yG[:, u, 512:768], in0=thG[:, u, 512:768], scalar=1.0,
                                                   in1=bank[4 * u + 3][:, 0:T], op0=ALU.add, op1=ALU.mult))
                    chain(dve.tensor_tensor(yG[:, u, 0:T], yG[:, u, 0:T], yG[:, u, T:512], ALU.add))
                    dve.tensor_tensor(yT2[:, bass.ds(m, 1), :].rearrange("p a t -> p (a t)"), yG[:, u, 0:T],
                                      yG[:, u, 512:768], ALU.add).then_inc(mg_free, 1)
                chain.leave(4)

            def post(base, scale):
                for t in range(NT):
                    n, c = 4 * base + 2 * t, 12 + 2 * base + t
                    dve.wait_ge(y_sq, n + 2)
                    chain(dve.tensor_tensor(stat[:, c:c + 1], sq[:, 26 + n:27 + n], sq[:, 27 + n:28 + n], ALU.add))
                    rsqrt(rst[:, c:c + 1], stat[:, c:c + 1], D, 1)
                    for h in range(2):
                        o = slice(h * 512, (h + 1) * 512)
                        chain(dve.scalar_tensor_tensor(out=ysF[:, t, o], in0=bank[2 * t + h], scalar=rst[:, c:c + 1],
                                                       in1=grows[:, 1 + base, o], op0=ALU.mult, op1=ALU.mult))
                        dve.scalar_tensor_tensor(out=x[:, t, o], in0=ysF[:, t, o], scalar=scale, in1=x[:, t, o],
                                                 op0=ALU.mult, op1=ALU.add).then_inc(x4_done, 1)
                    if not base:
                        tile_normed(5, x, xF, t)
                        tile_gained(5, 4, t)

            post(0, 0.5)

            def ff(s, par):
                for f in range(2):
                    b = bank[4 + 2 * par + f]
                    dve.wait_ge(ff_th, s * 2 + f + 1)
                    chain(dve.scalar_tensor_tensor(out=vF[:, par, f, :], in0=thF[:, par, f, :], scalar=1.0,
                                                   in1=b[:, 0:T], op0=ALU.add, op1=ALU.mult))
                    dve.scalar_tensor_tensor(out=hF[:, par, f, :], in0=vF[:, par, f, :], scalar=0.5, in1=b[:, T:2 * T],
                                             op0=ALU.mult, op1=ALU.mult).then_inc(ff_h, 1)

            ff(0, 0)
            ff(1, 1)
            with dve.Fori(0, 4) as i:
                chain.enter(i, 4)
                ff(i * 2 + 2, 0)
                ff(i * 2 + 3, 1)
                chain.leave(4)
            ff(10, 0)
            post(1, 1.0)


_NAMES = ["x", "p", "w_in", "w_pool", "rpb", "w_out", "w_gate", "w_up", "w_down", "w_ple_gate", "w_ple_proj",
          "norm_ple_post", "mem_2", "w_in_2", "cmp_w1_k_2", "cmp_w1_v_2", "ml_head_g_2", "w_mem_kv_2",
          "w_proj_nsa_2", "w_proj_ml_2", "w_proj_mem_2", "w_out_2", "g_post_mix_2", "w_ffn_in_2", "w_ffn_down_2",
          "g_post_ffn_2"]


def laid_out(name, value):
    value = np.asarray(value)
    if name == "rpb":
        value = value[0].transpose(1, 0, 2)[..., ::-1]
    return np.ascontiguousarray(value)


def packed_vectors(inputs):
    v = np.zeros((P, NVEC + CMP_L + 2), np.float32)
    get = lambda n: np.asarray(inputs[n])[0]
    for c, n in enumerate(("norm_mix", "g_mem_2", "norm_ffn", "norm_ple", "g_pre_mix_2", "g_pre_ffn_2")):
        v[:, GAIN(c):GAIN(c) + 8] = get(n).reshape(8, P).T
    v[:, PSCALE:PSCALE + 4] = get("pool_scale").reshape(4, P).T
    taps, bias = get("ml_conv_w_2").reshape(4, 2, 4, P), get("ml_conv_b_2").reshape(2, 4, P)
    for m in range(2):
        for j in range(4):
            v[:, CONV + 5 * m + j:CONV + 40:10] = taps[j, m].T
        v[:, CONV + 5 * m + 4:CONV + 40:10] = bias[m].T
    for n, c in (("q_norm", QN), ("k_norm", KN)):
        v[0:HD, c] = v[HD:P, c] = get(n)
    v[0:HD, NVEC:NVEC + CMP_L] = get("cmp_pe_k_2").T
    v[HD:P, NVEC:NVEC + CMP_L] = get("cmp_pe_v_2").T
    v[0:4, NVEC + CMP_L:] = get("ml_gate_b_2").reshape(2, 4).T
    return v


def packed_weights(inputs):
    get = lambda n: np.asarray(inputs[n])[0]
    rows = lambda w: w.reshape(KC, P, -1).transpose(1, 0, 2).reshape(P, -1)
    w_in = get("w_in_2")
    gates = np.concatenate([w_in[:, GATE0:GATE0 + 48], w_in[:, IF0:IF0 + 8]], 1)
    return np.ascontiguousarray(np.concatenate([rows(get("w_router")), rows(gates), get("cmp_w2_k_2"),
                                                get("cmp_w2_v_2")], 1))


def kernel(**inputs):
    import concourse.bacc as _bacc
    from concourse.bass_utils import run_bass_kernel_spmd as _run

    nc = _bacc.Bacc("TRN2", target_bir_lowering=False, num_devices=1)
    arrays, aps = {}, {}
    masks, pool = constants()
    packed = [("vecs", packed_vectors(inputs)), ("small", packed_weights(inputs))]
    for name, value in [(n, laid_out(n, inputs[n])) for n in _NAMES] + packed + [("consts", masks), ("pool", pool)]:
        arrays[f"in_{name}"] = value
        aps[name] = nc.dram_tensor(f"in_{name}", value.shape, mybir.dt.from_np(value.dtype), kind="ExternalInput").ap()
    out = nc.dram_tensor("out_0", (1, T, D), F32, kind="ExternalOutput").ap()
    two_blocks(nc, aps, out)
    r = _run(nc, [arrays], core_ids=[0])
    return r.results[0]["out_0"]
```
